# Optimizing a Trainium2 kernel written in Bass

```python
import math
import jax, jax.numpy as jnp
from jax import lax
import numpy as np

D_MODEL = 1024
BATCH = 1
SEQ = 512
DEPTH = 1
DEC_BATCH = 1
DEC_SEQ = 32
PAST_LEN = 256

CHUNK = 64
SSM_EXPAND = 2
D_INNER = SSM_EXPAND * D_MODEL
SSM_HEAD_DIM = 64
SSM_HEADS = D_INNER // SSM_HEAD_DIM
SSM_GROUPS = 8
SSM_HPG = SSM_HEADS // SSM_GROUPS
D_STATE = 128
SSM_CONV = 4
CONV_DIM = D_INNER + 2 * SSM_GROUPS * D_STATE
HEAD_DIM = 64
N_HEADS = D_MODEL // HEAD_DIM
N_KV_HEADS = 4
Q_PER_KV = N_HEADS // N_KV_HEADS
WINDOW = 128
PREV_CHUNKS = WINDOW // CHUNK
ROT_DIM = HEAD_DIM // 4
ROPE_THETA = 500000.0
D_FF = ((8 * D_MODEL // 3 + 255) // 256) * 256
FFN_CONV = 3
NORM_EPS = 1e-6

_IN_WIDTHS = (D_INNER, CONV_DIM, SSM_HEADS, N_HEADS * HEAD_DIM, N_KV_HEADS * HEAD_DIM, N_KV_HEADS * HEAD_DIM, 2 * D_MODEL)
IN_SPLITS = tuple(sum(_IN_WIDTHS[:i + 1]) for i in range(len(_IN_WIDTHS) - 1))
IN_WIDTH = sum(_IN_WIDTHS)

kernel_name = 'hybrid_ssd_swa_sink_convffn_stream_step'

def rmsnorm(x, g):
    xf = x.astype(jnp.float32)
    y = xf * lax.rsqrt(jnp.mean(xf * xf, axis=-1, keepdims=True) + NORM_EPS)
    return (y * g.astype(jnp.float32)).astype(x.dtype)

def partial_rope(x, pos):
    half = ROT_DIM // 2
    inv = ROPE_THETA ** (-jnp.arange(half, dtype=jnp.float32) / half)
    ang = pos.astype(jnp.float32)[:, None] * inv[None, :]
    cos, sin = jnp.cos(ang)[:, None, :], jnp.sin(ang)[:, None, :]
    xr = x[..., :ROT_DIM].astype(jnp.float32)
    x1, x2 = xr[..., :half], xr[..., half:]
    rot = jnp.concatenate([x1 * cos - x2 * sin, x2 * cos + x1 * sin], axis=-1)
    return jnp.concatenate([rot.astype(x.dtype), x[..., ROT_DIM:]], axis=-1)

def causal_dwconv(x, ctx, w, b):
    K, T = w.shape[0], x.shape[1]
    xp = jnp.concatenate([ctx.astype(x.dtype), x], axis=1)
    y = b
    for j in range(K):
        y = y + xp[:, j:j + T] * w[j]
    return y, xp[:, T:]

def ssd_chunk(h, inp):
    x, a, Bm, Cm = inp
    l = x.shape[1]
    acs = jnp.cumsum(a, axis=1)
    diff = acs[:, :, None] - acs[:, None, :]
    causal = jnp.tril(jnp.ones((l, l), dtype=bool))[None, :, :, None, None]
    decay = jnp.exp(jnp.where(causal, diff, -jnp.inf))
    cb = jnp.einsum('blgn,bsgn->blsg', Cm, Bm)
    y = jnp.einsum('blsgr,bsgrp->blgrp', cb[..., None] * decay, x)
    y = y + jnp.einsum('blgn,bgrpn->blgrp', Cm, h) * jnp.exp(acs)[..., None]
    xt = x * jnp.exp(acs[:, -1:] - acs)[..., None]
    h = h * jnp.exp(acs[:, -1])[..., None, None] + jnp.einsum('blgn,blgrp->bgrpn', Bm, xt)
    return h, y

def ssd_scan(x, a, Bm, Cm, h0):
    b, T = x.shape[0], x.shape[1]
    L = min(CHUNK, T)
    nc = T // L
    def blocks(t):
        return jnp.moveaxis(t.reshape((b, nc, L) + t.shape[2:]), 1, 0)
    h, y = lax.scan(ssd_chunk, h0, (blocks(x), blocks(a), blocks(Bm), blocks(Cm)))
    return jnp.moveaxis(y, 0, 1).reshape(x.shape), h

def ssm_branch(z, xbc, dt, conv_ctx, h0, p):
    b, T = z.shape[0], z.shape[1]
    xbc, conv_new = causal_dwconv(xbc, conv_ctx, p['ssm_conv_w'], p['ssm_conv_b'])
    xbc = jax.nn.silu(xbc).astype(jnp.float32)
    xs, Bm, Cm = jnp.split(xbc, [D_INNER, D_INNER + SSM_GROUPS * D_STATE], axis=-1)
    xs = xs.reshape(b, T, SSM_GROUPS, SSM_HPG, SSM_HEAD_DIM)
    Bm = Bm.reshape(b, T, SSM_GROUPS, D_STATE)
    Cm = Cm.reshape(b, T, SSM_GROUPS, D_STATE)
    dt = jax.nn.softplus(dt.astype(jnp.float32) + p['ssm_dt_bias'].astype(jnp.float32))
    dt = dt.reshape(b, T, SSM_GROUPS, SSM_HPG)
    A = -jnp.exp(p['ssm_a_log'].astype(jnp.float32)).reshape(SSM_GROUPS, SSM_HPG)
    h0 = h0.astype(jnp.float32).reshape(b, SSM_GROUPS, SSM_HPG, SSM_HEAD_DIM, D_STATE)
    y, h = ssd_scan(xs * dt[..., None], dt * A, Bm, Cm, h0)
    y = y + xs * p['ssm_d'].astype(jnp.float32).reshape(SSM_GROUPS, SSM_HPG)[..., None]
    y = y.reshape(b, T, D_INNER) * jax.nn.silu(z.astype(jnp.float32))
    yg = y.reshape(b, T, SSM_GROUPS, D_INNER // SSM_GROUPS)
    yg = yg * lax.rsqrt(jnp.mean(yg * yg, axis=-1, keepdims=True) + NORM_EPS)
    y = yg.reshape(b, T, D_INNER) * p['ssm_norm'].astype(jnp.float32)
    h = h.reshape(b, SSM_HEADS, SSM_HEAD_DIM, D_STATE)
    return y.astype(z.dtype), conv_new, h.astype(z.dtype)

def sink_softmax(s, sink):
    m = jnp.maximum(jnp.max(s, axis=-1, keepdims=True), sink)
    e = jnp.exp(s - m)
    return e / (jnp.sum(e, axis=-1, keepdims=True) + jnp.exp(sink - m))

def swa_prompt(q, k, v, sinks):
    b, T = q.shape[0], q.shape[1]
    nc = T // CHUNK
    qc = q.reshape(b, nc, CHUNK, N_KV_HEADS, Q_PER_KV, HEAD_DIM)
    def band(t):
        tc = t.reshape(b, nc, CHUNK, N_KV_HEADS, HEAD_DIM)
        tp = jnp.pad(tc, ((0, 0), (PREV_CHUNKS, 0), (0, 0), (0, 0), (0, 0)))
        return jnp.concatenate([tp[:, i:i + nc] for i in range(PREV_CHUNKS + 1)], axis=2)
    kb, vb = band(k), band(v)
    s = jnp.einsum('bcqkrd,bcskd->bckrqs', qc, kb, preferred_element_type=jnp.float32) * (HEAD_DIM ** -0.5)
    key_chunk = jnp.arange(nc)[:, None] + (jnp.arange((PREV_CHUNKS + 1) * CHUNK) // CHUNK - PREV_CHUNKS)[None, :]
    valid = (key_chunk >= 0)[None, :, None, None, None, :]
    s = jnp.where(valid, s, jnp.finfo(jnp.float32).min)
    pr = sink_softmax(s, sinks)
    o = jnp.einsum('bckrqs,bcskd->bcqkrd', pr.astype(v.dtype), vb)
    return o.reshape(b, T, N_HEADS * HEAD_DIM)

def swa_cached(q, k, v, cache_k, cache_v, sinks):
    b, S = q.shape[0], q.shape[1]
    kk = jnp.concatenate([cache_k.astype(k.dtype), k], axis=1)
    vv = jnp.concatenate([cache_v.astype(v.dtype), v], axis=1)
    qg = q.reshape(b, S, N_KV_HEADS, Q_PER_KV, HEAD_DIM)
    s = jnp.einsum('bqkrd,bskd->bkrqs', qg, kk, preferred_element_type=jnp.float32) * (HEAD_DIM ** -0.5)
    pr = sink_softmax(s, sinks)
    o = jnp.einsum('bkrqs,bskd->bqkrd', pr.astype(vv.dtype), vv).reshape(b, S, N_HEADS * HEAD_DIM)
    rows = cache_k.shape[1]
    return o, kk[:, -rows:], vv[:, -rows:]

def layer(x, c, pos, conv_ctx, h0, kv_ctx, ffn_ctx, p):
    b, T = x.shape[0], x.shape[1]
    mod = jax.nn.silu(c) @ p['w_ada'] + p['b_ada']
    sh1, sc1, g1, sh2, sc2, g2 = jnp.split(mod[:, None, :], 6, axis=-1)
    hn = rmsnorm(x, p['norm_mix_pre']) * (1 + sc1) + sh1
    proj = hn @ p['w_in']
    z, xbc, dt, q, k, v, gates = jnp.split(proj, IN_SPLITS, axis=-1)
    y_ssm, conv_new, h_new = ssm_branch(z, xbc, dt, conv_ctx, h0, p)
    q = partial_rope(q.reshape(b, T, N_HEADS, HEAD_DIM), pos)
    k = partial_rope(k.reshape(b, T, N_KV_HEADS, HEAD_DIM), pos)
    v = v.reshape(b, T, N_KV_HEADS, HEAD_DIM)
    sinks = p['attn_sinks'].astype(jnp.float32).reshape(N_KV_HEADS, Q_PER_KV, 1, 1)
    if kv_ctx is None:
        y_att = swa_prompt(q, k, v, sinks)
        rows = min(WINDOW, PAST_LEN)
        k_new, v_new = k[:, -rows:], v[:, -rows:]
    else:
        y_att, k_new, v_new = swa_cached(q, k, v, kv_ctx[0], kv_ctx[1], sinks)
    g_ssm, g_att = jnp.split(jax.nn.sigmoid(gates), 2, axis=-1)
    merged = g_ssm * (y_ssm @ p['w_ssm_out']) + g_att * (y_att @ p['w_att_out'])
    x = x + g1 * rmsnorm(merged @ p['w_out'], p['norm_mix_post'])
    hn = rmsnorm(x, p['norm_ffn_pre']) * (1 + sc2) + sh2
    gate, up = jnp.split(hn @ p['w_ffn_in'], 2, axis=-1)
    gate, ffn_new = causal_dwconv(gate, ffn_ctx, p['ffn_conv_w'], p['ffn_conv_b'])
    f = (jax.nn.silu(gate) * up) @ p['w_ffn_out']
    x = x + g2 * rmsnorm(f, p['norm_ffn_post'])
    return x, (h_new, conv_new, k_new, v_new, ffn_new)

def setup_inputs(seed: int = 0) -> dict:
    key = jax.random.key(seed)
    ks = jax.random.split(key, 40)
    f32 = jnp.float32
    def nrm(i, shape, scale):
        return jax.random.normal(ks[i], shape, f32) * scale
    def gain(i, shape):
        return 1.0 + 0.05 * jax.random.normal(ks[i], shape, f32)
    rows = min(WINDOW, PAST_LEN)
    dt0 = jnp.exp(jax.random.uniform(ks[30], (DEPTH, SSM_HEADS), f32, math.log(1e-3), math.log(1e-1)))
    return {
        'x_prompt': nrm(0, (BATCH, SEQ, D_MODEL), 1.0),
        'x_sample': nrm(1, (DEC_BATCH, DEC_SEQ, D_MODEL), 1.0),
        'cache_k': nrm(2, (DEPTH, DEC_BATCH, rows, N_KV_HEADS, HEAD_DIM), 1.0),
        'cache_v': nrm(3, (DEPTH, DEC_BATCH, rows, N_KV_HEADS, HEAD_DIM), 1.0),
        'state_ssm': nrm(4, (DEPTH, DEC_BATCH, SSM_HEADS, SSM_HEAD_DIM, D_STATE), 0.1),
        'state_conv': nrm(5, (DEPTH, DEC_BATCH, SSM_CONV - 1, CONV_DIM), 1.0),
        'state_ffn_conv': nrm(6, (DEPTH, DEC_BATCH, FFN_CONV - 1, D_FF), 1.0),
        'c_prompt': nrm(7, (BATCH, D_MODEL), 1.0),
        'c_sample': nrm(8, (DEC_BATCH, D_MODEL), 1.0),
        'w_ada': nrm(9, (DEPTH, D_MODEL, 6 * D_MODEL), 0.5 * D_MODEL ** -0.5),
        'b_ada': nrm(10, (DEPTH, 6 * D_MODEL), 0.02),
        'norm_mix_pre': gain(11, (DEPTH, D_MODEL)),
        'norm_mix_post': gain(12, (DEPTH, D_MODEL)),
        'w_in': nrm(13, (DEPTH, D_MODEL, IN_WIDTH), D_MODEL ** -0.5),
        'ssm_conv_w': nrm(14, (DEPTH, SSM_CONV, CONV_DIM), SSM_CONV ** -0.5),
        'ssm_conv_b': nrm(15, (DEPTH, CONV_DIM), 0.02),
        'ssm_dt_bias': dt0 + jnp.log(-jnp.expm1(-dt0)),
        'ssm_a_log': jnp.log(jax.random.uniform(ks[16], (DEPTH, SSM_HEADS), f32, 1.0, 16.0)),
        'ssm_d': gain(17, (DEPTH, SSM_HEADS)),
        'ssm_norm': gain(18, (DEPTH, D_INNER)),
        'attn_sinks': nrm(19, (DEPTH, N_HEADS), 0.5),
        'w_ssm_out': nrm(20, (DEPTH, D_INNER, D_MODEL), D_INNER ** -0.5),
        'w_att_out': nrm(21, (DEPTH, N_HEADS * HEAD_DIM, D_MODEL), (N_HEADS * HEAD_DIM) ** -0.5),
        'w_out': nrm(22, (DEPTH, D_MODEL, D_MODEL), D_MODEL ** -0.5),
        'norm_ffn_pre': gain(23, (DEPTH, D_MODEL)),
        'norm_ffn_post': gain(24, (DEPTH, D_MODEL)),
        'w_ffn_in': nrm(25, (DEPTH, D_MODEL, 2 * D_FF), D_MODEL ** -0.5),
        'ffn_conv_w': nrm(26, (DEPTH, FFN_CONV, D_FF), FFN_CONV ** -0.5),
        'ffn_conv_b': nrm(27, (DEPTH, D_FF), 0.02),
        'w_ffn_out': nrm(28, (DEPTH, D_FF, D_MODEL), D_FF ** -0.5),
    }

def reference(x_prompt, x_sample, cache_k, cache_v, state_ssm, state_conv, state_ffn_conv, c_prompt, c_sample,
              w_ada, b_ada, norm_mix_pre, norm_mix_post, w_in, ssm_conv_w, ssm_conv_b, ssm_dt_bias, ssm_a_log,
              ssm_d, ssm_norm, attn_sinks, w_ssm_out, w_att_out, w_out, norm_ffn_pre, norm_ffn_post,
              w_ffn_in, ffn_conv_w, ffn_conv_b, w_ffn_out):
    bp, tp = x_prompt.shape[0], x_prompt.shape[1]
    pos_p = jnp.arange(tp)
    pos_s = PAST_LEN + jnp.arange(x_sample.shape[1])
    yp, ys = x_prompt, x_sample
    st_p, st_s = [], []
    for l in range(DEPTH):
        p = {
            'w_ada': w_ada[l], 'b_ada': b_ada[l], 'norm_mix_pre': norm_mix_pre[l], 'norm_mix_post': norm_mix_post[l],
            'w_in': w_in[l], 'ssm_conv_w': ssm_conv_w[l], 'ssm_conv_b': ssm_conv_b[l], 'ssm_dt_bias': ssm_dt_bias[l],
            'ssm_a_log': ssm_a_log[l], 'ssm_d': ssm_d[l], 'ssm_norm': ssm_norm[l], 'attn_sinks': attn_sinks[l],
            'w_ssm_out': w_ssm_out[l], 'w_att_out': w_att_out[l], 'w_out': w_out[l],
            'norm_ffn_pre': norm_ffn_pre[l], 'norm_ffn_post': norm_ffn_post[l], 'w_ffn_in': w_ffn_in[l],
            'ffn_conv_w': ffn_conv_w[l], 'ffn_conv_b': ffn_conv_b[l], 'w_ffn_out': w_ffn_out[l],
        }
        conv0 = jnp.zeros((bp, SSM_CONV - 1, CONV_DIM), x_prompt.dtype)
        h0 = jnp.zeros((bp, SSM_HEADS, SSM_HEAD_DIM, D_STATE), jnp.float32)
        ffn0 = jnp.zeros((bp, FFN_CONV - 1, D_FF), x_prompt.dtype)
        yp, sp = layer(yp, c_prompt, pos_p, conv0, h0, None, ffn0, p)
        ys, ss = layer(ys, c_sample, pos_s, state_conv[l], state_ssm[l], (cache_k[l], cache_v[l]), state_ffn_conv[l], p)
        st_p.append(sp)
        st_s.append(ss)
    ssm_p, conv_p, k_p, v_p, ffn_p = [jnp.stack(t) for t in zip(*st_p)]
    ssm_s, conv_s, k_s, v_s, ffn_s = [jnp.stack(t) for t in zip(*st_s)]
    return (yp, ys, ssm_p, conv_p, k_p, v_p, ffn_p, ssm_s, conv_s, k_s, v_s, ffn_s)


_drawn_inputs = setup_inputs


def setup_inputs(seed=0):
    import zlib

    import numpy as np

    out = dict(_drawn_inputs(seed))
    spreads = {}
    factors = {'norm_mix_post': 3.79,
     'ssm_d': 8.0,
     'ssm_norm': 4.084,
     'attn_sinks': 32.037,
     'norm_ffn_post': 4.316,
     'ffn_conv_b': 8.0}
    for name, (base, spread) in spreads.items():
        noise = np.random.default_rng([zlib.crc32(name.encode()), seed]).standard_normal(out[name].shape)
        drawn = base * np.exp(spread * noise) if base else spread * noise
        out[name] = __import__('jax').numpy.asarray(drawn.astype(out[name].dtype))
    for name, factor in factors.items():
        out[name] = (out[name] * factor).astype(out[name].dtype)
    return out
```

```python
from contextlib import ExitStack

import concourse.bass as bass
import numpy as np
from concourse import mybir

F32 = mybir.dt.float32
F32R = mybir.dt.float32r
ALU = mybir.AluOpType
ACT = mybir.ActivationFunctionType
AX = mybir.AxisListType

P = 128
D = 1024
KB = D // P
T, S = 512, 32
GAP = 4
S0 = T + GAP
TW = S0 + S
HW = TW // 2
LEAD = 4
GROUPS, HPG, HD, NS = 8, 4, 64, 128
GT = 6
KV, CH, WIN = 4, 64, 128
KEYS = WIN + CH
FT = 22
ATT_CHUNKS = T // CH
EPS = 1e-6
TAPS, FTAPS = 4, 3
GP_W, GP_B, GP_CTX, GP_D, GP_N = 0, 16, 20, 32, 34
SCAN = [(128 * c, 128) for c in range(T // 128)] + [(S0, S)]
RAW_SLOTS, HL_SLOTS = 3, 2
ADA_W = 512
ADA_UP = 2 * D // ADA_W
ADA_LATE = 4 * D // ADA_W
assert ADA_LATE == GROUPS
RANGES = [(0, T, 0), (S0, S, 1)]


def halves(ap):
    return ap.rearrange("p (a b) -> p a b", a=2)


def flat(t):
    return t[:].rearrange("p a b -> p (a b)")


def bcast_mid(ap, n):
    return ap.unsqueeze(2).to_broadcast((ap.shape[0], ap.shape[1], n))


def build_layer(nc, i, o, scratch):
    top = ExitStack()

    def sb(stack, name, shape, dt=F32):
        return stack.enter_context(nc.sbuf_tensor(name, shape, dt))

    def sems(stack, names):
        return [stack.enter_context(nc.semaphore(n)) for n in names.split()]

    with top:
        psum = top.enter_context(nc.psum_tensor("psum", [P, 8, 512], F32))
        ident = sb(top, "ident", [P, P])
        ones = sb(top, "ones", [P, P])
        consts = sb(top, "consts", [P, 2])
        eps_c, one_c = consts[:, 0:1], consts[:, 1:2]
        vecs = sb(top, "vecs", [P, 4, KB])
        mod = sb(top, "mod", [P, 48, 2])
        gain = sb(top, "gain", [P, 2, KB, 2])
        gate = sb(top, "gate", [P, 2, KB, 2])
        c_silu = sb(top, "c_silu", [P, KB, 2])
        b_ada = sb(top, "b_ada", [P, 48])
        raw_w = [sb(top, f"raw_w{n}", [P, D]) for n in range(RAW_SLOTS)]
        w_hi = [sb(top, f"w_hi{n}", [P, KB, P], F32R) for n in range(HL_SLOTS)]
        w_lo = [sb(top, f"w_lo{n}", [P, KB, P], F32R) for n in range(HL_SLOTS)]
        hp_hi = sb(top, "hp_hi", [P, KB, TW], F32R)
        hp_lo = sb(top, "hp_lo", [P, KB, TW], F32R)

        def slot(s):
            return psum[:, 2 * s:2 * s + 2, 0:HW]

        class Stream:

            def __init__(self, stack, tag, sources, base, ready, following):
                self.own, self.src, self.base = len(sources), sources + following, base
                self.raw_ready, self.hl_ready = (RAW_SLOTS, HL_SLOTS) if ready else (0, 0)
                self.landed = sems(stack, " ".join(f"{tag}_landed{n}" for n in range(RAW_SLOTS)))
                self.hi_done, self.lo_done, self.used = sems(stack, f"{tag}_hi {tag}_lo {tag}_used")
                self.all = [*self.landed, self.hi_done, self.lo_done, self.used]
                self.block = 0

            def raw_slot(self, n):
                return (self.base + n) % RAW_SLOTS

            def hl_slot(self, n):
                return (self.base + n) % HL_SLOTS

            def landings(self, n):
                return (n - self.raw_ready) // RAW_SLOTS + 1

            def load(self, sp, n):
                if not self.raw_ready <= n < len(self.src):
                    return
                if n - RAW_SLOTS >= self.hl_ready:
                    sp.wait_ge(self.lo_done, n - RAW_SLOTS - self.hl_ready + 1)
                sp.dma_start(raw_w[self.raw_slot(n)][:], self.src[n]).then_inc(self.landed[self.raw_slot(n)], 16)

            def all_landed(self, sp):
                for n in range(max(len(self.src) - RAW_SLOTS, self.raw_ready), len(self.src)):
                    sp.wait_ge(self.landed[self.raw_slot(n)], 16 * self.landings(n))

            def splits(self, n):
                return self.hl_ready <= n < min(self.own + HL_SLOTS, len(self.src))

            def split_hi(self, act, n):
                if not self.splits(n):
                    return
                if n >= self.raw_ready:
                    act.wait_ge(self.landed[self.raw_slot(n)], 16 * self.landings(n))
                if n >= HL_SLOTS:
                    act.wait_ge(self.used, n - HL_SLOTS + 1)
                act.activation(flat(w_hi[self.hl_slot(n)]), raw_w[self.raw_slot(n)][:], ACT.Copy).then_inc(self.hi_done, 1)

            def split_lo(self, eng, n):
                if not self.splits(n):
                    return
                eng.wait_ge(self.hi_done, n - self.hl_ready + 1)
                eng.tensor_tensor(flat(w_lo[self.hl_slot(n)]), raw_w[self.raw_slot(n)][:],
                                  flat(w_hi[self.hl_slot(n)]).bitcast(F32), ALU.subtract).then_inc(self.lo_done, 1)

            def all_split(self, eng):
                eng.wait_ge(self.lo_done, min(self.own + HL_SLOTS, len(self.src)) - self.hl_ready)

            def wait_split(self, pe, n):
                if n >= self.hl_ready:
                    pe.wait_ge(self.lo_done, n - self.hl_ready + 1)

            def multiply(self, pe, out, hi, lo, first, last, done=None):
                n, k = divmod(self.block, KB)
                self.block += 1
                if k == 0:
                    self.wait_split(pe, n)
                wh, wl = w_hi[self.hl_slot(n)][:, k, :], w_lo[self.hl_slot(n)][:, k, :]
                for h in range(2):
                    cols = slice(h * HW, (h + 1) * HW)
                    for j, (w, x) in enumerate(((wh, hi), (wh, lo), (wl, hi))):
                        mm = pe.matmul(out[:, h, :], w, x[:, cols], start=first and j == 0, stop=last and j == 2)
                if k == KB - 1:
                    mm.then_inc(self.used, 1)
                elif done is not None:
                    mm.then_inc(done, 1)

        def chain(sem):
            count = [0]

            def link(eng, ins):
                count[0] += 1
                ins.then_inc(sem, 1)
                eng.wait_ge(sem, count[0])
            return link

        with ExitStack() as st:
            ada = [sb(st, f"ada{n}", [P, KB, ADA_W]) for n in range(ADA_UP)]
            mod_row = sb(st, "mod_row", [2, ADA_UP, ADA_W])
            x = sb(st, "x", [P, KB, TW])
            c_in = sb(st, "c_in", [P, KB, 2])
            c_th = sb(st, "c_th", [P, KB, 2])
            sq = [sb(st, f"sq{n}", [P, TW]) for n in range(2)]
            rstd = sb(st, "rstd", [P, TW])
            h = [sb(st, f"h{n}", [P, TW]) for n in range(2)]
            xr = [sb(st, f"xr{n}", [P, TW]) for n in range(2)]
            (in_x, in_c, c_s, ada_done, row_s, turn_s, sq_s, root_s, dve_s, h_s, hi_s, sq_used, const_s,
             lo_s) = sems(
                st, "a_x a_c a_silu a_ada_done a_row a_turn a_sq a_root a_dve a_h a_hi a_squsd a_const a_lo")
            in_ada = sems(st, " ".join(f"a_ada{n}" for n in range(2 * ADA_UP)))
            w = Stream(st, "aw", [], 0, False, [i["w_qkv"][n] for n in range(RAW_SLOTS)])
            first_sem = in_x.num
            with nc.Block(no_gpsimd_drain=True) as block:
                @block.sync
                def _(sp):
                    sp.dma_start(c_in[:], i["c"]).then_inc(in_c, 16)
                    sp.dma_start(ident[:], i["ident"]).then_inc(in_c, 16)
                    sp.dma_start(consts[:], i["consts"]).then_inc(in_c, 16)
                    sp.dma_start(vecs[:], i["vecs"]).then_inc(in_c, 16)
                    sp.dma_start(b_ada[:], i["b_ada"]).then_inc(in_c, 16)
                    sp.dma_start(x[:], i["x"]).then_inc(in_x, 16)
                    for n in range(2 * ADA_UP):
                        a, ks = n // 2, slice(KB // 2 * (n % 2), KB // 2 * (n % 2 + 1))
                        sp.dma_start(ada[a][:, ks, :], i["w_ada"][ADA_LATE + a, :, ks, :]).then_inc(in_ada[n], 16)
                    for n in range(RAW_SLOTS):
                        w.load(sp, n)
                    w.all_landed(sp)

                @block.gpsimd
                def _(pool):
                    pool.memset(ones[:], 1.0).then_inc(const_s, 1)
                    pool.memset(h[0][:, T:S0], 0.0).then_inc(const_s, 1)
                    pool.memset(h[1][:, T:S0], 0.0).then_inc(const_s, 1)
                    for n in range(HL_SLOTS):
                        w.split_lo(pool, n)
                    for t in range(KB):
                        pool.wait_ge(hi_s, t + 1)
                        pool.tensor_tensor(hp_lo[:, t, :], h[t % 2][:], hp_hi[:, t, :].bitcast(F32),
                                           ALU.subtract).then_inc(lo_s, 1)
                    w.all_split(pool)
                    pool.wait_ge(lo_s, KB)

                @block.scalar
                def _(act):
                    act.wait_ge(in_c, 80)
                    act.activation(c_th[:], c_in[:], ACT.Tanh, scale=0.5).then_inc(c_s, 1)
                    act.wait_ge(in_x, 16)
                    for t in range(KB):
                        if t >= 2:
                            act.wait_ge(sq_used, t - 1)
                        act.activation(sq[t % 2][:], x[:, t, :], ACT.Square).then_inc(sq_s, 1)
                    act.wait_ge(sq_used, KB)
                    act.activation(halves(rstd[:]), slot(0), ACT.Sqrt, bias=eps_c, scale=1.0 / D).then_inc(root_s, 1)
                    for a in range(ADA_UP):
                        act.wait_ge(ada_done, a + 1)
                        act.activation(mod_row[:, a, :], psum[0:2, 2 + a, :], ACT.Copy).then_inc(row_s, 1)
                    for n in range(HL_SLOTS):
                        w.split_hi(act, n)
                    for t in range(KB):
                        act.wait_ge(h_s, t + 1)
                        act.activation(hp_hi[:, t, :], h[t % 2][:], ACT.Copy).then_inc(hi_s, 1)

                @block.vector
                def _(dve):
                    link = chain(dve_s)
                    dve.wait_ge(c_s, 1)
                    link(dve, dve.scalar_tensor_tensor(out=c_silu[:], in0=c_th[:], scalar=1.0, in1=c_in[:],
                                                       op0=ALU.add, op1=ALU.mult))
                    dve.tensor_scalar(c_silu[:], c_silu[:], 0.5, None, ALU.mult).then_inc(c_s, 1)
                    dve.wait_ge(root_s, 1)
                    link(dve, dve.reciprocal(rstd[:], rstd[:]))
                    dve.wait_ge(turn_s, 1)
                    link(dve, dve.tensor_tensor(mod[:, 0:2 * KB, :], psum[:, 6, 0:4 * KB].rearrange("p (a b) -> p a b", b=2),
                                                bcast_mid(b_ada[:, 0:2 * KB], 2), ALU.add))
                    link(dve, dve.scalar_tensor_tensor(out=gain[:, 0], in0=mod[:, KB:2 * KB, :], scalar=1.0,
                                                       in1=bcast_mid(vecs[:, 0, :], 2), op0=ALU.add, op1=ALU.mult))
                    dve.wait_ge(const_s, 3)
                    for t in range(KB):
                        link(dve, dve.tensor_tensor(xr[t % 2][:], x[:, t, :], rstd[:], ALU.mult))
                        if t >= 2:
                            dve.wait_ge(lo_s, t - 1)
                        dve.tensor_scalar(h[t % 2][:, 0:T], xr[t % 2][:, 0:T], gain[:, 0, t, 0:1],
                                          mod[:, t, 0:1], ALU.mult, ALU.add)
                        dve.tensor_scalar(h[t % 2][:, S0:TW], xr[t % 2][:, S0:TW], gain[:, 0, t, 1:2],
                                          mod[:, t, 1:2], ALU.mult, ALU.add).then_inc(h_s, 1)

                @block.tensor
                def _(pe):
                    pe.wait_ge(const_s, 1)
                    for t in range(KB):
                        pe.wait_ge(sq_s, t + 1)
                        for hh in range(2):
                            mm = pe.matmul(psum[:, hh, 0:HW], ones[:], sq[t % 2][:, hh * HW:(hh + 1) * HW],
                                           start=t == 0, stop=t == KB - 1)
                        mm.then_inc(sq_used, 1)
                    pe.wait_ge(c_s, 2)
                    for n in range(2 * ADA_UP):
                        a, half = divmod(n, 2)
                        pe.wait_ge(in_ada[n], 16)
                        for k in range(KB // 2 * half, KB // 2 * (half + 1)):
                            mm = pe.matmul(psum[0:2, 2 + a, :], c_silu[:, k, :], ada[a][:, k, :], start=k == 0, stop=k == KB - 1)
                        if half:
                            mm.then_inc(ada_done, 1)
                    pe.wait_ge(in_c, 80)
                    for t in range(2 * KB):
                        a, b = divmod(t, ADA_W // P)
                        if b == 0:
                            pe.wait_ge(row_s, a + 1)
                        mm = pe.transpose(psum[:, 6, 2 * t:2 * t + 2], mod_row[:, a, b * P:(b + 1) * P], ident[0:2, 0:2])
                    mm.then_inc(turn_s, 1)

        with ExitStack() as loop_st:
            raw = sb(loop_st, "raw", [P, GT, LEAD + TW])
            gp_all = sb(loop_st, "gp_all", [P, GROUPS, GP_N])
            tok_all = sb(loop_st, "tok_all", [P, GROUPS, 5, 3, HPG])
            mask_u = sb(loop_st, "mask_u", [P, P])
            ada = sb(loop_st, "ada_g", [P, KB, ADA_W])

            def group_chunk(n):
                return i["w_grp"][bass.ds(n * P, P), :]

            with ExitStack() as st:
                cos = sb(st, "cos", [P, TW])
                sin = sb(st, "sin", [P, TW])
                rot = sb(st, "rot", [P, P])
                zeros = sb(st, "zeros", [P, 256])
                qk = [sb(st, f"qk{n}", [P, TW]) for n in range(2)]
                t_cos = [sb(st, f"t_cos{n}", [P, TW]) for n in range(2)]
                qk_rot = [sb(st, f"qk_rot{n}", [P, TW]) for n in range(2)]
                v_sb = sb(st, "v_sb", [P, 5, 256])
                dt_v = sb(st, "dt_v", [32, TW])
                dt_n = sb(st, "dt_n", [32, TW])
                dt_e = sb(st, "dt_e", [32, TW])
                dt_l = sb(st, "dt_l", [32, TW])
                dt = sb(st, "dt", [32, TW])
                da = sb(st, "da", [32, TW])
                acs = sb(st, "acs", [32, TW])
                edt = sb(st, "edt", [32, TW])
                dt_par = sb(st, "dt_par", [32, 2])
                a_exp = sb(st, "a_exp", [32, 1])
                NK, NQ = 2, 8
                QK = NK + NQ
                DT, V0, G0 = QK, QK + 1, QK + 3
                w = Stream(st, "b", [i["w_qkv"][n] for n in range(QK + 3)] + [group_chunk(n) for n in range(GT)],
                           0, True, [group_chunk(GT + n) for n in range(RAW_SLOTS)])
                NCH = w.own
                (in_s, init_s, evac_s, rot_s, rope_s, out_s0, out_s1, copy_s, acs_s, tr_s, dtp_s, sc_s,
                 dve_s, e_s) = sems(
                    st, "b_in b_init b_evac b_rot b_rope b_out0 b_out1 b_copy b_acs b_tr b_dtp b_sc b_dve b_e")
                ada_in, = sems(st, "b_ada_in")
                out_s = [out_s0, out_s1]

                def q_dst(t):
                    return scratch["q"][:, :, t, :].rearrange("c p k -> p c k")

                with nc.Block(no_gpsimd_drain=True) as block:
                    @block.sync
                    def _(sp):
                        for n in range(RAW_SLOTS, RAW_SLOTS + HL_SLOTS):
                            w.load(sp, n)
                        for dst, name in ((cos, "cos"), (sin, "sin"), (rot, "rot"), (dt_par, "dt_par"),
                                          (gp_all, "gp"), (mask_u, "mask_u")):
                            sp.dma_start(dst[:], i[name]).then_inc(in_s, 16)
                        sp.wait_ge(init_s, 1)
                        sp.dma_start(scratch["k"][:, 0:2, 0:WIN], zeros[0:64, :].rearrange("p (a b) -> p a b", a=2)).then_inc(copy_s, 16)
                        sp.dma_start(scratch["k"][:, 2:4, 0:WIN], zeros[0:64, :].rearrange("p (a b) -> p a b", a=2)).then_inc(copy_s, 16)
                        sp.dma_start(scratch["v"][0:WIN, :], zeros[:]).then_inc(copy_s, 16)
                        sp.dma_start(scratch["att"][:, :, T:S0], zeros[:, 0:KB * GAP].rearrange("p (a b) -> p a b", a=KB)).then_inc(copy_s, 16)
                        sp.dma_start(scratch["ks"][:, :, 0:WIN], i["cache_k"]).then_inc(copy_s, 16)
                        sp.dma_start(scratch["vs"][0:WIN, :], i["cache_v"]).then_inc(copy_s, 16)
                        for j in range(NK):
                            for a in range(2):
                                kv = 2 * j + a
                                sp.dma_start(o["k_s"][64 * kv:64 * kv + 64, 0:WIN - S], i["cache_k"][:, kv, S:WIN]).then_inc(copy_s, 16)
                        sp.dma_start(o["v_s"][0:WIN - S, :], i["cache_v"][S:WIN, :]).then_inc(copy_s, 16)
                        n_copy = 11
                        sp.dma_start(ada[:], i["w_ada"][0]).then_inc(ada_in, 16)
                        for n in range(RAW_SLOTS + HL_SLOTS, NCH):
                            w.load(sp, n)
                            j = n - RAW_SLOTS - HL_SLOTS
                            if j < QK:
                                sp.wait_ge(rope_s, j + 1)
                                r = qk_rot[j % 2]
                                if j < NK:
                                    for a in range(2):
                                        rows, kv = slice(64 * a, 64 * a + 64), 2 * j + a
                                        sp.dma_start(scratch["k"][:, kv, WIN:WIN + T], r[rows, 0:T]).then_inc(out_s[j % 2], 16)
                                        sp.dma_start(scratch["ks"][:, kv, WIN:WIN + S], r[rows, S0:TW]).then_inc(out_s[j % 2], 16)
                                    sp.dma_start(o["k_p"][P * j:P * j + P, :], r[:, T - WIN:T]).then_inc(out_s[j % 2], 16)
                                    sp.dma_start(o["k_s"][P * j:P * j + P, WIN - S:WIN], r[:, S0:TW]).then_inc(out_s[j % 2], 16)
                                else:
                                    t = j - NK
                                    sp.dma_start(q_dst(t), r[:, 0:T].rearrange("p (c k) -> p c k", k=CH)).then_inc(out_s[j % 2], 16)
                                    sp.dma_start(scratch["qs"][:, t, :], r[:, S0:TW]).then_inc(out_s[j % 2], 16)
                        sp.wait_ge(evac_s, G0)
                        sp.dma_start(scratch["v"][WIN:WIN + T, :].rearrange("(a p) d -> p a d", p=P), v_sb[:, 0:4, :]).then_inc(copy_s, 16)
                        sp.dma_start(scratch["vs"][WIN:WIN + S, :], v_sb[0:S, 4, :]).then_inc(copy_s, 16)
                        sp.dma_start(o["v_p"], v_sb[:, 3, :]).then_inc(copy_s, 16)
                        sp.dma_start(o["v_s"][WIN - S:WIN, :], v_sb[0:S, 4, :]).then_inc(copy_s, 16)
                        sp.wait_ge(acs_s, 1)
                        sp.dma_start(scratch["acs"], acs[:]).then_inc(copy_s, 16)
                        for n in range(NCH, NCH + RAW_SLOTS):
                            w.load(sp, n)
                        w.all_landed(sp)
                        sp.wait_ge(ada_in, 16)
                        sp.wait_ge(copy_s, 16 * (n_copy + 5))
                        for s in out_s:
                            sp.wait_ge(s, 96 + 32 * (NQ // 2))

                    @block.gpsimd
                    def _(pool):
                        pool.memset(zeros[:], 0.0).then_inc(init_s, 1)
                        pool.memset(raw[:, :, 0:LEAD], 0.0).then_inc(init_s, 1)
                        pool.memset(acs[:], 0.0).then_inc(init_s, 1)
                        pool.memset(edt[:], 0.0).then_inc(init_s, 1)
                        pool.memset(tok_all[:], 0.0).then_inc(init_s, 1)
                        for n in range(NCH + HL_SLOTS):
                            w.split_lo(pool, n)
                        w.all_split(pool)

                    @block.scalar
                    def _(act):
                        for n in range(NCH):
                            w.split_hi(act, n + 2)
                            act.wait_ge(w.used, n + 1)
                            if n < QK:
                                if n >= 2:
                                    act.wait_ge(rope_s, n - 1)
                                act.activation(halves(qk[n % 2][:]), slot(n % 2), ACT.Copy).then_inc(evac_s, 1)
                            elif n == DT:
                                act.wait_ge(in_s, 96)
                                act.activation(halves(dt_v[:]), psum[0:32, 2 * (n % 2):2 * (n % 2) + 2, 0:HW], ACT.Identity,
                                               bias=dt_par[:, 0:1]).then_inc(evac_s, 1)
                                act.activation(a_exp[:], dt_par[:, 1:2], ACT.Exp).then_inc(e_s, 1)
                                act.wait_ge(dtp_s, 1)
                                act.activation(dt_e[:], dt_n[:], ACT.Exp).then_inc(e_s, 1)
                                act.wait_ge(e_s, 2)
                                act.activation(dt_l[:], dt_e[:], ACT.Ln, bias=one_c[0:32]).then_inc(e_s, 1)
                            elif n < G0:
                                j = n - V0
                                b = 2 * (n % 2)
                                act.activation(v_sb[:, 0:4, j * P:(j + 1) * P],
                                               psum[:, b, :].rearrange("p (a c) -> p a c", a=4), ACT.Copy)
                                act.activation(v_sb[0:S, 4, j * P:(j + 1) * P], psum[0:S, b + 1, 0:P], ACT.Copy).then_inc(evac_s, 1)
                            else:
                                if n == G0:
                                    act.wait_ge(acs_s, 1)
                                    for ci, (c0, L) in enumerate(SCAN):
                                        act.activation(edt[:, c0:c0 + L], acs[:, c0:c0 + L], ACT.Exp, scale=-1.0,
                                                       bias=acs[:, c0 + L - 1:c0 + L]).then_inc(sc_s, 1)
                                    act.wait_ge(init_s, 5)
                                act.activation(halves(raw[:, n - G0, LEAD:]), slot(n % 2), ACT.Copy).then_inc(evac_s, 1)

                    @block.vector
                    def _(dve):
                        link = chain(dve_s)
                        dve.wait_ge(in_s, 96)
                        for n in range(QK):
                            dve.wait_ge(evac_s, n + 1)
                            if n >= 2:
                                dve.wait_ge(out_s[n % 2], 96 + 32 * ((n - 2) // 2))
                            link(dve, dve.tensor_tensor(t_cos[n % 2][:], qk[n % 2][:], cos[:], ALU.mult))
                            dve.wait_ge(rot_s, n + 1)
                            link(dve, dve.tensor_tensor(halves(qk_rot[n % 2][:]), slot(2 + n % 2), halves(sin[:]), ALU.mult))
                            dve.tensor_tensor(qk_rot[n % 2][:], qk_rot[n % 2][:], t_cos[n % 2][:], ALU.add).then_inc(rope_s, 1)
                        dve.wait_ge(evac_s, DT + 1)
                        dve.scalar_tensor_tensor(out=dt_n[:], in0=dt_v[:], scalar=-1.0, in1=dt_v[:], op0=ALU.mult,
                                                 op1=ALU.min).then_inc(dtp_s, 1)
                        dve.wait_ge(e_s, 3)
                        dve.wait_ge(init_s, 5)
                        link(dve, dve.scalar_tensor_tensor(out=dt[:], in0=dt_v[:], scalar=0.0, in1=dt_l[:], op0=ALU.max, op1=ALU.add))
                        link(dve, dve.tensor_scalar(da[:], dt[:], a_exp[:], -1.0, ALU.mult, ALU.mult))
                        for c0, L in SCAN:
                            ins = dve.tensor_tensor_scan(acs[:, c0:c0 + L], ones[0:32, 0:L], da[:, c0:c0 + L], 0.0,
                                                         ALU.mult, ALU.add)
                        ins.then_inc(acs_s, 1)
                        dve.wait_ge(sc_s, 5)
                        dve.tensor_tensor(edt[:], edt[:], dt[:], ALU.mult).then_inc(sc_s, 1)
                        dve.wait_ge(tr_s, 1)
                        for ci, (c0, L) in enumerate(SCAN):
                            ins = dve.tensor_copy(tok_all[0:L, :, ci, :, :],
                                            psum[0:L, 7, 96 * ci:96 * ci + 96].rearrange("p (a g r) -> p g a r", a=3, g=GROUPS))
                        link(dve, ins)

                    @block.tensor
                    def _(pe):
                        for n in range(NCH):
                            if n >= 2:
                                pe.wait_ge(evac_s, n - 1)
                            if V0 <= n < G0:
                                w.wait_split(pe, n)
                                wh, wl = w_hi[w.hl_slot(n)], w_lo[w.hl_slot(n)]
                                for a, (c0, L) in enumerate(SCAN):
                                    out = psum[0:L, 2 * (n % 2) + a // 4, (a % 4) * P:(a % 4 + 1) * P]
                                    for k in range(KB):
                                        xh, xl = hp_hi[:, k, c0:c0 + L], hp_lo[:, k, c0:c0 + L]
                                        for j, (p, q) in enumerate(((xh, wh), (xl, wh), (xh, wl))):
                                            mm = pe.matmul(out, p, q[:, k, :], start=k == 0 and j == 0, stop=k == KB - 1 and j == 2)
                                mm.then_inc(w.used, 1)
                                w.block += KB
                            else:
                                for k in range(KB):
                                    w.multiply(pe, slot(n % 2), hp_hi[:, k, :], hp_lo[:, k, :], k == 0, k == KB - 1)
                            if 1 <= n <= QK:
                                j = n - 1
                                if j == 0:
                                    pe.wait_ge(in_s, 96)
                                pe.wait_ge(evac_s, j + 1)
                                if j >= 2:
                                    pe.wait_ge(rope_s, j - 1)
                                for hh in range(2):
                                    mm = pe.matmul(psum[:, 4 + 2 * (j % 2) + hh, 0:HW], rot[:], qk[j % 2][:, hh * HW:(hh + 1) * HW],
                                                   start=True, stop=True)
                                mm.then_inc(rot_s, 1)
                            if n == G0 + 2:
                                pe.wait_ge(sc_s, 6)
                                pe.wait_ge(rope_s, QK)
                                for ci, (c0, L) in enumerate(SCAN):
                                    for a, src in enumerate((dt, edt, acs)):
                                        mm = pe.transpose(psum[0:L, 7, 96 * ci + 32 * a:96 * ci + 32 * a + 32],
                                                          src[:, c0:c0 + L], ident[0:32, 0:32])
                                mm.then_inc(tr_s, 1)

            att = ExitStack()
            loop_st.enter_context(att)
            kw = sb(att, "kw", [P, KV, KEYS])
            vw0 = sb(att, "vw0", [P, 256])
            vw1 = sb(att, "vw1", [CH, 256])
            mask_k = sb(att, "mask_k", [P, KEYS])
            sink = sb(att, "sink", [P, 2 * KV])
            sc = sb(att, "sc", [P, 2 * KV, KEYS])
            mx = sb(att, "mx", [P, 2 * KV])
            nmx = sb(att, "nmx", [P, 2 * KV])
            sm = sb(att, "sm", [P, 2 * KV])
            es = sb(att, "es", [P, 2 * KV])
            rden = sb(att, "rden", [P, 2 * KV])
            pt0 = sb(att, "pt0", [P, 2, P])
            pt1 = sb(att, "pt1", [CH, 2, P])
            oc = sb(att, "oc", [P, KB, CH])

            class Attention:

                def __init__(self, stack, tag, rows, masked):
                    self.n, self.masked = rows, masked
                    self.q = sb(stack, f"{tag}_q", [P, KB, rows])
                    self.all = sems(stack, " ".join(f"{tag}_{x}" for x in (
                        "keys_in scores scores_read maxima exps normed turned turned_read values out_read stored order").split()))
                    (self.in_s, self.s_s, self.se_s, self.nm_s, self.ex_s, self.pn_s, self.pt_s, self.pe_s, self.pv_s,
                     self.oc_s, self.out_s, self.dv_s) = self.all

                def load(self, sp, q, k, v0, v1, mask):
                    n = self.n
                    sp.dma_start(self.q[:], q).then_inc(self.in_s, 16)
                    sp.dma_start(kw[0:64, :, 0:WIN + n], k).then_inc(self.in_s, 16)
                    sp.dma_start(kw[64:128, :, 0:WIN + n], k).then_inc(self.in_s, 16)
                    sp.dma_start(vw0[:], v0).then_inc(self.in_s, 16)
                    sp.dma_start(vw1[0:n, :], v1).then_inc(self.in_s, 16)
                    sp.dma_start(mask_k[:], mask).then_inc(self.in_s, 16)
                    sp.dma_start(sink[:], i["sinks"] if n == CH else i["sinks_s"]).then_inc(self.in_s, 16)

                LOADS = 7 * 16

                def scores(self, pe, kv):
                    n, m = self.n, 2 * self.n
                    if kv == 0:
                        pe.wait_ge(self.in_s, self.LOADS)
                    if kv >= 2:
                        pe.wait_ge(self.se_s, kv - 1)
                    for par in range(2):
                        rows = slice(64 * par, 64 * par + 64)
                        mm = pe.matmul(psum[0:m, 4 + 2 * (kv % 2) + par, 0:WIN + n], self.q[rows, 2 * kv:2 * kv + 2, :].rearrange("p a b -> p (a b)"),
                                       kw[rows, kv, 0:WIN + n], start=True, stop=True)
                    mm.then_inc(self.s_s, 1)

                def evac_scores(self, dve, kv):
                    n, m = self.n, 2 * self.n
                    dve.wait_ge(self.s_s, kv + 1)
                    dst = sc[0:m, 2 * kv:2 * kv + 2, 0:WIN + n]
                    src = psum[0:m, 4 + 2 * (kv % 2):6 + 2 * (kv % 2), 0:WIN + n]
                    if self.masked:
                        dve.scalar_tensor_tensor(out=dst, in0=src, scalar=HD ** -0.5,
                                                 in1=mask_k[0:m, 0:WIN + n].unsqueeze(1).to_broadcast((m, 2, WIN + n)),
                                                 op0=ALU.mult, op1=ALU.add).then_inc(self.se_s, 1)
                    else:
                        dve.tensor_scalar(dst, src, HD ** -0.5, None, ALU.mult).then_inc(self.se_s, 1)

                def maxima(self, dve):
                    m, w_ = 2 * self.n, WIN + self.n
                    dve.wait_ge(self.se_s, KV)
                    dve.tensor_reduce(mx[0:m], sc[0:m, :, 0:w_], AX.X, ALU.max).then_inc(self.dv_s, 1)
                    dve.wait_ge(self.dv_s, 1)
                    dve.tensor_tensor(mx[0:m], mx[0:m], sink[0:m], ALU.max).then_inc(self.dv_s, 1)
                    dve.wait_ge(self.dv_s, 2)
                    dve.tensor_scalar(nmx[0:m], mx[0:m], -1.0, None, ALU.mult).then_inc(self.nm_s, 1)
                    dve.tensor_tensor(es[0:m], sink[0:m], mx[0:m], ALU.subtract).then_inc(self.nm_s, 1)

                def exps(self, act):
                    m, w_ = 2 * self.n, WIN + self.n
                    act.wait_ge(self.nm_s, 2)
                    for u in range(2 * KV):
                        act.activation(sc[0:m, u, 0:w_], sc[0:m, u, 0:w_], ACT.Exp, bias=nmx[0:m, u:u + 1],
                                       accum_out=sm[0:m, u:u + 1])
                    act.activation(es[0:m], es[0:m], ACT.Exp).then_inc(self.ex_s, 1)

                def normalise(self, dve):
                    m, w_ = 2 * self.n, WIN + self.n
                    dve.wait_ge(self.ex_s, 1)
                    dve.tensor_tensor(sm[0:m], sm[0:m], es[0:m], ALU.add).then_inc(self.dv_s, 1)
                    dve.wait_ge(self.dv_s, 3)
                    dve.reciprocal(rden[0:m], sm[0:m]).then_inc(self.dv_s, 1)
                    dve.wait_ge(self.dv_s, 4)
                    for u in range(2 * KV):
                        dve.tensor_scalar(sc[0:m, u, 0:w_], sc[0:m, u, 0:w_], rden[0:m, u:u + 1], None,
                                          ALU.mult).then_inc(self.pn_s, 1)

                def turn(self, pe, kv):
                    n, m = self.n, 2 * self.n
                    pe.wait_ge(self.pn_s, 2 * kv + 2)
                    if kv >= 1:
                        pe.wait_ge(self.pe_s, kv)
                    for par in range(2):
                        pe.transpose(psum[:, 6, par * P:par * P + m], sc[0:m, 2 * kv + par, 0:WIN], ident[0:m, 0:m])
                        mm = pe.transpose(psum[0:n, 6, 256 + par * P:256 + par * P + m], sc[0:m, 2 * kv + par, WIN:WIN + n],
                                          ident[0:m, 0:m])
                    mm.then_inc(self.pt_s, 1)

                def evac_turned(self, act, kv):
                    n, m = self.n, 2 * self.n
                    act.wait_ge(self.pt_s, kv + 1)
                    if kv >= 1:
                        act.wait_ge(self.pv_s, kv)
                    act.activation(pt0[:, :, 0:m], psum[:, 6, 0:256].rearrange("p (a b) -> p a b", a=2)[:, :, 0:m], ACT.Copy)
                    act.activation(pt1[0:n, :, 0:m], psum[0:n, 6, 256:512].rearrange("p (a b) -> p a b", a=2)[:, :, 0:m],
                                   ACT.Copy).then_inc(self.pe_s, 1)

                def values(self, pe, kv):
                    n, m = self.n, 2 * self.n
                    pe.wait_ge(self.pe_s, kv + 1)
                    for par in range(2):
                        out = psum[64 * par:64 * par + 64, 7, kv * m:kv * m + m]
                        pe.matmul(out, vw0[:, 64 * kv:64 * kv + 64], pt0[:, par, 0:m], start=True, stop=False)
                        mm = pe.matmul(out, vw1[0:n, 64 * kv:64 * kv + 64], pt1[0:n, par, 0:m], start=False, stop=True)
                    mm.then_inc(self.pv_s, 1)

                def evac_out(self, act):
                    n = self.n
                    act.wait_ge(self.pv_s, KV)
                    act.activation(oc[:, :, 0:n], psum[:, 7, 0:8 * n].rearrange("p (a b) -> p a b", a=8), ACT.Copy).then_inc(self.oc_s, 1)

                def store(self, sp, dst):
                    sp.wait_ge(self.oc_s, 1)
                    sp.dma_start(dst, oc[:, :, 0:self.n]).then_inc(self.out_s, 16)

            with ExitStack() as st:
                gp = sb(st, "gp", [P, GP_N])
                tok = sb(st, "tok", [P, 5, 3, HPG])
                cv = sb(st, "cv", [P, GT, TW])
                th = [sb(st, f"th{n}", [P, TW]) for n in range(2)]
                acs_b = sb(st, "acs_b", [P, HPG, TW])
                e_b = sb(st, "e_b", [P, HPG, TW])
                c_s_ = sb(st, "c_dec", [P, HPG, TW])
                xdt = [sb(st, f"xdt{n}", [P, HPG, HD]) for n in range(2)]
                xt = [sb(st, f"xt{n}", [P, HPG, HD]) for n in range(2)]
                bt = [sb(st, f"bt{n}", [P, NS]) for n in range(2)]
                cbm = [sb(st, f"cbm{n}", [P, P]) for n in range(2)]
                dec = [sb(st, f"dec{n}", [P, HPG, P]) for n in range(2)]
                y = sb(st, "y", [P, 2, TW])
                h_p = sb(st, "h_p", [P, HPG, HD])
                h_s0 = sb(st, "h_s0", [P, HPG, HD])
                mod_row = sb(st, "mod_row_g", [2, ADA_W])
                names = ("g_in g_par g_conv g_th g_silu g_eb g_cdec g_tr g_cb g_xd g_bt g_w g_dif g_dece g_y g_ds g_ye g_h"
                         " g_tile g_evac g_yout g_out g_acs g_dve g_h0 g_cbe g_conv_out g_ctx"
                         " g_ada_used g_ada_in g_row g_row_out")
                handles = sems(st, names)
                (h_in, par_s, conv_s, th_s, silu_s, eb_s, cdec_s, tr_s, cb_s, xd_s, bt_s, w_s, dif_s, dece_s, y_s, ds_s,
                 ye_s, hst_s, tile_s, evac_s, yout_s, gout_s, acsb_s, dve_s, h0_s, cbe_s, cout_s, ctx_s,
                 ada_used, ada_in, row_s, row_out) = handles
                w = Stream(st, "g", [None] * GT, NCH, True, [None] * RAW_SLOTS)
                assert GT % RAW_SLOTS == 0 and GT % HL_SLOTS == 0
                at = Attention(st, "g", CH, True)
                nums = sorted(s.num for s in handles + w.all + at.all)
                assert nums == list(range(nums[0], nums[-1] + 1))
                sem_range = range(nums[0], nums[-1] + 1)
                NC5 = len(SCAN)

                def group(g):
                    w.src = [group_chunk(GT + n + g * GT) for n in range(GT + RAW_SLOTS)]
                    w.block = 0
                    with nc.Block(no_gpsimd_drain=True) as block:
                        @block.sync
                        def _(sp):
                            at.load(sp, scratch["q"][bass.ds(g, 1)].rearrange("c p t k -> p (c t) k"),
                                    scratch["k"][:, :, bass.ds(g * CH, KEYS)],
                                    scratch["v"][bass.ds(g * CH, WIN), :],
                                    scratch["v"][bass.ds(g * CH + WIN, CH), :],
                                    i["mask_k"][:, bass.ds(g * CH, KEYS)].to_broadcast((P, KEYS)))
                            for n in range(RAW_SLOTS, RAW_SLOTS + HL_SLOTS):
                                w.load(sp, n)
                            sp.wait_ge(ctx_s, 1)
                            sp.dma_start(acs_b[:], scratch["acs"][bass.ds(g * HPG, HPG), :].unsqueeze(0)
                                         .to_broadcast((P, HPG, TW))).then_inc(acsb_s, 16)
                            sp.dma_start(h_s0[:].rearrange("p a b -> p (a b)"), i["state"][bass.ds(g * P, P), :]).then_inc(h0_s, 16)
                            sp.dma_start(o["conv_p"][bass.ds(g * P, P), :], raw_last(T)).then_inc(cout_s, 16)
                            sp.dma_start(o["conv_s"][bass.ds(g * P, P), :], raw_last(TW)).then_inc(cout_s, 16)
                            w.load(sp, RAW_SLOTS + HL_SLOTS)
                            sp.wait_ge(ada_used, 1)
                            sp.dma_start(ada[:], i["w_ada"][bass.ds(g + 1, 1)].rearrange("a p k c -> p (a k) c")).then_inc(ada_in, 16)
                            sp.wait_ge(row_s, 1)
                            sp.dma_start(scratch["mod"][bass.ds(2 * g, 2), :], mod_row[:]).then_inc(row_out, 16)
                            at.store(sp, scratch["att"][:, :, bass.ds(g * CH, CH)])
                            for n in range(GT, GT + RAW_SLOTS):
                                w.load(sp, n)
                            sp.wait_ge(hst_s, 4)
                            sp.dma_start(o["ssm_p"][bass.ds(g * P, P), :], h_p[:].rearrange("p a b -> p (a b)")).then_inc(gout_s, 16)
                            sp.wait_ge(hst_s, 5)
                            sp.dma_start(o["ssm_s"][bass.ds(g * P, P), :], h_s0[:].rearrange("p a b -> p (a b)")).then_inc(gout_s, 16)
                            sp.wait_ge(yout_s, 1)
                            sp.dma_start(scratch["y"][bass.ds(g * P, P), :], y[:].rearrange("p a b -> p (a b)")).then_inc(gout_s, 16)
                            w.all_landed(sp)
                            sp.wait_ge(ada_in, 16)
                            sp.wait_ge(row_out, 16)
                            sp.wait_ge(gout_s, 48)
                            sp.wait_ge(cout_s, 32)
                            sp.wait_ge(at.out_s, 16)

                        @block.gpsimd
                        def _(pool):
                            pool.tensor_copy(gp[:], gp_all[:, bass.ds(g, 1), :].rearrange("p a b -> p (a b)")).then_inc(par_s, 1)
                            pool.tensor_copy(tok[:].rearrange("p a b c -> p (a b c)"),
                                             tok_all[:, bass.ds(g, 1)].rearrange("p g a b c -> p (g a b c)")).then_inc(par_s, 1)
                            w.split_lo(pool, 2)
                            pool.wait_ge(eb_s, 1)
                            pool.wait_ge(silu_s, 2)
                            for r in range(HPG):
                                pool.tensor_tensor(c_s_[:, r, :], e_b[:, r, :], cv[:, 1, :], ALU.mult).then_inc(cdec_s, 1)
                            for n in range(3, GT + HL_SLOTS):
                                w.split_lo(pool, n)
                            w.all_split(pool)

                        @block.scalar
                        def _(act):
                            def tanh(t):
                                act.wait_ge(conv_s, min(t, 3) + 1)
                                if t >= 2:
                                    act.wait_ge(silu_s, t - 1)
                                if t < 4:
                                    act.activation(th[t % 2][:], cv[:, t, :], ACT.Tanh).then_inc(th_s, 1)
                                else:
                                    act.activation(th[t % 2][:], raw[:, t, LEAD:], ACT.Tanh, scale=0.5).then_inc(th_s, 1)

                            def evac(t):
                                act.wait_ge(w.used, t + 1)
                                if t < 4:
                                    act.wait_ge(conv_s, t + 1)
                                    act.wait_ge(cout_s, 32)
                                else:
                                    act.wait_ge(silu_s, t + 1)
                                act.activation(halves(raw[:, t, LEAD:]), slot(t % 2), ACT.Copy).then_inc(evac_s, 1)

                            def scan_exp(c):
                                L = SCAN[c][1]
                                act.wait_ge(dif_s, c + 1)
                                act.activation(dec[c % 2][0:L, :, 0:L], dec[c % 2][0:L, :, 0:L], ACT.Exp).then_inc(dece_s, 1)

                            tanh(0)
                            act.wait_ge(ada_used, 1)
                            act.activation(mod_row[:], psum[0:2, 2, :], ACT.Copy).then_inc(row_s, 1)
                            act.wait_ge(acsb_s, 16)
                            act.activation(e_b[:], acs_b[:], ACT.Exp).then_inc(eb_s, 1)
                            tanh(1)
                            w.split_hi(act, 2)
                            evac(0)
                            at.exps(act)
                            tanh(2)
                            w.split_hi(act, 3)
                            evac(1)
                            for kv in range(KV):
                                at.evac_turned(act, kv)
                            tanh(3)
                            at.evac_out(act)
                            w.split_hi(act, 4)
                            evac(2)
                            tanh(4)
                            scan_exp(0)
                            tanh(5)
                            scan_exp(1)
                            w.split_hi(act, 5)
                            evac(3)
                            for c in range(2, NC5):
                                scan_exp(c)
                                if c == 3:
                                    evac(4)
                                    w.split_hi(act, GT)
                            evac(5)
                            w.split_hi(act, GT + 1)

                        @block.vector
                        def _(dve):
                            link = chain(dve_s)

                            def conv(t):
                                link(dve, dve.tensor_scalar(cv[:, t, :], raw[:, t, 1:1 + TW], gp[:, GP_W + 4 * t:GP_W + 4 * t + 1],
                                                            gp[:, GP_B + t:GP_B + t + 1], ALU.mult, ALU.add))
                                for k in range(1, TAPS):
                                    ins = dve.scalar_tensor_tensor(
                                        out=cv[:, t, :], in0=raw[:, t, 1 + k:1 + k + TW],
                                        scalar=gp[:, GP_W + 4 * t + k:GP_W + 4 * t + k + 1], in1=cv[:, t, :],
                                        op0=ALU.mult, op1=ALU.add)
                                    if k < TAPS - 1:
                                        link(dve, ins)
                                ins.then_inc(conv_s, 1)

                            def silu(t):
                                dve.wait_ge(th_s, t + 1)
                                src = cv[:, t, :] if t < 4 else raw[:, t, LEAD:]
                                dve.scalar_tensor_tensor(out=cv[:, t, :], in0=th[t % 2][:], scalar=1.0, in1=src,
                                                         op0=ALU.add, op1=ALU.mult).then_inc(silu_s, 1)

                            def weights(c):
                                c0, L = SCAN[c]
                                b = c % 2
                                dve.wait_ge(tr_s, c + 1)
                                if c >= 2:
                                    dve.wait_ge(ds_s, c - 1)
                                src = psum[0:L, 4, 0:256].rearrange("p (r d) -> p r d", r=HPG)
                                dve.tensor_tensor(xdt[b][0:L], src, bcast_mid(tok[0:L, c, 0, :], HD), ALU.mult).then_inc(xd_s, 1)
                                dve.tensor_tensor(xt[b][0:L], src, bcast_mid(tok[0:L, c, 1, :], HD), ALU.mult).then_inc(xd_s, 1)
                                dve.tensor_copy(bt[b][0:L, :], psum[0:L, 4, 256:384]).then_inc(bt_s, 1)
                                for r in range(HPG):
                                    ins = dve.tensor_scalar(dec[b][0:L, r, 0:L], acs_b[0:L, r, c0:c0 + L],
                                                            tok[0:L, c, 2, r:r + 1], 0.0, ALU.subtract, ALU.min)
                                ins.then_inc(dif_s, 1)
                                dve.wait_ge(cb_s, c + 1)
                                dve.tensor_tensor(cbm[b][0:L, 0:L], psum[0:L, 5, 0:L], mask_u[0:L, 0:L],
                                                  ALU.mult).then_inc(cbe_s, 1)
                                dve.wait_ge(cbe_s, c + 1)
                                dve.wait_ge(dece_s, c + 1)
                                dve.tensor_tensor(dec[b][0:L, :, 0:L], dec[b][0:L, :, 0:L],
                                                  cbm[b][0:L, 0:L].unsqueeze(1).to_broadcast((L, HPG, L)), ALU.mult).then_inc(w_s, 1)

                            def outputs(c):
                                c0, L = SCAN[c]
                                dve.wait_ge(y_s, c + 1)
                                for t in range(2):
                                    ins = dve.scalar_tensor_tensor(out=y[:, t, c0:c0 + L], in0=cv[:, 2 + t, c0:c0 + L],
                                                             scalar=gp[:, GP_D + t:GP_D + t + 1],
                                                             in1=psum[:, 6, t * P:t * P + L], op0=ALU.mult, op1=ALU.add)
                                ins.then_inc(ye_s, 1)
                                dve.wait_ge(ds_s, c + 1)
                                d_s = psum[:, 7, 0:256].rearrange("p (r d) -> p r d", r=HPG)
                                if c == 0:
                                    dve.tensor_copy(h_p[:], d_s).then_inc(hst_s, 1)
                                    return
                                h_ = h_p if c < 4 else h_s0
                                link(dve, dve.tensor_tensor(h_[:], h_[:], e_b[:, :, c0 + L - 1:c0 + L].to_broadcast((P, HPG, HD)), ALU.mult))
                                dve.tensor_tensor(h_[:], h_[:], d_s, ALU.add).then_inc(hst_s, 1)

                            dve.wait_ge(par_s, 2)
                            dve.tensor_copy(raw[:, 0:4, LEAD + S0 - 3:LEAD + S0],
                                            gp[:, GP_CTX:GP_CTX + 12].rearrange("p (a b) -> p a b", a=4)).then_inc(ctx_s, 1)
                            dve.wait_ge(ctx_s, 1)
                            conv(0)
                            at.evac_scores(dve, 0)
                            at.evac_scores(dve, 1)
                            conv(1)
                            silu(0)
                            at.evac_scores(dve, 2)
                            at.evac_scores(dve, 3)
                            silu(1)
                            at.maxima(dve)
                            conv(2)
                            at.normalise(dve)
                            conv(3)
                            silu(2)
                            silu(3)
                            dve.wait_ge(eb_s, 1)
                            weights(0)
                            silu(4)
                            weights(1)
                            outputs(0)
                            silu(5)
                            dve.memset(y[:, :, T:S0], 0.0)
                            for c in range(1, NC5):
                                if c + 1 < NC5:
                                    weights(c + 1)
                                if c == 4:
                                    dve.wait_ge(h0_s, 16)
                                outputs(c)
                            dve.wait_ge(ye_s, NC5)
                            dve.wait_ge(silu_s, 6)
                            dve.scalar_tensor_tensor(out=y[:], in0=y[:], scalar=0.5, in1=cv[:, 4:6, :], op0=ALU.mult,
                                                     op1=ALU.mult).then_inc(yout_s, 1)

                        @block.tensor
                        def _(pe):
                            steps = iter(range(GT * KB))

                            def fill(n):
                                for _ in range(n):
                                    u = next(steps, None)
                                    if u is None:
                                        return
                                    t, k = divmod(u, KB)
                                    if k == 0 and t == 1:
                                        pe.wait_ge(row_s, 1)
                                    if k == 0 and t >= 2:
                                        pe.wait_ge(evac_s, t - 1)
                                    w.multiply(pe, slot(t % 2), hp_hi[:, k, :], hp_lo[:, k, :], k == 0, k == KB - 1)

                            def turn_scores(c):
                                c0, L = SCAN[c]
                                if c == 0:
                                    pe.wait_ge(silu_s, 4)
                                    pe.wait_ge(at.oc_s, 1)
                                else:
                                    pe.wait_ge(xd_s, 2 * c)
                                    pe.wait_ge(bt_s, c)
                                    pe.wait_ge(cbe_s, c)
                                for a, t in enumerate((2, 3, 0)):
                                    mm = pe.transpose(psum[0:L, 4, a * P:a * P + P], cv[:, t, c0:c0 + L], ident[:])
                                mm.then_inc(tr_s, 1)
                                pe.matmul(psum[0:L, 5, 0:L], cv[:, 0, c0:c0 + L], cv[:, 1, c0:c0 + L], start=True,
                                          stop=True).then_inc(cb_s, 1)

                            def scan(c):
                                c0, L = SCAN[c]
                                b = c % 2
                                pe.wait_ge(w_s, c + 1)
                                if c >= 1:
                                    pe.wait_ge(ye_s, c)
                                    pe.wait_ge(hst_s, c)
                                if c == 4:
                                    pe.wait_ge(h0_s, 16)
                                pe.wait_ge(cdec_s, HPG)
                                h_ = h_p if c < 4 else h_s0
                                for r in range(HPG):
                                    half, t = r % 2, r // 2
                                    out = psum[64 * half:64 * half + 64, 6, t * P:t * P + L]
                                    mm = pe.matmul(out, xdt[b][0:L, r, :], dec[b][0:L, r, 0:L], start=True, stop=c == 0)
                                    if c > 0:
                                        mm = pe.matmul(out, h_[:, r, :], c_s_[:, r, c0:c0 + L], start=False, stop=True)
                                mm.then_inc(y_s, 1)
                                pe.wait_ge(bt_s, c + 1)
                                pe.matmul(psum[:, 7, 0:256], bt[b][0:L, :], xt[b][0:L].rearrange("p r d -> p (r d)"),
                                          start=True, stop=True).then_inc(ds_s, 1)

                            for k in range(KB):
                                mm = pe.matmul(psum[0:2, 2, :], c_silu[:, k, :], ada[:, k, :], start=k == 0, stop=k == KB - 1)
                            mm.then_inc(ada_used, 1)
                            at.scores(pe, 0)
                            at.scores(pe, 1)
                            fill(6)
                            at.scores(pe, 2)
                            at.scores(pe, 3)
                            fill(14)
                            for kv in range(KV):
                                at.turn(pe, kv)
                                fill(1)
                                at.values(pe, kv)
                            fill(4)
                            turn_scores(0)
                            fill(3)
                            for c in range(NC5):
                                if c + 1 < NC5:
                                    turn_scores(c + 1)
                                fill(2)
                                scan(c)
                                fill(1)
                            fill(GT * KB)
                    nc.all_engine_barrier(sems_to_clear=sem_range)

                def raw_last(end):
                    return raw[:, 0:4, LEAD + end - 3:LEAD + end]

                nc.all_engine_barrier(sems_to_clear=range(first_sem, sem_range.stop))
                with nc.Block(no_gpsimd_drain=True) as block:
                    @block.vector
                    def _(dve):
                        dve.tensor_scalar(gp_all[:, :, 0:GP_CTX], gp_all[:, :, 0:GP_CTX], 0.5, None, ALU.mult).then_inc(dve_s, 1)
                        dve.wait_ge(dve_s, 1)
                nc.all_engine_barrier(sems_to_clear=sem_range)
                with nc.Fori(0, GROUPS) as g:
                    group(g)

            with ExitStack() as st:
                at = Attention(st, "s", S, False)
                gate_out, = sems(st, "s_gate_out")
                with nc.Block(no_gpsimd_drain=True) as block:
                    @block.sync
                    def _(sp):
                        at.load(sp, scratch["qs"], scratch["ks"], scratch["vs"][0:WIN, :], scratch["vs"][WIN:WIN + S, :],
                                i["mask_k"][:, 0:KEYS].to_broadcast((P, KEYS)))
                        sp.dma_start(scratch["gate"], raw[:, :, LEAD:]).then_inc(gate_out, 16)
                        at.store(sp, scratch["att"][:, :, S0:TW])
                        sp.wait_ge(gate_out, 16)
                        sp.wait_ge(at.out_s, 16)

                    @block.vector
                    def _(dve):
                        for kv in range(KV):
                            at.evac_scores(dve, kv)
                        at.maxima(dve)
                        at.normalise(dve)

                    @block.scalar
                    def _(act):
                        at.exps(act)
                        for kv in range(KV):
                            at.evac_turned(act, kv)
                        at.evac_out(act)

                    @block.tensor
                    def _(pe):
                        for kv in range(KV):
                            at.scores(pe, kv)
                        for kv in range(KV):
                            at.turn(pe, kv)
                            at.values(pe, kv)

        with ExitStack() as st:
            wide_hi = sb(st, "wide_hi", [P, 16, TW], F32R)
            wide_lo = sb(st, "wide_lo", [P, 16, TW], F32R)
            mrg = sb(st, "mrg", [P, KB, TW])
            tmp = [sb(st, f"tmp{n}", [P, TW]) for n in range(3)]
            th = sb(st, "th", [P, TW])
            hq_st = ExitStack()
            hq_hi = sb(hq_st, "hq_hi", [P, KB, TW], F32R)
            hq_lo = sb(hq_st, "hq_lo", [P, KB, TW], F32R)

            def norm_terms(act, src, dst, sem, scale, bank_slot):
                act.activation(halves(dst[:]), slot(bank_slot), ACT.Sqrt, bias=eps_c, scale=scale).then_inc(sem, 1)

            with ExitStack() as ms:
                yl = [sb(ms, f"yl{n}", [P, 2, TW]) for n in range(2)]
                ys = sb(ms, "ys", [P, TW])
                rs = sb(ms, "rs", [P, TW])
                snorm = sb(ms, "snorm", [P, 16])
                mod_rows = sb(ms, "mod_rows", [8 * KB, P])
                first_att = [m + max(m - GT + 1, 0) for m in range(KB)]
                N1 = first_att[-1] + 1
                src = []
                for m in range(KB):
                    src += ([i["w_gate"][8 + m]] if m >= GT else []) + [i["w_att"][m]]
                for m in range(KB):
                    src += [i["w_gate"][m], i["w_ssm"][2 * m], i["w_ssm"][2 * m + 1]]
                w = Stream(ms, "m", src, NCH + GROUPS * GT, True, [i["w_out"][n] for n in range(RAW_SLOTS)])
                (in_att0, in_att1, in_att2, in_y0, in_y1, in_c, ahi_s, alo_s, sq_s, ss_s, root_s, rec_s, yn_s, yhi_s, ylo_s, th_s, m_s, dve_s,
                 in_g0, in_g1, in_mod, turn_s) = sems(
                    ms, "m_att0 m_att1 m_att2 m_y0 m_y1 m_c m_ahi m_alo m_sq m_ss m_root m_rec m_yn m_yhi m_ylo m_th m_m m_dve"
                        " m_g0 m_g1 m_mod m_turn")
                in_g = [in_g0, in_g1]
                in_att, in_y = [in_att0, in_att1, in_att2], [in_y0, in_y1]
                AT_IN = 3
                gl = [tmp[2], tmp[1]]
                with nc.Block(no_gpsimd_drain=True) as block:
                    @block.sync
                    def _(sp):
                        for t in range(AT_IN):
                            sp.dma_start(tmp[t][:], scratch["att"][:, t, :]).then_inc(in_att[t], 16)
                        for n in range(RAW_SLOTS, RAW_SLOTS + HL_SLOTS):
                            w.load(sp, n)
                        sp.dma_start(mod_rows[:], scratch["mod"].rearrange("r (b p) -> (r b) p", p=P)).then_inc(in_mod, 16)
                        for t in range(AT_IN, KB):
                            sp.wait_ge(alo_s, t - AT_IN + 1)
                            sp.dma_start(tmp[t % AT_IN][:], scratch["att"][:, t, :]).then_inc(in_att[t % AT_IN], 16)
                        sp.dma_start(snorm[:], i["ssm_norm"]).then_inc(in_c, 16)
                        for m, last in ((0, KB - 3), (1, KB - 1)):
                            sp.wait_ge(alo_s, last + 1)
                            sp.dma_start(gl[m][:], scratch["gate"][:, m, :]).then_inc(in_g[m], 16)
                        for g in range(2):
                            sp.dma_start(yl[g][:].rearrange("p a b -> p (a b)"), scratch["y"][g * P:(g + 1) * P, :]).then_inc(in_y[g % 2], 16)
                        n = RAW_SLOTS + HL_SLOTS
                        for g in range(2, GROUPS):
                            while n <= first_att[g] + 1:
                                w.load(sp, n)
                                n += 1
                            if g < GT:
                                sp.wait_ge(th_s, g - 1)
                                sp.dma_start(gl[g % 2][:], scratch["gate"][:, g, :]).then_inc(in_g[g % 2], 16)
                            sp.wait_ge(ylo_s, 2 * (g - 1))
                            sp.dma_start(yl[g % 2][:].rearrange("p a b -> p (a b)"), scratch["y"][g * P:(g + 1) * P, :]).then_inc(in_y[g % 2], 16)
                        while n < w.own + RAW_SLOTS:
                            w.load(sp, n)
                            n += 1
                        w.all_landed(sp)

                    @block.gpsimd
                    def _(pool):
                        for t in range(KB):
                            pool.wait_ge(ahi_s, t + 1)
                            pool.tensor_tensor(hq_lo[:, t, :], tmp[t % AT_IN][:], hq_hi[:, t, :].bitcast(F32), ALU.subtract).then_inc(alo_s, 1)
                        for n in range(w.own + HL_SLOTS):
                            w.split_lo(pool, n)
                        w.all_split(pool)

                    @block.scalar
                    def _(act):
                        def gate_tanh(n, k, src):
                            if n is None:
                                act.wait_ge(in_g[k % 2], 16 * (k // 2 + 1))
                            else:
                                act.wait_ge(w.used, n + 1)
                            if k >= 1:
                                act.wait_ge(m_s, k)
                            act.activation(halves(th[:]), src, ACT.Tanh, scale=0.5).then_inc(th_s, 1)

                        def y_norm(g):
                            act.wait_ge(in_y[g % 2], 16 * (g // 2 + 1))
                            for t in range(2):
                                if t == 1 or g > 0:
                                    act.wait_ge(ss_s, 2 * g + t)
                                act.activation(ys[:], yl[g % 2][:, t, :], ACT.Square).then_inc(sq_s, 1)
                            act.wait_ge(ss_s, 2 * g + 2)
                            if g >= 1:
                                act.wait_ge(yn_s, 2 * g)
                            norm_terms(act, None, rs, root_s, 1.0 / 256, 3)
                            for t in range(2):
                                act.wait_ge(yn_s, 2 * g + t + 1)
                                act.activation(wide_hi[:, 2 * g + t, :], yl[g % 2][:, t, :], ACT.Copy).then_inc(yhi_s, 1)

                        for t in range(KB):
                            act.wait_ge(in_att[t % AT_IN], 16 * (t // AT_IN + 1))
                            act.activation(hq_hi[:, t, :], tmp[t % AT_IN][:], ACT.Copy).then_inc(ahi_s, 1)
                        for m in range(KB):
                            n = first_att[m]
                            if m >= GT:
                                w.split_hi(act, n + 1)
                                gate_tanh(n - 1, m, slot(0))
                            else:
                                gate_tanh(None, m, halves(gl[m % 2][:]))
                            w.split_hi(act, n + 2)
                            y_norm(m)
                        for n in range(24):
                            w.split_hi(act, N1 + n + 2)
                            if n % 3 == 0:
                                gate_tanh(N1 + n, 8 + n // 3, slot(2))

                    @block.vector
                    def _(dve):
                        link = chain(dve_s)
                        dve.wait_ge(in_c, 16)
                        dve.wait_ge(turn_s, 1)
                        link(dve, dve.tensor_tensor(
                            mod[:, 2 * KB:, :].rearrange("p (n b) s -> p n b s", n=ADA_LATE),
                            psum[:, 4, 0:8 * KB].rearrange("p (n s b) -> p n b s", n=ADA_LATE, s=2),
                            bcast_mid(b_ada[:, 2 * KB:], 2).rearrange("p (n b) s -> p n b s", n=ADA_LATE), ALU.add))
                        for s in range(2):
                            link(dve, dve.tensor_tensor(gate[:, s], mod[:, 24 * s + 16:24 * s + 24, :],
                                                        bcast_mid(vecs[:, 2 * s + 1, :], 2), ALU.mult))
                        link(dve, dve.scalar_tensor_tensor(out=gain[:, 1], in0=mod[:, 32:40, :], scalar=1.0,
                                                           in1=bcast_mid(vecs[:, 2, :], 2), op0=ALU.add, op1=ALU.mult))
                        for m in range(KB):
                            dve.wait_ge(th_s, m + 1)
                            dve.wait_ge(w.used, first_att[m] + 1)
                            dve.scalar_tensor_tensor(out=halves(mrg[:, m, :]), in0=halves(th[:]), scalar=1.0, in1=slot(1),
                                                     op0=ALU.add, op1=ALU.mult).then_inc(m_s, 1)
                            dve.wait_ge(root_s, m + 1)
                            link(dve, dve.reciprocal(rs[:], rs[:]))
                            for t in range(2):
                                dve.scalar_tensor_tensor(out=yl[m % 2][:, t, :], in0=yl[m % 2][:, t, :],
                                                         scalar=snorm[:, 2 * m + t:2 * m + t + 1], in1=rs[:], op0=ALU.mult,
                                                         op1=ALU.mult).then_inc(yn_s, 1)
                            for t in range(2):
                                dve.wait_ge(yhi_s, 2 * m + t + 1)
                                dve.tensor_tensor(wide_lo[:, 2 * m + t, :], yl[m % 2][:, t, :],
                                                  wide_hi[:, 2 * m + t, :].bitcast(F32), ALU.subtract).then_inc(ylo_s, 1)
                        for m in range(KB):
                            dve.wait_ge(th_s, 8 + m + 1)
                            dve.wait_ge(w.used, N1 + 3 * m + 3)
                            link(dve, dve.scalar_tensor_tensor(out=halves(tmp[0][:]), in0=halves(th[:]), scalar=1.0, in1=slot(m % 2),
                                                               op0=ALU.add, op1=ALU.mult))
                            dve.tensor_tensor(mrg[:, m, :], mrg[:, m, :], tmp[0][:], ALU.add).then_inc(m_s, 1)
                            dve.wait_ge(m_s, 8 + m + 1)

                    @block.tensor
                    def _(pe):
                        def tile(s, hi, lo, k0=0, nk=KB):
                            for k in range(k0, k0 + KB):
                                w.multiply(pe, slot(s), hi[:, k, :], lo[:, k, :], k == 0, k == nk - 1)

                        pe.wait_ge(in_mod, 16)
                        pe.transpose(psum[:, 4, 0:8 * KB], mod_rows[:], ident[0:8 * KB, 0:8 * KB]).then_inc(turn_s, 1)
                        for m in range(KB):
                            if m >= GT:
                                pe.wait_ge(th_s, m)
                                tile(0, hp_hi, hp_lo)
                            if m == 0:
                                pe.wait_ge(alo_s, KB)
                            else:
                                pe.wait_ge(m_s, m)
                            tile(1, hq_hi, hq_lo)
                            for t in range(2):
                                if m >= 1 and t == 0:
                                    pe.wait_ge(root_s, m)
                                pe.wait_ge(sq_s, 2 * m + t + 1)
                                for hh in range(2):
                                    mm = pe.matmul(psum[:, 6 + hh, 0:HW], ones[:], ys[:, hh * HW:(hh + 1) * HW], start=t == 0, stop=t == 1)
                                mm.then_inc(ss_s, 1)
                        for m in range(KB):
                            if m >= 1:
                                pe.wait_ge(th_s, 8 + m)
                            if m == 0:
                                pe.wait_ge(turn_s, 1)
                            tile(2, hp_hi, hp_lo)
                            if m == 0:
                                pe.wait_ge(ylo_s, 16)
                                pe.wait_ge(m_s, KB)
                            elif m >= 2:
                                pe.wait_ge(m_s, KB + m - 1)
                            tile(m % 2, wide_hi, wide_lo, 0, 16)
                            tile(m % 2, wide_hi, wide_lo, 8, 16)

            with ExitStack() as ms:
                sq = [sb(ms, f"osq{n}", [P, TW]) for n in range(2)]
                rs = [sb(ms, f"ors{n}", [P, TW]) for n in range(2)]
                xl = [*(sb(ms, f"xl{n}", [P, TW]) for n in range(2)), th]
                w = Stream(ms, "o", [i["w_out"][m] for m in range(KB)], w.base + w.own, True,
                           [i["w_ffn_in"][n] for n in range(RAW_SLOTS)])
                (hi_s, lo_s, ev_s, sq_s, ss_s, root_s, x_in0, x_in1, x_in2, x_s, h_s, hhi_s, dve_s, hlo_s) = sems(
                    ms, "o_hi_s o_lo_s o_ev o_sq o_ss o_root o_xin0 o_xin1 o_xin2 o_x o_h o_hhi o_dve o_hlo")
                x_in = [x_in0, x_in1, x_in2]
                with nc.Block(no_gpsimd_drain=True) as block:
                    @block.sync
                    def _(sp):
                        for n in range(RAW_SLOTS, RAW_SLOTS + HL_SLOTS):
                            w.load(sp, n)
                        for t in range(3):
                            sp.dma_start(xl[t][:], i["x"][:, t, :]).then_inc(x_in[t % 3], 16)
                        for n in range(RAW_SLOTS + HL_SLOTS, KB + RAW_SLOTS):
                            w.load(sp, n)
                        for t in range(3, KB):
                            sp.wait_ge(x_s, t - 2)
                            sp.dma_start(xl[t % 3][:], i["x"][:, t, :]).then_inc(x_in[t % 3], 16)
                        w.all_landed(sp)

                    @block.gpsimd
                    def _(pool):
                        for n in range(KB + HL_SLOTS):
                            w.split_lo(pool, n)
                        for t in range(KB):
                            pool.wait_ge(hhi_s, t + 1)
                            pool.tensor_tensor(hq_lo[:, t, :], tmp[t % 3][:], hq_hi[:, t, :].bitcast(F32), ALU.subtract).then_inc(hlo_s, 1)
                        w.all_split(pool)
                        pool.wait_ge(hlo_s, KB)

                    @block.scalar
                    def _(act):
                        def square(t, count):
                            if count >= 2:
                                act.wait_ge(ss_s, count - 1)
                            act.activation(sq[count % 2][:], mrg[:, t, :], ACT.Square).then_inc(sq_s, 1)

                        for t in range(KB):
                            act.activation(hp_hi[:, t, :], mrg[:, t, :], ACT.Copy, scale=0.5).then_inc(hi_s, 1)
                        for n in range(KB):
                            w.split_hi(act, n + 2)
                            act.wait_ge(w.used, n + 1)
                            act.activation(halves(mrg[:, n, :]), slot(n % 2), ACT.Copy).then_inc(ev_s, 1)
                            act.wait_ge(ev_s, n + 1)
                            square(n, n)
                        act.wait_ge(ss_s, KB)
                        norm_terms(act, None, rs[0], root_s, 1.0 / D, 3)
                        for t in range(KB):
                            act.wait_ge(x_s, t + 1)
                            square(t, KB + t)
                        act.wait_ge(ss_s, 2 * KB)
                        norm_terms(act, None, rs[1], root_s, 1.0 / D, 2)
                        for t in range(KB):
                            act.wait_ge(h_s, t + 1)
                            act.activation(hq_hi[:, t, :], tmp[t % 3][:], ACT.Copy).then_inc(hhi_s, 1)

                    @block.vector
                    def _(dve):
                        link = chain(dve_s)
                        for t in range(KB):
                            dve.wait_ge(hi_s, t + 1)
                            dve.scalar_tensor_tensor(out=hp_lo[:, t, :], in0=mrg[:, t, :], scalar=0.5, in1=hp_hi[:, t, :].bitcast(F32),
                                                     op0=ALU.mult, op1=ALU.subtract).then_inc(lo_s, 1)
                        dve.wait_ge(root_s, 1)
                        link(dve, dve.reciprocal(rs[0][:], rs[0][:]))
                        for t in range(KB):
                            link(dve, dve.tensor_tensor(mrg[:, t, :], mrg[:, t, :], rs[0][:], ALU.mult))
                            dve.wait_ge(x_in[t % 3], 16 * (t // 3 + 1))
                            for c0, L, g in RANGES:
                                ins = dve.scalar_tensor_tensor(out=mrg[:, t, c0:c0 + L], in0=mrg[:, t, c0:c0 + L],
                                                               scalar=gate[:, 0, t, g:g + 1], in1=xl[t % 3][:, c0:c0 + L],
                                                               op0=ALU.mult, op1=ALU.add)
                            ins.then_inc(x_s, 1)
                        dve.wait_ge(root_s, 2)
                        link(dve, dve.reciprocal(rs[1][:], rs[1][:]))
                        for t in range(KB):
                            if t >= 3:
                                dve.wait_ge(hlo_s, t - 2)
                            link(dve, dve.tensor_tensor(tmp[t % 3][:], mrg[:, t, :], rs[1][:], ALU.mult))
                            for c0, L, g in RANGES:
                                ins = dve.tensor_scalar(tmp[t % 3][:, c0:c0 + L], tmp[t % 3][:, c0:c0 + L], gain[:, 1, t, g:g + 1],
                                                        mod[:, 24 + t, g:g + 1], ALU.mult, ALU.add)
                            ins.then_inc(h_s, 1)

                    @block.tensor
                    def _(pe):
                        def squares(t, count, s):
                            pe.wait_ge(sq_s, count + 1)
                            for hh in range(2):
                                mm = pe.matmul(psum[:, 2 * s + hh, 0:HW], ones[:], sq[count % 2][:, hh * HW:(hh + 1) * HW],
                                               start=t == 0, stop=t == KB - 1)
                            mm.then_inc(ss_s, 1)

                        for m in range(KB):
                            if m == 0:
                                pe.wait_ge(lo_s, KB)
                            if m >= 2:
                                pe.wait_ge(ev_s, m - 1)
                            for k in range(KB):
                                w.multiply(pe, slot(m % 2), hp_hi[:, k, :], hp_lo[:, k, :], k == 0, k == KB - 1)
                            if m >= 1:
                                squares(m - 1, m - 1, 3)
                        squares(KB - 1, KB - 1, 3)
                        for t in range(KB):
                            squares(t, KB + t, 2)

            with ExitStack() as ms:
                fpar = sb(ms, "fpar", [P, FT, 6])
                fr = [sb(ms, f"fr{n}", [P, LEAD + TW]) for n in range(2)]
                fst = sb(ms, "fst", [P, FT, 4])
                cvf = [tmp[1], tmp[2]]
                w = Stream(ms, "f", [i["w_ffn_in"][n] for n in range(2 * FT)], w.base + w.own, True,
                           [i["w_ffn_out"][n] for n in range(RAW_SLOTS)])
                (in_s, par_s, fe_s, ctx_s, fcv_s, fth_s, fsl_s, ff_s, fhi_s, flo_s, fst_s, dve_s, z_s, o_s) = sems(
                    ms, "f_in f_par f_e f_ctx f_cv f_th f_sl f_f f_fhi f_flo f_st f_dve f_z f_o")
                sl = [sb(ms, f"fs{n}", [P, TW]) for n in range(2)]

                def wide(f, part):
                    return ((hp_hi, hp_lo)[part][:, f, :] if f < KB else (wide_hi, wide_lo)[part][:, f - KB, :])

                with nc.Block(no_gpsimd_drain=True) as block:
                    @block.sync
                    def _(sp):
                        sp.dma_start(fpar[:], i["fpar"]).then_inc(in_s, 16)
                        for n in range(2 * FT + RAW_SLOTS):
                            w.load(sp, n)
                        w.all_landed(sp)
                        sp.wait_ge(fst_s, 2 * FT)
                        sp.dma_start(o["ffn"], fst[:]).then_inc(o_s, 16)
                        sp.wait_ge(o_s, 16)

                    @block.gpsimd
                    def _(pool):
                        for n in range(2):
                            pool.memset(fr[n][:, 0:LEAD], 0.0).then_inc(z_s, 1)
                        for n in range(2 * FT + HL_SLOTS):
                            w.split_lo(pool, n)
                            f, up = divmod(n, 2)
                            if up and f < FT:
                                pool.wait_ge(fe_s, f + 1)
                                pool.tensor_copy(fst[:, f, 0:2], fr[f % 2][:, LEAD + T - 2:LEAD + T]).then_inc(fst_s, 1)
                                pool.tensor_copy(fst[:, f, 2:4], fr[f % 2][:, LEAD + TW - 2:LEAD + TW]).then_inc(fst_s, 1)
                        w.all_split(pool)

                    @block.scalar
                    def _(act):
                        act.wait_ge(z_s, 2)

                        def round_hi(f):
                            act.wait_ge(ff_s, f + 1)
                            act.activation(wide(f, 0), sl[f % 2][:], ACT.Copy).then_inc(fhi_s, 1)

                        for n in range(2 * FT):
                            w.split_hi(act, n + 2)
                            f, up = divmod(n, 2)
                            if not up:
                                act.wait_ge(w.used, n + 1)
                                if f >= 2:
                                    act.wait_ge(fcv_s, f - 1)
                                    act.wait_ge(fst_s, 2 * (f - 1))
                                act.activation(halves(fr[f % 2][:, LEAD:]), slot(f % 2), ACT.Copy).then_inc(fe_s, 1)
                                if f >= 1:
                                    round_hi(f - 1)
                            else:
                                act.wait_ge(fcv_s, f + 1)
                                if f >= 1:
                                    act.wait_ge(fsl_s, f)
                                act.activation(th[:], cvf[f % 2][:], ACT.Tanh).then_inc(fth_s, 1)
                        round_hi(FT - 1)

                    @block.vector
                    def _(dve):
                        link = chain(dve_s)
                        dve.wait_ge(in_s, 16)
                        link(dve, dve.tensor_scalar(fpar[:, :, 0:4], fpar[:, :, 0:4], 0.5, None, ALU.mult))

                        def round_lo(f):
                            dve.wait_ge(fhi_s, f + 1)
                            dve.tensor_tensor(wide(f, 1), sl[f % 2][:], wide(f, 0).bitcast(F32), ALU.subtract).then_inc(flo_s, 1)

                        for f in range(FT):
                            dve.wait_ge(fe_s, f + 1)
                            r, c = fr[f % 2], cvf[f % 2]
                            link(dve, dve.tensor_copy(r[:, LEAD + S0 - 2:LEAD + S0], fpar[:, f, 4:6]))
                            link(dve, dve.tensor_scalar(c[:], r[:, 2:2 + TW], fpar[:, f, 0:1], fpar[:, f, 3:4], ALU.mult, ALU.add))
                            link(dve, dve.scalar_tensor_tensor(out=c[:], in0=r[:, 3:3 + TW], scalar=fpar[:, f, 1:2], in1=c[:],
                                                               op0=ALU.mult, op1=ALU.add))
                            dve.scalar_tensor_tensor(out=c[:], in0=r[:, 4:4 + TW], scalar=fpar[:, f, 2:3], in1=c[:],
                                                     op0=ALU.mult, op1=ALU.add).then_inc(fcv_s, 1)
                            if f >= 1:
                                round_lo(f - 1)
                            dve.wait_ge(fth_s, f + 1)
                            if f >= 2:
                                dve.wait_ge(flo_s, f - 1)
                            dve.scalar_tensor_tensor(out=sl[f % 2][:], in0=th[:], scalar=1.0, in1=c[:], op0=ALU.add,
                                                     op1=ALU.mult).then_inc(fsl_s, 1)
                            dve.wait_ge(fsl_s, f + 1)
                            dve.wait_ge(w.used, 2 * f + 2)
                            dve.tensor_tensor(halves(sl[f % 2][:]), halves(sl[f % 2][:]), slot(2 + f % 2), ALU.mult).then_inc(ff_s, 1)
                        round_lo(FT - 1)

                    @block.tensor
                    def _(pe):
                        for n in range(2 * FT):
                            f, up = divmod(n, 2)
                            if f >= 2:
                                if up:
                                    pe.wait_ge(ff_s, f - 1)
                                else:
                                    pe.wait_ge(fe_s, f - 1)
                            for k in range(KB):
                                w.multiply(pe, slot(2 * up + f % 2), hq_hi[:, k, :], hq_lo[:, k, :], k == 0, k == KB - 1)

            hq_st.close()
            with ExitStack() as ms:
                sq = [sb(ms, f"zsq{n}", [P, TW]) for n in range(2)]
                rs0 = sb(ms, "zrs", [P, TW])
                w = Stream(ms, "z", [i["w_ffn_out"][n] for n in range(FT)], w.base + w.own, True, [])
                ev_s, tile_s, sq_s, ss_s, root_s, y_s, dve_s, o_s = sems(ms, "z_ev z_tile z_sq z_ss z_root z_y z_dve z_o")
                fo = sb(ms, "fo", [P, KB, TW])
                with nc.Block(no_gpsimd_drain=True) as block:
                    @block.sync
                    def _(sp):
                        for n in range(FT):
                            w.load(sp, n)
                        for t in range(KB):
                            sp.wait_ge(y_s, t + 1)
                            sp.dma_start(o["y"][:, t, :], mrg[:, t, :]).then_inc(o_s, 16)
                        sp.wait_ge(o_s, 16 * KB)

                    @block.gpsimd
                    def _(pool):
                        for n in range(FT):
                            w.split_lo(pool, n)

                    @block.scalar
                    def _(act):
                        n = 2
                        for m in range(KB):
                            while n < FT and (n - 2 + 1) * KB <= (m + 1) * FT:
                                w.split_hi(act, n)
                                n += 1
                            if (m + 1) * FT % KB == 0:
                                act.wait_ge(w.used, (m + 1) * FT // KB)
                            else:
                                act.wait_ge(tile_s, sum((j + 1) * FT % KB != 0 for j in range(m + 1)))
                            act.activation(halves(fo[:, m, :]), slot(m % 2), ACT.Copy).then_inc(ev_s, 1)
                            act.wait_ge(ev_s, m + 1)
                            if m >= 2:
                                act.wait_ge(ss_s, m - 1)
                            act.activation(sq[m % 2][:], fo[:, m, :], ACT.Square).then_inc(sq_s, 1)
                        act.wait_ge(ss_s, KB)
                        norm_terms(act, None, rs0, root_s, 1.0 / D, 3)

                    @block.vector
                    def _(dve):
                        link = chain(dve_s)
                        dve.wait_ge(root_s, 1)
                        link(dve, dve.reciprocal(rs0[:], rs0[:]))
                        for t in range(KB):
                            link(dve, dve.tensor_tensor(tmp[t % 2][:], fo[:, t, :], rs0[:], ALU.mult))
                            for c0, L, g in RANGES:
                                ins = dve.scalar_tensor_tensor(out=mrg[:, t, c0:c0 + L], in0=tmp[t % 2][:, c0:c0 + L],
                                                               scalar=gate[:, 1, t, g:g + 1], in1=mrg[:, t, c0:c0 + L],
                                                               op0=ALU.mult, op1=ALU.add)
                            ins.then_inc(y_s, 1)

                    @block.tensor
                    def _(pe):
                        def squares(t):
                            pe.wait_ge(sq_s, t + 1)
                            for hh in range(2):
                                mm = pe.matmul(psum[:, 6 + hh, 0:HW], ones[:], sq[t % 2][:, hh * HW:(hh + 1) * HW],
                                               start=t == 0, stop=t == KB - 1)
                            mm.then_inc(ss_s, 1)

                        for m in range(KB):
                            if m >= 2:
                                pe.wait_ge(ev_s, m - 1)
                            for k in range(FT):
                                w.multiply(pe, slot(m % 2), wide(k, 0), wide(k, 1), k == 0, k == FT - 1,
                                           tile_s if k == FT - 1 else None)
                            if m >= 1:
                                squares(m - 1)
                        squares(KB - 1)


def columns(v):
    v = np.asarray(v)
    v = v.reshape(v.shape[:-1] + (-1, P))
    return np.ascontiguousarray(np.moveaxis(v, -1, 0))


def chunks(m):
    k, n = m.shape[0] // D, m.shape[1] // P
    return np.ascontiguousarray(m.reshape(k, KB, P, n, P).transpose(3, 0, 2, 1, 4).reshape(n * k, P, D))


def kernel(**inputs):
    import concourse.bacc as bacc
    from concourse.bass_utils import run_bass_kernel_spmd

    a = {n: np.asarray(v) for n, v in inputs.items()}
    f32 = np.float32
    x = np.zeros((P, KB, TW), a["x_prompt"].dtype)
    x[:, :, 0:T] = a["x_prompt"][0].T.reshape(KB, P, T).transpose(1, 0, 2)
    x[:, :, S0:] = a["x_sample"][0].T.reshape(KB, P, S).transpose(1, 0, 2)
    c = np.stack([a["c_prompt"][0], a["c_sample"][0]], -1).reshape(KB, P, 2).transpose(1, 0, 2)

    w_in = a["w_in"][0]
    inner, conv_dim, n_heads = 2048, 4096, 32
    at = np.cumsum([0, inner, conv_dim, n_heads, 1024, 256, 256, 2048])
    w_z, w_xbc, w_dt, w_q, w_k, w_v, w_g = (w_in[:, at[j]:at[j + 1]] for j in range(7))
    w_dt = np.concatenate([w_dt, np.zeros((D, P - n_heads), w_dt.dtype)], 1)
    zc, xc = chunks(w_z), chunks(w_xbc)
    w_grp = np.concatenate([np.stack([xc[16 + g], xc[24 + g], xc[2 * g], xc[2 * g + 1], zc[2 * g], zc[2 * g + 1]])
                            for g in range(GROUPS)])
    gc = chunks(w_g)
    w_att = chunks(a["w_att_out"][0])
    w_grp = np.concatenate([w_grp, gc[8:8 + GT], w_att[0:RAW_SLOTS]]).reshape(-1, D)
    fi = chunks(a["w_ffn_in"][0])
    w_ffn_in = np.stack([fi[f + FT * u] for f in range(FT) for u in range(2)])
    fo = a["w_ffn_out"][0].reshape(FT, P, KB, P).transpose(2, 0, 1, 3).reshape(FT, KB, P, P)
    w_ffn_out = np.ascontiguousarray(fo.transpose(0, 2, 1, 3)).reshape(FT, P, D)
    ada = np.roll(a["w_ada"][0].reshape(KB, P, ADA_UP + ADA_LATE, ADA_W).transpose(2, 1, 0, 3), -ADA_UP, axis=0)

    cw, cb, ctx = columns(a["ssm_conv_w"][0]), columns(a["ssm_conv_b"][0]), columns(a["state_conv"][0, 0])
    heads = a["ssm_d"][0].reshape(GROUPS, 2, 2)
    gp = np.zeros((P, GROUPS, GP_N), cw.dtype)
    for g in range(GROUPS):
        for j, t in enumerate((16 + g, 24 + g, 2 * g, 2 * g + 1)):
            gp[:, g, GP_W + TAPS * j:GP_W + TAPS * (j + 1)] = cw[:, :, t]
            gp[:, g, GP_B + j] = cb[:, t]
            gp[:, g, GP_CTX + 3 * j:GP_CTX + 3 * j + 3] = ctx[:, :, t]
        gp[:, g, GP_D:GP_D + 2] = np.repeat(heads[g], HD, axis=1).T
    fw, fb, fctx = columns(a["ffn_conv_w"][0]), columns(a["ffn_conv_b"][0]), columns(a["state_ffn_conv"][0, 0])
    fpar = np.concatenate([fw.transpose(0, 2, 1), fb[:, :, None], fctx.transpose(0, 2, 1)], 2)

    half, theta = 8, 500000.0
    pos = np.zeros(TW, f32)
    pos[0:T] = np.arange(T)
    pos[S0:] = 256 + np.arange(S)
    inv = (f32(theta) ** (-np.arange(half, dtype=f32) / f32(half))).astype(f32)
    ang = (pos[None, :] * inv[:, None]).astype(f32)
    cos, sin, rot = np.ones((P, TW), f32), np.zeros((P, TW), f32), np.zeros((P, P), f32)
    for b in (0, 64):
        for j in range(half):
            cos[b + j] = cos[b + half + j] = np.cos(ang[j])
            sin[b + j], sin[b + half + j] = -np.sin(ang[j]), np.sin(ang[j])
            rot[b + half + j, b + j] = rot[b + j, b + half + j] = 1.0

    mask_k = np.zeros((1, WIN + T), f32)
    mask_k[0, 0:WIN] = np.finfo(f32).min
    sk = a["attn_sinks"][0].reshape(KV, 2, 2)
    sinks = np.repeat(sk.transpose(1, 0, 2).reshape(2, 2 * KV), CH, axis=0)
    sinks_s = np.concatenate([np.repeat(sk.transpose(1, 0, 2).reshape(2, 2 * KV), S, axis=0)] * 2, axis=0)
    state = a["state_ssm"][0, 0].reshape(GROUPS, HPG * HD, NS).transpose(0, 2, 1).reshape(GROUPS * P, HPG * HD)
    consts = np.zeros((P, 2), f32)
    consts[:, 0], consts[:, 1] = EPS, 1.0

    ins = dict(
        x=x, c=c, ident=np.eye(P, dtype=f32), consts=consts, mask_u=np.triu(np.ones((P, P), f32)),
        vecs=np.stack([columns(a[n][0]) for n in ("norm_mix_pre", "norm_mix_post", "norm_ffn_pre", "norm_ffn_post")], 1),
        b_ada=columns(a["b_ada"][0]), w_ada=ada, w_qkv=np.concatenate([chunks(w_k), chunks(w_q), chunks(w_dt), chunks(w_v)]),
        w_grp=w_grp, w_gate=gc, w_att=w_att, w_ssm=chunks(a["w_ssm_out"][0]), w_out=chunks(a["w_out"][0]),
        w_ffn_in=w_ffn_in, w_ffn_out=w_ffn_out, gp=gp, fpar=fpar, cos=cos, sin=sin, rot=rot,
        dt_par=np.stack([a["ssm_dt_bias"][0], a["ssm_a_log"][0]], 1), mask_k=mask_k, sinks=sinks, sinks_s=sinks_s, state=state,
        ssm_norm=columns(a["ssm_norm"][0]),
        cache_k=a["cache_k"][0, 0].transpose(2, 1, 0), cache_v=a["cache_v"][0, 0].reshape(WIN, 256),
    )
    outs = dict(y=(P, KB, TW), ssm_p=(GROUPS * P, 256), ssm_s=(GROUPS * P, 256), conv_p=(GROUPS * P, 4, 3), conv_s=(GROUPS * P, 4, 3),
                k_p=(256, WIN), k_s=(256, WIN), v_p=(WIN, 256), v_s=(WIN, 256), ffn=(P, FT, 4))
    inner_dram = dict(q=(ATT_CHUNKS, P, KB, CH), qs=(P, KB, S), k=(64, KV, WIN + T), ks=(64, KV, WIN + S), v=(WIN + T, 256),
                      vs=(WIN + S, 256), acs=(32, TW), att=(P, KB, TW), gate=(P, GT, TW),
                      mod=(2 * ADA_LATE, ADA_W), y=(GROUPS * P, 2 * TW))

    nc = bacc.Bacc("TRN2", target_bir_lowering=False, num_devices=1)
    arrays = {f"in_{n}": np.ascontiguousarray(v) for n, v in ins.items()}
    i = {n: nc.dram_tensor(f"in_{n}", v.shape, F32, kind="ExternalInput").ap() for n, v in ins.items()}
    o = {n: nc.dram_tensor(f"out_{n}", s, F32, kind="ExternalOutput").ap() for n, s in outs.items()}
    scratch = {n: nc.dram_tensor(f"mem_{n}", s, F32, kind="Internal").ap() for n, s in inner_dram.items()}
    build_layer(nc, i, o, scratch)
    r = run_bass_kernel_spmd(nc, [arrays], core_ids=[0]).results[0]
    got = {n: np.asarray(r[f"out_{n}"]) for n in outs}

    def rows(cols):
        return got["y"][:, :, cols].transpose(2, 1, 0).reshape(1, -1, D)

    def state_out(s):
        return s.reshape(GROUPS, NS, HPG, HD).transpose(0, 2, 3, 1).reshape(1, 1, 32, HD, NS)

    def conv_out(s):
        s = s.reshape(GROUPS, P, 4, 3)
        parts = [s[:, :, 2:4].transpose(3, 0, 2, 1).reshape(3, inner), s[:, :, 0].transpose(2, 0, 1).reshape(3, 1024),
                 s[:, :, 1].transpose(2, 0, 1).reshape(3, 1024)]
        return np.concatenate(parts, 1).reshape(1, 1, 3, conv_dim)

    def kv_out(s):
        return s.reshape(1, 1, WIN, KV, HD)

    def ffn_out(s):
        return s.transpose(2, 1, 0).reshape(1, 1, 2, FT * P)

    return (rows(slice(0, T)), rows(slice(S0, TW)), state_out(got["ssm_p"]), conv_out(got["conv_p"]), kv_out(got["k_p"].T),
            kv_out(got["v_p"]), ffn_out(got["ffn"][:, :, 0:2]), state_out(got["ssm_s"]), conv_out(got["conv_s"]),
            kv_out(got["k_s"].T), kv_out(got["v_s"]), ffn_out(got["ffn"][:, :, 2:4]))
```

```python
from contextlib import ExitStack

import concourse.bass as bass
import numpy as np
from concourse import mybir

F32 = mybir.dt.float32
F32R = mybir.dt.float32r
ALU = mybir.AluOpType
ACT = mybir.ActivationFunctionType
AX = mybir.AxisListType

P = 128
D = 1024
KB = D // P
T, S = 512, 32
GAP = 4
S0 = T + GAP
TW = S0 + S
HW = TW // 2
LEAD = 4
GROUPS, HPG, HD, NS = 8, 4, 64, 128
GT = 6
KV, CH, WIN = 4, 64, 128
KEYS = WIN + CH
FT = 22
ATT_CHUNKS = T // CH
EPS = 1e-6
TAPS, FTAPS = 4, 3
GP_W, GP_B, GP_CTX, GP_D, GP_N = 0, 16, 20, 32, 34
SCAN = [(128 * c, 128) for c in range(T // 128)] + [(S0, S)]
RAW_SLOTS, HL_SLOTS = 3, 2
HL_AHEAD = 1
ADA_W = 512
(SHIFT1, SCALE1, GATE1, SHIFT2, SCALE2, GATE2) = range(0, 6 * D // ADA_W, D // ADA_W)
RANGES = [(0, T, 0), (S0, S, 1)]


def halves(ap):
    return ap.rearrange("p (a b) -> p a b", a=2)


def flat(t):
    return t[:].rearrange("p a b -> p (a b)")


def bcast_mid(ap, n):
    return ap.unsqueeze(2).to_broadcast((ap.shape[0], ap.shape[1], n))


def build_layer(nc, i, o, scratch):
    top = ExitStack()

    def sb(stack, name, shape, dt=F32, side=None):
        return stack.enter_context(nc.sbuf_tensor(name, shape, dt, side=side))

    def sems(stack, names):
        return [stack.enter_context(nc.semaphore(n)) for n in names.split()]

    with top:
        psum = top.enter_context(nc.psum_tensor("psum", [P, 8, 512], F32))
        ident = sb(top, "ident", [P, P])
        ones = sb(top, "ones", [P, P])
        consts = sb(top, "consts", [P, 2])
        eps_c, one_c = consts[:, 0:1], consts[:, 1:2]
        vecs = sb(top, "vecs", [P, 4, KB])
        mod = sb(top, "mod", [P, 48, 2])
        gain = sb(top, "gain", [P, 2, KB, 2])
        gate = sb(top, "gate", [P, 2, KB, 2])
        c_silu = sb(top, "c_silu", [P, KB, 2])
        b_ada = sb(top, "b_ada", [P, 48])
        raw_w = [sb(top, f"raw_w{n}", [P, D]) for n in range(RAW_SLOTS)]
        w_hi = [sb(top, f"w_hi{n}", [P, KB, P], F32R) for n in range(HL_SLOTS)]
        w_lo = [sb(top, f"w_lo{n}", [P, KB, P], F32R) for n in range(HL_SLOTS)]
        hp_hi = sb(top, "hp_hi", [P, KB, TW], F32R)
        hp_lo = sb(top, "hp_lo", [P, KB, TW], F32R)

        def slot(s):
            return psum[:, 2 * s:2 * s + 2, 0:HW]

        class Stream:

            def __init__(self, stack, tag, sources, base, ready, following):
                self.own, self.src, self.base = len(sources), sources + following, base
                self.raw_ready, self.hl_ready = (RAW_SLOTS, HL_AHEAD) if ready else (0, 0)
                self.landed = sems(stack, " ".join(f"{tag}_landed{n}" for n in range(RAW_SLOTS)))
                self.hi_done, self.lo_done, self.used = sems(stack, f"{tag}_hi {tag}_lo {tag}_used")
                self.all = [*self.landed, self.hi_done, self.lo_done, self.used]
                self.block = 0

            def raw_slot(self, n):
                return (self.base + n) % RAW_SLOTS

            def hl_slot(self, n):
                return (self.base + n) % HL_SLOTS

            def landings(self, n):
                return (n - self.raw_ready) // RAW_SLOTS + 1

            def load(self, sp, n):
                if not self.raw_ready <= n < len(self.src):
                    return
                if n - RAW_SLOTS >= self.hl_ready:
                    sp.wait_ge(self.lo_done, n - RAW_SLOTS - self.hl_ready + 1)
                sp.dma_start(raw_w[self.raw_slot(n)][:], self.src[n]).then_inc(self.landed[self.raw_slot(n)], 16)

            def all_landed(self, sp):
                for n in range(max(len(self.src) - RAW_SLOTS, self.raw_ready), len(self.src)):
                    sp.wait_ge(self.landed[self.raw_slot(n)], 16 * self.landings(n))

            def splits(self, n):
                return self.hl_ready <= n < min(self.own + HL_AHEAD, len(self.src))

            def split_hi(self, act, n):
                if not self.splits(n):
                    return
                if n >= self.raw_ready:
                    act.wait_ge(self.landed[self.raw_slot(n)], 16 * self.landings(n))
                if n >= HL_SLOTS:
                    act.wait_ge(self.used, n - HL_SLOTS + 1)
                act.activation(flat(w_hi[self.hl_slot(n)]), raw_w[self.raw_slot(n)][:], ACT.Copy).then_inc(self.hi_done, 1)

            def split_lo(self, eng, n):
                if not self.splits(n):
                    return
                eng.wait_ge(self.hi_done, n - self.hl_ready + 1)
                eng.tensor_tensor(flat(w_lo[self.hl_slot(n)]), raw_w[self.raw_slot(n)][:],
                                  flat(w_hi[self.hl_slot(n)]).bitcast(F32), ALU.subtract).then_inc(self.lo_done, 1)

            def all_split(self, eng):
                eng.wait_ge(self.lo_done, min(self.own + HL_AHEAD, len(self.src)) - self.hl_ready)

            def wait_split(self, pe, n):
                if n >= self.hl_ready:
                    pe.wait_ge(self.lo_done, n - self.hl_ready + 1)

            def multiply(self, pe, out, hi, lo, first, last, done=None):
                n, k = divmod(self.block, KB)
                self.block += 1
                if k == 0:
                    self.wait_split(pe, n)
                wh, wl = w_hi[self.hl_slot(n)][:, k, :], w_lo[self.hl_slot(n)][:, k, :]
                for h in range(2):
                    cols = slice(h * HW, (h + 1) * HW)
                    for j, (w, x) in enumerate(((wh, hi), (wh, lo), (wl, hi))):
                        mm = pe.matmul(out[:, h, :], w, x[:, cols], start=first and j == 0, stop=last and j == 2)
                if k == KB - 1:
                    mm.then_inc(self.used, 1)
                elif done is not None:
                    mm.then_inc(done, 1)

        def chain(sem):
            count = [0]

            def link(eng, ins):
                count[0] += 1
                ins.then_inc(sem, 1)
                eng.wait_ge(sem, count[0])
            return link

        def modulation(pe, out, block, ready=None):
            for k in range(KB):
                mm = pe.matmul(out, c_silu[:, k, :], block[:, k, :], start=k == 0, stop=k == KB - 1)
            return mm

        def turn_rows(pe, bank, col, row):
            for b in range(ADA_W // P):
                mm = pe.transpose(psum[:, bank, col + 2 * b:col + 2 * b + 2], row[:, b * P:(b + 1) * P], ident[0:2, 0:2])
            return mm

        def add_bias(dve, first, count, bank):
            return dve.tensor_tensor(mod[:, first:first + count, :], psum[:, bank, 0:2 * count].rearrange("p (a b) -> p a b", b=2),
                                     bcast_mid(b_ada[:, first:first + count], 2), ALU.add)

        late_st = ExitStack()
        late_row = sb(late_st, "late_row", [2, 4, ADA_W])

        with ExitStack() as st:
            UP = [SHIFT1, SHIFT1 + 1, SCALE1, SCALE1 + 1]
            BLOCKS = UP + [SHIFT2, SHIFT2 + 1]
            ADA_SLOTS = 5
            ada = [sb(st, f"ada{n}", [P, KB, ADA_W]) for n in range(ADA_SLOTS)]
            mod_row = sb(st, "mod_row", [2, len(UP), ADA_W])
            x = sb(st, "x", [P, KB, TW])
            c_in = sb(st, "c_in", [P, KB, 2])
            c_th = sb(st, "c_th", [P, KB, 2])
            sq = [sb(st, f"sq{n}", [P, TW]) for n in range(2)]
            rstd = sb(st, "rstd", [P, TW])
            h = [sb(st, f"h{n}", [P, TW]) for n in range(2)]
            xr = [sb(st, f"xr{n}", [P, TW]) for n in range(2)]
            (in_x, in_c, c_s, ada_done, row_s, turn_s, sq_s, root_s, dve_s, h_s, hi_s, sq_used, const_s,
             lo_s) = sems(
                st, "a_x a_c a_silu a_ada_done a_row a_turn a_sq a_root a_dve a_h a_hi a_squsd a_const a_lo")
            in_ada = sems(st, " ".join(f"a_ada{n}" for n in range(2 * len(BLOCKS))))
            w = Stream(st, "aw", [], 0, False, [i["w_qkv"][n] for n in range(RAW_SLOTS)])
            first_sem = in_x.num
            with nc.Block(no_gpsimd_drain=True) as block:
                @block.sync
                def _(sp):
                    sp.dma_start(c_in[:], i["c"]).then_inc(in_c, 16)
                    sp.dma_start(ident[:], i["ident"]).then_inc(in_c, 16)
                    sp.dma_start(consts[:], i["consts"]).then_inc(in_c, 16)
                    sp.dma_start(vecs[:], i["vecs"]).then_inc(in_c, 16)
                    sp.dma_start(b_ada[:], i["b_ada"]).then_inc(in_c, 16)
                    sp.dma_start(x[:], i["x"]).then_inc(in_x, 16)
                    for n in range(2 * len(BLOCKS)):
                        a, ks = n // 2, slice(KB // 2 * (n % 2), KB // 2 * (n % 2 + 1))
                        if a >= ADA_SLOTS:
                            sp.wait_ge(ada_done, a - ADA_SLOTS + 1)
                        sp.dma_start(ada[a % ADA_SLOTS][:, ks, :], i["w_ada"][BLOCKS[a], :, ks, :]).then_inc(in_ada[n], 16)
                    for n in range(RAW_SLOTS):
                        w.load(sp, n)
                    w.all_landed(sp)

                @block.gpsimd
                def _(pool):
                    pool.memset(ones[:], 1.0).then_inc(const_s, 1)
                    pool.memset(h[0][:, T:S0], 0.0).then_inc(const_s, 1)
                    pool.memset(h[1][:, T:S0], 0.0).then_inc(const_s, 1)
                    for n in range(HL_AHEAD):
                        w.split_lo(pool, n)
                    for t in range(KB):
                        pool.wait_ge(hi_s, t + 1)
                        pool.tensor_tensor(hp_lo[:, t, :], h[t % 2][:], hp_hi[:, t, :].bitcast(F32),
                                           ALU.subtract).then_inc(lo_s, 1)
                    w.all_split(pool)
                    pool.wait_ge(lo_s, KB)

                @block.scalar
                def _(act):
                    act.wait_ge(in_c, 80)
                    act.activation(c_th[:], c_in[:], ACT.Tanh, scale=0.5).then_inc(c_s, 1)
                    act.wait_ge(in_x, 16)
                    for t in range(KB):
                        if t >= 2:
                            act.wait_ge(sq_used, t - 1)
                        act.activation(sq[t % 2][:], x[:, t, :], ACT.Square).then_inc(sq_s, 1)
                    act.wait_ge(sq_used, KB)
                    act.activation(halves(rstd[:]), slot(0), ACT.Sqrt, bias=eps_c, scale=1.0 / D).then_inc(root_s, 1)
                    for a in range(len(UP)):
                        act.wait_ge(ada_done, a + 1)
                        act.activation(mod_row[:, a, :], psum[0:2, 2 + a, :], ACT.Copy).then_inc(row_s, 1)
                    for n in range(HL_AHEAD):
                        w.split_hi(act, n)
                    for t in range(KB):
                        act.wait_ge(h_s, t + 1)
                        act.activation(hp_hi[:, t, :], h[t % 2][:], ACT.Copy).then_inc(hi_s, 1)
                    for a in range(len(UP), len(BLOCKS)):
                        act.wait_ge(ada_done, a + 1)
                        act.activation(late_row[:, a - 2, :], psum[0:2, 2 + a % 4, :], ACT.Copy).then_inc(row_s, 1)

                @block.vector
                def _(dve):
                    link = chain(dve_s)
                    dve.wait_ge(c_s, 1)
                    link(dve, dve.scalar_tensor_tensor(out=c_silu[:], in0=c_th[:], scalar=1.0, in1=c_in[:],
                                                       op0=ALU.add, op1=ALU.mult))
                    dve.tensor_scalar(c_silu[:], c_silu[:], 0.5, None, ALU.mult).then_inc(c_s, 1)
                    dve.wait_ge(root_s, 1)
                    link(dve, dve.reciprocal(rstd[:], rstd[:]))
                    dve.wait_ge(turn_s, 1)
                    link(dve, add_bias(dve, 0, 2 * KB, 6))
                    link(dve, dve.scalar_tensor_tensor(out=gain[:, 0], in0=mod[:, KB:2 * KB, :], scalar=1.0,
                                                       in1=bcast_mid(vecs[:, 0, :], 2), op0=ALU.add, op1=ALU.mult))
                    dve.wait_ge(const_s, 3)
                    for t in range(KB):
                        link(dve, dve.tensor_tensor(xr[t % 2][:], x[:, t, :], rstd[:], ALU.mult))
                        if t >= 2:
                            dve.wait_ge(lo_s, t - 1)
                        dve.tensor_scalar(h[t % 2][:, 0:T], xr[t % 2][:, 0:T], gain[:, 0, t, 0:1],
                                          mod[:, t, 0:1], ALU.mult, ALU.add)
                        dve.tensor_scalar(h[t % 2][:, S0:TW], xr[t % 2][:, S0:TW], gain[:, 0, t, 1:2],
                                          mod[:, t, 1:2], ALU.mult, ALU.add).then_inc(h_s, 1)

                @block.tensor
                def _(pe):
                    pe.wait_ge(const_s, 1)
                    for t in range(KB):
                        pe.wait_ge(sq_s, t + 1)
                        for hh in range(2):
                            mm = pe.matmul(psum[:, hh, 0:HW], ones[:], sq[t % 2][:, hh * HW:(hh + 1) * HW],
                                           start=t == 0, stop=t == KB - 1)
                        mm.then_inc(sq_used, 1)
                    pe.wait_ge(c_s, 2)
                    def block_product(a):
                        out = psum[0:2, 2 + a % 4, :]
                        for k in range(KB):
                            if k % (KB // 2) == 0:
                                pe.wait_ge(in_ada[2 * a + k // (KB // 2)], 16)
                            mm = pe.matmul(out, c_silu[:, k, :], ada[a % ADA_SLOTS][:, k, :], start=k == 0, stop=k == KB - 1)
                        mm.then_inc(ada_done, 1)

                    for a in range(len(UP)):
                        block_product(a)
                    pe.wait_ge(in_c, 80)
                    for a in range(len(UP)):
                        pe.wait_ge(row_s, a + 1)
                        mm = turn_rows(pe, 6, 8 * a, mod_row[:, a, :])
                    mm.then_inc(turn_s, 1)
                    for a in range(len(UP), len(BLOCKS)):
                        block_product(a)

        with ExitStack() as loop_st:
            raw = sb(loop_st, "raw", [P, GT, LEAD + TW])
            gp_all = sb(loop_st, "gp_all", [P, GROUPS, GP_N])
            tok_all = sb(loop_st, "tok_all", [P, GROUPS, 5, 3, HPG])
            mask_u = sb(loop_st, "mask_u", [P, P])
            ada_g1 = [sb(loop_st, f"ada_g{n}", [P, KB, ADA_W]) for n in range(2)]

            def group_chunk(n):
                return i["w_grp"][bass.ds(n * P, P), :]

            att = ExitStack()
            loop_st.enter_context(att)
            kw = sb(att, "kw", [P, KV, KEYS])
            vw0 = sb(att, "vw0", [P, 256])
            vw1 = sb(att, "vw1", [CH, 256])
            mask_k = sb(att, "mask_k", [P, KEYS])
            sink = sb(att, "sink", [P, 2 * KV])
            sc = sb(att, "sc", [P, 2 * KV, KEYS])
            mx = sb(att, "mx", [P, 2 * KV])
            nmx = sb(att, "nmx", [P, 2 * KV])
            sm = sb(att, "sm", [P, 2 * KV])
            es = sb(att, "es", [P, 2 * KV])
            rden = sb(att, "rden", [P, 2 * KV])
            pt0 = [sb(att, f"pt0{n}", [P, 2, P]) for n in range(2)]
            pt1 = [sb(att, f"pt1{n}", [CH, 2, P]) for n in range(2)]
            oc = sb(att, "oc", [P, KB, CH])

            q_loop = sb(att, "q_loop", [P, KB, CH])

            def load_attention(sp, sem, n, q_buf, q, k, v0, v1, mask):
                for dst, src in ((q_buf[:], q), (kw[0:64, :, 0:WIN + n], k), (kw[64:128, :, 0:WIN + n], k), (vw0[:], v0),
                                 (vw1[0:n, :], v1), (mask_k[:], mask), (sink[:], i["sinks"] if n == CH else i["sinks_s"])):
                    sp.dma_start(dst, src).then_inc(sem, 16)

            ATT_IN = 7 * 16

            def load_chunk(sp, sem, g):
                load_attention(sp, sem, CH, q_loop, scratch["q"][bass.ds(g, 1)].rearrange("c p t k -> p (c t) k"),
                               scratch["k"][:, :, bass.ds(g * CH, KEYS)], scratch["v"][bass.ds(g * CH, WIN), :],
                               scratch["v"][bass.ds(g * CH + WIN, CH), :],
                               i["mask_k"][:, bass.ds(g * CH, KEYS)].to_broadcast((P, KEYS)))

            class Attention:

                def __init__(self, stack, tag, rows, masked, q, ahead):
                    self.n, self.masked, self.q, self.ahead = rows, masked, q, ahead
                    self.all = sems(stack, " ".join(f"{tag}_{x}" for x in (
                        "keys_in scores scores_read maxima exps normed turned turned_read values out_read stored order").split()))
                    (self.in_s, self.s_s, self.se_s, self.nm_s, self.ex_s, self.pn_s, self.pt_s, self.pe_s, self.pv_s,
                     self.oc_s, self.out_s, self.dv_s) = self.all

                def scores(self, pe, kv):
                    n, m = self.n, 2 * self.n
                    if kv == 0 and not self.ahead:
                        pe.wait_ge(self.in_s, ATT_IN)
                    if kv >= 2:
                        pe.wait_ge(self.se_s, kv - 1)
                    for par in range(2):
                        rows = slice(64 * par, 64 * par + 64)
                        mm = pe.matmul(psum[0:m, 4 + 2 * (kv % 2) + par, 0:WIN + n], self.q[rows, 2 * kv:2 * kv + 2, :].rearrange("p a b -> p (a b)"),
                                       kw[rows, kv, 0:WIN + n], start=True, stop=True)
                    mm.then_inc(self.s_s, 1)

                def evac_scores(self, dve, kv):
                    n, m = self.n, 2 * self.n
                    dve.wait_ge(self.s_s, kv + 1)
                    dst = sc[0:m, 2 * kv:2 * kv + 2, 0:WIN + n]
                    src = psum[0:m, 4 + 2 * (kv % 2):6 + 2 * (kv % 2), 0:WIN + n]
                    if self.masked:
                        dve.scalar_tensor_tensor(out=dst, in0=src, scalar=HD ** -0.5,
                                                 in1=mask_k[0:m, 0:WIN + n].unsqueeze(1).to_broadcast((m, 2, WIN + n)),
                                                 op0=ALU.mult, op1=ALU.add).then_inc(self.se_s, 1)
                    else:
                        dve.tensor_scalar(dst, src, HD ** -0.5, None, ALU.mult).then_inc(self.se_s, 1)

                def maxima(self, dve):
                    m, w_ = 2 * self.n, WIN + self.n
                    dve.wait_ge(self.se_s, KV)
                    dve.tensor_reduce(mx[0:m], sc[0:m, :, 0:w_], AX.X, ALU.max).then_inc(self.dv_s, 1)
                    dve.wait_ge(self.dv_s, 1)
                    dve.tensor_tensor(mx[0:m], mx[0:m], sink[0:m], ALU.max).then_inc(self.dv_s, 1)
                    dve.wait_ge(self.dv_s, 2)
                    dve.tensor_scalar(nmx[0:m], mx[0:m], -1.0, None, ALU.mult).then_inc(self.nm_s, 1)
                    dve.tensor_tensor(es[0:m], sink[0:m], mx[0:m], ALU.subtract).then_inc(self.nm_s, 1)

                def exps(self, act):
                    m, w_ = 2 * self.n, WIN + self.n
                    act.wait_ge(self.nm_s, 2)
                    for u in range(2 * KV):
                        act.activation(sc[0:m, u, 0:w_], sc[0:m, u, 0:w_], ACT.Exp, bias=nmx[0:m, u:u + 1],
                                       accum_out=sm[0:m, u:u + 1])
                    act.activation(es[0:m], es[0:m], ACT.Exp).then_inc(self.ex_s, 1)

                def normalise(self, dve):
                    m, w_ = 2 * self.n, WIN + self.n
                    dve.wait_ge(self.ex_s, 1)
                    dve.tensor_tensor(sm[0:m], sm[0:m], es[0:m], ALU.add).then_inc(self.dv_s, 1)
                    dve.wait_ge(self.dv_s, 3)
                    dve.reciprocal(rden[0:m], sm[0:m]).then_inc(self.dv_s, 1)
                    dve.wait_ge(self.dv_s, 4)
                    for u in range(2 * KV):
                        dve.tensor_scalar(sc[0:m, u, 0:w_], sc[0:m, u, 0:w_], rden[0:m, u:u + 1], None,
                                          ALU.mult).then_inc(self.pn_s, 1)

                def turn(self, pe, kv):
                    n, m, bank = self.n, 2 * self.n, 4 + kv % 2
                    pe.wait_ge(self.pn_s, 2 * kv + 2)
                    if kv >= 2:
                        pe.wait_ge(self.pe_s, kv - 1)
                    for par in range(2):
                        pe.transpose(psum[:, bank, par * P:par * P + m], sc[0:m, 2 * kv + par, 0:WIN], ident[0:m, 0:m])
                        mm = pe.transpose(psum[0:n, bank, 256 + par * P:256 + par * P + m], sc[0:m, 2 * kv + par, WIN:WIN + n],
                                          ident[0:m, 0:m])
                    mm.then_inc(self.pt_s, 1)

                def evac_turned(self, act, kv):
                    n, m, bank = self.n, 2 * self.n, 4 + kv % 2
                    act.wait_ge(self.pt_s, kv + 1)
                    if kv >= 2:
                        act.wait_ge(self.pv_s, kv - 1)
                    act.activation(pt0[kv % 2][:, :, 0:m], psum[:, bank, 0:256].rearrange("p (a b) -> p a b", a=2)[:, :, 0:m], ACT.Copy)
                    act.activation(pt1[kv % 2][0:n, :, 0:m], psum[0:n, bank, 256:512].rearrange("p (a b) -> p a b", a=2)[:, :, 0:m],
                                   ACT.Copy).then_inc(self.pe_s, 1)

                def values(self, pe, kv):
                    n, m = self.n, 2 * self.n
                    pe.wait_ge(self.pe_s, kv + 1)
                    for par in range(2):
                        out = psum[64 * par:64 * par + 64, 7, kv * m:kv * m + m]
                        pe.matmul(out, vw0[:, 64 * kv:64 * kv + 64], pt0[kv % 2][:, par, 0:m], start=True, stop=False)
                        mm = pe.matmul(out, vw1[0:n, 64 * kv:64 * kv + 64], pt1[kv % 2][0:n, par, 0:m], start=False, stop=True)
                    mm.then_inc(self.pv_s, 1)

                def evac_out(self, act):
                    n = self.n
                    act.wait_ge(self.pv_s, KV)
                    act.activation(oc[:, :, 0:n], psum[:, 7, 0:8 * n].rearrange("p (a b) -> p a b", a=8), ACT.Copy).then_inc(self.oc_s, 1)

                def store(self, sp, dst):
                    sp.wait_ge(self.oc_s, 1)
                    sp.dma_start(dst, oc[:, :, 0:self.n]).then_inc(self.out_s, 16)

            with ExitStack() as st:
                cos = sb(st, "cos", [P, TW])
                sin = sb(st, "sin", [P, TW])
                rot = sb(st, "rot", [P, P])
                zeros = sb(st, "zeros", [P, 256])
                qk = [sb(st, f"qk{n}", [P, TW]) for n in range(2)]
                t_cos = [sb(st, f"t_cos{n}", [P, TW]) for n in range(2)]
                qk_rot = [sb(st, f"qk_rot{n}", [P, TW]) for n in range(2)]
                v_sb = sb(st, "v_sb", [P, 5, 256])
                dt_v = sb(st, "dt_v", [32, TW])
                dt_n = sb(st, "dt_n", [32, TW])
                dt_e = sb(st, "dt_e", [32, TW])
                dt_l = sb(st, "dt_l", [32, TW])
                dt = sb(st, "dt", [32, TW])
                da = sb(st, "da", [32, TW])
                acs = sb(st, "acs", [32, TW])
                edt = sb(st, "edt", [32, TW])
                nacs = sb(st, "nacs", [32, TW])
                dt_par = sb(st, "dt_par", [32, 2])
                a_exp = sb(st, "a_exp", [32, 1])
                NK, NQ = 2, 8
                QK = NK + NQ
                DT, V0, G0 = QK, QK + 1, QK + 3
                AT = G0 + 2
                w = Stream(st, "b", [i["w_qkv"][n] for n in range(QK + 3)] + [group_chunk(n) for n in range(GT)],
                           0, True, [group_chunk(GT + n) for n in range(RAW_SLOTS)])
                NCH = w.own
                (in_s, init_s, evac_s, rot_s, rope_s, out_s0, out_s1, copy_s, acs_s, tr_s, dtp_s, sc_s,
                 dve_s, e_s) = sems(
                    st, "b_in b_init b_evac b_rot b_rope b_out0 b_out1 b_copy b_acs b_tr b_dtp b_sc b_dve b_e")
                ada_in, acs_out, tok_s = sems(st, "b_ada_in b_acs_out b_tok")
                at = Attention(st, "s", S, False, sb(st, "q_sample", [P, KB, S]), False)
                next_in, = sems(st, "b_next_in")
                out_s = [out_s0, out_s1]

                def q_dst(t):
                    return scratch["q"][0:ATT_CHUNKS, :, t, :].rearrange("c p k -> p c k")

                with nc.Block(no_gpsimd_drain=True) as block:
                    @block.sync
                    def _(sp):
                        for n in range(RAW_SLOTS, RAW_SLOTS + HL_SLOTS):
                            w.load(sp, n)
                        for dst, name in ((cos, "cos"), (sin, "sin"), (rot, "rot"), (dt_par, "dt_par"),
                                          (gp_all, "gp"), (mask_u, "mask_u")):
                            sp.dma_start(dst[:], i[name]).then_inc(in_s, 16)
                        sp.wait_ge(init_s, 1)
                        sp.dma_start(scratch["k"][:, 0:2, 0:WIN], zeros[0:64, :].rearrange("p (a b) -> p a b", a=2)).then_inc(copy_s, 16)
                        sp.dma_start(scratch["k"][:, 2:4, 0:WIN], zeros[0:64, :].rearrange("p (a b) -> p a b", a=2)).then_inc(copy_s, 16)
                        sp.dma_start(scratch["v"][0:WIN, :], zeros[:]).then_inc(copy_s, 16)
                        sp.dma_start(scratch["k"][:, :, WIN + T:], zeros[0:64, 0:KV * CH].rearrange("p (a b) -> p a b", a=KV)).then_inc(copy_s, 16)
                        sp.dma_start(scratch["v"][WIN + T:, :], zeros[0:CH, :]).then_inc(copy_s, 16)
                        for t in range(0, KB, 4):
                            sp.dma_start(scratch["q"][ATT_CHUNKS, :, t:t + 4, :], zeros[:].rearrange("p (a b) -> p a b", a=4)).then_inc(copy_s, 16)
                        sp.dma_start(scratch["att"][:, :, T:S0], zeros[:, 0:KB * GAP].rearrange("p (a b) -> p a b", a=KB)).then_inc(copy_s, 16)
                        sp.dma_start(scratch["ks"][:, :, 0:WIN], i["cache_k"]).then_inc(copy_s, 16)
                        sp.dma_start(scratch["vs"][0:WIN, :], i["cache_v"]).then_inc(copy_s, 16)
                        for j in range(NK):
                            for a in range(2):
                                kv = 2 * j + a
                                sp.dma_start(o["k_s"][64 * kv:64 * kv + 64, 0:WIN - S], i["cache_k"][:, kv, S:WIN]).then_inc(copy_s, 16)
                        sp.dma_start(o["v_s"][0:WIN - S, :], i["cache_v"][S:WIN, :]).then_inc(copy_s, 16)
                        n_copy = 15
                        for n in range(2):
                            sp.dma_start(ada_g1[n][:], i["w_ada"][GATE1 + n]).then_inc(ada_in, 16)
                        for n in range(RAW_SLOTS + HL_SLOTS, NCH):
                            w.load(sp, n)
                            j = n - RAW_SLOTS - HL_SLOTS
                            if j < QK:
                                sp.wait_ge(rope_s, j + 1)
                                r = qk_rot[j % 2]
                                if j < NK:
                                    for a in range(2):
                                        rows, kv = slice(64 * a, 64 * a + 64), 2 * j + a
                                        sp.dma_start(scratch["k"][:, kv, WIN:WIN + T], r[rows, 0:T]).then_inc(out_s[j % 2], 16)
                                        sp.dma_start(scratch["ks"][:, kv, WIN:WIN + S], r[rows, S0:TW]).then_inc(out_s[j % 2], 16)
                                    sp.dma_start(o["k_p"][P * j:P * j + P, :], r[:, T - WIN:T]).then_inc(out_s[j % 2], 16)
                                    sp.dma_start(o["k_s"][P * j:P * j + P, WIN - S:WIN], r[:, S0:TW]).then_inc(out_s[j % 2], 16)
                                else:
                                    t = j - NK
                                    sp.dma_start(q_dst(t), r[:, 0:T].rearrange("p (c k) -> p c k", k=CH)).then_inc(out_s[j % 2], 16)
                                    sp.dma_start(scratch["qs"][:, t, :], r[:, S0:TW]).then_inc(out_s[j % 2], 16)
                        sp.wait_ge(evac_s, G0)
                        sp.dma_start(scratch["v"][WIN:WIN + T, :].rearrange("(a p) d -> p a d", p=P), v_sb[:, 0:4, :]).then_inc(copy_s, 16)
                        sp.dma_start(scratch["vs"][WIN:WIN + S, :], v_sb[0:S, 4, :]).then_inc(copy_s, 16)
                        sp.dma_start(o["v_p"], v_sb[:, 3, :]).then_inc(copy_s, 16)
                        sp.dma_start(o["v_s"][WIN - S:WIN, :], v_sb[0:S, 4, :]).then_inc(copy_s, 16)
                        sp.wait_ge(acs_s, 1)
                        sp.dma_start(scratch["acs"], acs[:]).then_inc(acs_out, 16)
                        for s in out_s:
                            sp.wait_ge(s, 96 + 32 * (NQ // 2))
                        sp.wait_ge(copy_s, 16 * (n_copy + 4))
                        load_attention(sp, at.in_s, S, at.q, scratch["qs"], scratch["ks"], scratch["vs"][0:WIN, :], scratch["vs"][WIN:WIN + S, :],
                                i["mask_k"][:, 0:KEYS].to_broadcast((P, KEYS)))
                        for n in range(NCH, NCH + RAW_SLOTS):
                            w.load(sp, n)
                        w.all_landed(sp)
                        sp.wait_ge(ada_in, 32)
                        sp.wait_ge(acs_out, 16)
                        at.store(sp, scratch["att"][:, :, S0:TW])
                        load_chunk(sp, next_in, 0)
                        sp.wait_ge(next_in, ATT_IN)
                        sp.wait_ge(at.out_s, 16)

                    @block.gpsimd
                    def _(pool):
                        pool.memset(zeros[:], 0.0).then_inc(init_s, 1)
                        pool.memset(raw[:, :, 0:LEAD], 0.0).then_inc(init_s, 1)
                        pool.memset(acs[:], 0.0).then_inc(init_s, 1)
                        pool.memset(edt[:], 0.0).then_inc(init_s, 1)
                        pool.memset(tok_all[:], 0.0).then_inc(init_s, 1)
                        for n in range(NCH + HL_AHEAD):
                            w.split_lo(pool, n)
                        w.all_split(pool)

                    @block.scalar
                    def _(act):
                        w.split_hi(act, 1)
                        for n in range(NCH):
                            w.split_hi(act, n + 2)
                            act.wait_ge(w.used, n + 1)
                            if n < QK:
                                if n >= 2:
                                    act.wait_ge(rope_s, n - 1)
                                act.activation(halves(qk[n % 2][:]), slot(n % 2), ACT.Copy).then_inc(evac_s, 1)
                            elif n == DT:
                                act.wait_ge(in_s, 96)
                                act.activation(halves(dt_v[:]), psum[0:32, 2 * (n % 2):2 * (n % 2) + 2, 0:HW], ACT.Identity,
                                               bias=dt_par[:, 0:1]).then_inc(evac_s, 1)
                                act.activation(a_exp[:], dt_par[:, 1:2], ACT.Exp).then_inc(e_s, 1)
                                act.wait_ge(dtp_s, 1)
                                act.activation(dt_e[:], dt_n[:], ACT.Exp).then_inc(e_s, 1)
                                act.wait_ge(e_s, 2)
                                act.activation(dt_l[:], dt_e[:], ACT.Ln, bias=one_c[0:32]).then_inc(e_s, 1)
                            elif n < G0:
                                j = n - V0
                                b = 2 * (n % 2)
                                act.activation(v_sb[:, 0:4, j * P:(j + 1) * P],
                                               psum[:, b, :].rearrange("p (a c) -> p a c", a=4), ACT.Copy)
                                act.activation(v_sb[0:S, 4, j * P:(j + 1) * P], psum[0:S, b + 1, 0:P], ACT.Copy).then_inc(evac_s, 1)
                            else:
                                if n == G0:
                                    act.wait_ge(acs_s, 1)
                                    for ci, (c0, L) in enumerate(SCAN):
                                        act.activation(edt[:, c0:c0 + L], acs[:, c0:c0 + L], ACT.Exp, scale=-1.0,
                                                       bias=acs[:, c0 + L - 1:c0 + L]).then_inc(sc_s, 1)
                                    act.wait_ge(init_s, 5)
                                act.activation(halves(raw[:, n - G0, LEAD:]), slot(n % 2), ACT.Copy).then_inc(evac_s, 1)
                                if n == AT + 1:
                                    at.exps(act)
                                    for kv in range(KV):
                                        at.evac_turned(act, kv)
                                    at.evac_out(act)

                    @block.vector
                    def _(dve):
                        link = chain(dve_s)
                        dve.wait_ge(in_s, 96)
                        for n in range(QK):
                            dve.wait_ge(evac_s, n + 1)
                            if n >= 2:
                                dve.wait_ge(out_s[n % 2], 96 + 32 * ((n - 2) // 2))
                            link(dve, dve.tensor_tensor(t_cos[n % 2][:], qk[n % 2][:], cos[:], ALU.mult))
                            dve.wait_ge(rot_s, n + 1)
                            link(dve, dve.tensor_tensor(halves(qk_rot[n % 2][:]), slot(2 + n % 2), halves(sin[:]), ALU.mult))
                            dve.tensor_tensor(qk_rot[n % 2][:], qk_rot[n % 2][:], t_cos[n % 2][:], ALU.add).then_inc(rope_s, 1)
                        dve.wait_ge(evac_s, DT + 1)
                        dve.scalar_tensor_tensor(out=dt_n[:], in0=dt_v[:], scalar=-1.0, in1=dt_v[:], op0=ALU.mult,
                                                 op1=ALU.min).then_inc(dtp_s, 1)
                        dve.wait_ge(e_s, 3)
                        dve.wait_ge(init_s, 5)
                        link(dve, dve.scalar_tensor_tensor(out=dt[:], in0=dt_v[:], scalar=0.0, in1=dt_l[:], op0=ALU.max, op1=ALU.add))
                        link(dve, dve.tensor_scalar(da[:], dt[:], a_exp[:], -1.0, ALU.mult, ALU.mult))
                        for c0, L in SCAN:
                            ins = dve.tensor_tensor_scan(acs[:, c0:c0 + L], ones[0:32, 0:L], da[:, c0:c0 + L], 0.0,
                                                         ALU.mult, ALU.add)
                        ins.then_inc(acs_s, 1)
                        dve.wait_ge(sc_s, 5)
                        dve.tensor_scalar(nacs[:], acs[:], -1.0, None, ALU.mult).then_inc(sc_s, 1)
                        dve.wait_ge(tr_s, 1)
                        for ci, (c0, L) in enumerate(SCAN):
                            ins = dve.tensor_copy(tok_all[0:L, :, ci, :, :],
                                            psum[0:L, 7, 96 * ci:96 * ci + 96].rearrange("p (a g r) -> p g a r", a=3, g=GROUPS))
                        ins.then_inc(tok_s, 1)
                        for kv in range(KV):
                            at.evac_scores(dve, kv)
                        at.maxima(dve)
                        at.normalise(dve)

                    @block.tensor
                    def _(pe):
                        for n in range(NCH):
                            if n >= 2:
                                pe.wait_ge(evac_s, n - 1)
                            if V0 <= n < G0:
                                w.wait_split(pe, n)
                                wh, wl = w_hi[w.hl_slot(n)], w_lo[w.hl_slot(n)]
                                for a, (c0, L) in enumerate(SCAN):
                                    out = psum[0:L, 2 * (n % 2) + a // 4, (a % 4) * P:(a % 4 + 1) * P]
                                    for k in range(KB):
                                        xh, xl = hp_hi[:, k, c0:c0 + L], hp_lo[:, k, c0:c0 + L]
                                        for j, (p, q) in enumerate(((xh, wh), (xl, wh), (xh, wl))):
                                            mm = pe.matmul(out, p, q[:, k, :], start=k == 0 and j == 0, stop=k == KB - 1 and j == 2)
                                mm.then_inc(w.used, 1)
                                w.block += KB
                            else:
                                for k in range(KB):
                                    w.multiply(pe, slot(n % 2), hp_hi[:, k, :], hp_lo[:, k, :], k == 0, k == KB - 1)
                                    if n == AT + 1 and k == 1:
                                        pe.wait_ge(tok_s, 1)
                                    if n == AT + 1 and k in (1, 3):
                                        for kv in (k - 1, k):
                                            at.scores(pe, kv)
                                    if n == AT + 2:
                                        if k % 2:
                                            at.values(pe, k // 2)
                                        else:
                                            at.turn(pe, k // 2)
                            if 1 <= n <= QK:
                                j = n - 1
                                if j == 0:
                                    pe.wait_ge(in_s, 96)
                                pe.wait_ge(evac_s, j + 1)
                                if j >= 2:
                                    pe.wait_ge(rope_s, j - 1)
                                for hh in range(2):
                                    mm = pe.matmul(psum[:, 4 + 2 * (j % 2) + hh, 0:HW], rot[:], qk[j % 2][:, hh * HW:(hh + 1) * HW],
                                                   start=True, stop=True)
                                mm.then_inc(rot_s, 1)
                            if n == AT:
                                pe.wait_ge(sc_s, 6)
                                pe.wait_ge(rope_s, QK)
                                for ci, (c0, L) in enumerate(SCAN):
                                    for a, src in enumerate((dt, edt, nacs)):
                                        mm = pe.transpose(psum[0:L, 7, 96 * ci + 32 * a:96 * ci + 32 * a + 32],
                                                          src[:, c0:c0 + L], ident[0:32, 0:32])
                                mm.then_inc(tr_s, 1)

            with ExitStack() as st:
                gp = sb(st, "gp", [P, GP_N])
                tok = sb(st, "tok", [P, 5, 3, HPG])
                cv = sb(st, "cv", [P, GT, TW])
                th = [sb(st, f"th{n}", [P, TW]) for n in range(2)]
                acs_b = sb(st, "acs_b", [P, HPG, TW])
                e_b = sb(st, "e_b", [P, HPG, TW])
                c_s_ = sb(st, "c_dec", [P, HPG, TW])
                xdt = [sb(st, f"xdt{n}", [P, HPG, HD]) for n in range(2)]
                xt = [sb(st, f"xt{n}", [P, HPG, HD]) for n in range(2)]
                bt = [sb(st, f"bt{n}", [P, NS]) for n in range(2)]
                cbm = [sb(st, f"cbm{n}", [P, P]) for n in range(2)]
                dec = [sb(st, f"dec{n}", [P, HPG, P]) for n in range(2)]
                y = sb(st, "y", [P, 2, TW])
                h_p = sb(st, "h_p", [P, HPG, HD])
                h_s0 = sb(st, "h_s0", [P, HPG, HD])
                names = ("g_in g_par g_conv g_th g_silu g_eb g_cdec g_tr g_cb g_xd g_bt g_w g_xt g_dif g_dece g_y g_ds g_ye g_h"
                         " g_tile g_evac g_yout g_out g_acs g_dve g_h0 g_cbe g_conv_out g_ctx")
                handles = sems(st, names)
                (h_in, par_s, conv_s, th_s, silu_s, eb_s, cdec_s, tr_s, cb_s, xd_s, bt_s, w_s, xt_s, dif_s, dece_s, y_s, ds_s,
                 ye_s, hst_s, tile_s, evac_s, yout_s, gout_s, acsb_s, dve_s, h0_s, cbe_s, cout_s, ctx_s) = handles
                w = Stream(st, "g", [None] * GT, NCH, True, [None] * RAW_SLOTS)
                assert GT % RAW_SLOTS == 0 and GT % HL_SLOTS == 0
                at = Attention(st, "g", CH, True, q_loop, True)
                nums = sorted(s.num for s in handles + w.all + at.all)
                assert nums == list(range(nums[0], nums[-1] + 1))
                sem_range = range(nums[0], nums[-1] + 1)
                NC5 = len(SCAN)

                def group(g):
                    w.src = [group_chunk(GT + n + g * GT) for n in range(GT + RAW_SLOTS)]
                    w.block = 0
                    with nc.Block(no_gpsimd_drain=True) as block:
                        @block.sync
                        def _(sp):
                            for n in range(RAW_SLOTS, RAW_SLOTS + HL_SLOTS):
                                w.load(sp, n)
                            sp.wait_ge(ctx_s, 1)
                            sp.dma_start(acs_b[:], scratch["acs"][bass.ds(g * HPG, HPG), :].unsqueeze(0)
                                         .to_broadcast((P, HPG, TW))).then_inc(acsb_s, 16)
                            sp.dma_start(h_s0[:].rearrange("p a b -> p (a b)"), i["state"][bass.ds(g * P, P), :]).then_inc(h0_s, 16)
                            sp.dma_start(o["conv_p"][bass.ds(g * P, P), :], raw_last(T)).then_inc(cout_s, 16)
                            sp.dma_start(o["conv_s"][bass.ds(g * P, P), :], raw_last(TW)).then_inc(cout_s, 16)
                            w.load(sp, RAW_SLOTS + HL_SLOTS)
                            at.store(sp, scratch["att"][:, :, bass.ds(g * CH, CH)])
                            load_chunk(sp, at.in_s, g + 1)
                            for n in range(GT, GT + RAW_SLOTS):
                                w.load(sp, n)
                            sp.wait_ge(hst_s, 4)
                            sp.dma_start(o["ssm_p"][bass.ds(g * P, P), :], h_p[:].rearrange("p a b -> p (a b)")).then_inc(gout_s, 16)
                            sp.wait_ge(hst_s, 5)
                            sp.dma_start(o["ssm_s"][bass.ds(g * P, P), :], h_s0[:].rearrange("p a b -> p (a b)")).then_inc(gout_s, 16)
                            sp.wait_ge(yout_s, 1)
                            sp.dma_start(scratch["y"][bass.ds(g * P, P), :], y[:].rearrange("p a b -> p (a b)")).then_inc(gout_s, 16)
                            w.all_landed(sp)
                            sp.wait_ge(at.in_s, ATT_IN)
                            sp.wait_ge(gout_s, 48)
                            sp.wait_ge(cout_s, 32)
                            sp.wait_ge(at.out_s, 16)

                        @block.gpsimd
                        def _(pool):
                            pool.tensor_copy(gp[:], gp_all[:, bass.ds(g, 1), :].rearrange("p a b -> p (a b)")).then_inc(par_s, 1)
                            pool.tensor_copy(tok[:].rearrange("p a b c -> p (a b c)"),
                                             tok_all[:, bass.ds(g, 1)].rearrange("p g a b c -> p (g a b c)")).then_inc(par_s, 1)
                            w.split_lo(pool, 1)
                            w.split_lo(pool, 2)
                            pool.wait_ge(eb_s, 1)
                            pool.wait_ge(silu_s, 2)
                            for r in range(HPG):
                                pool.tensor_tensor(c_s_[:, r, :], e_b[:, r, :], cv[:, 1, :], ALU.mult).then_inc(cdec_s, 1)

                            def end_weighted(c):
                                L, b = SCAN[c][1], c % 2
                                pool.wait_ge(xd_s, c + 1)
                                if c >= 2:
                                    pool.wait_ge(ds_s, c - 1)
                                pool.tensor_tensor(xt[b][0:L], xdt[b][0:L], bcast_mid(tok[0:L, c, 1, :], HD),
                                                   ALU.mult).then_inc(xt_s, 1)

                            w.split_lo(pool, 3)
                            w.split_lo(pool, 4)
                            end_weighted(0)
                            end_weighted(1)
                            w.split_lo(pool, 5)
                            end_weighted(2)
                            end_weighted(3)
                            end_weighted(4)
                            for n in range(GT, GT + HL_AHEAD):
                                w.split_lo(pool, n)
                            w.all_split(pool)

                        @block.scalar
                        def _(act):
                            def tanh(t):
                                act.wait_ge(conv_s, min(t, 3) + 1)
                                if t >= 2:
                                    act.wait_ge(silu_s, t - 1)
                                if t < 4:
                                    act.activation(th[t % 2][:], cv[:, t, :], ACT.Tanh).then_inc(th_s, 1)
                                else:
                                    act.activation(th[t % 2][:], raw[:, t, LEAD:], ACT.Tanh, scale=0.5).then_inc(th_s, 1)

                            def evac(t):
                                act.wait_ge(w.used, t + 1)
                                if t < 4:
                                    act.wait_ge(conv_s, t + 1)
                                    act.wait_ge(cout_s, 32)
                                else:
                                    act.wait_ge(silu_s, t + 1)
                                act.activation(halves(raw[:, t, LEAD:]), slot(t % 2), ACT.Copy).then_inc(evac_s, 1)

                            def scan_exp(c):
                                L = SCAN[c][1]
                                b = c % 2
                                act.wait_ge(dif_s, c + 1)
                                act.activation(dec[b][0:L, :, 0:L], dec[b][0:L, :, 0:L], ACT.Exp).then_inc(dece_s, 1)
                                act.wait_ge(tr_s, c + 1)
                                act.activation(bt[b][0:L, :], psum[0:L, 5, 0:P], ACT.Copy).then_inc(bt_s, 1)

                            w.split_hi(act, 1)
                            tanh(0)
                            w.split_hi(act, 2)
                            at.exps(act)
                            evac(0)
                            tanh(1)
                            act.wait_ge(acsb_s, 16)
                            act.activation(e_b[:], acs_b[:], ACT.Exp).then_inc(eb_s, 1)
                            tanh(2)
                            w.split_hi(act, 3)
                            evac(1)
                            for kv in range(KV):
                                at.evac_turned(act, kv)
                            at.evac_out(act)
                            tanh(3)
                            tanh(4)
                            tanh(5)
                            w.split_hi(act, 4)
                            evac(2)
                            scan_exp(0)
                            scan_exp(1)
                            scan_exp(2)
                            w.split_hi(act, 5)
                            evac(3)
                            scan_exp(3)
                            scan_exp(4)
                            w.split_hi(act, GT)
                            evac(4)
                            evac(5)

                        @block.vector
                        def _(dve):
                            link = chain(dve_s)

                            def conv(t):
                                link(dve, dve.tensor_scalar(cv[:, t, :], raw[:, t, 1:1 + TW], gp[:, GP_W + 4 * t:GP_W + 4 * t + 1],
                                                            gp[:, GP_B + t:GP_B + t + 1], ALU.mult, ALU.add))
                                for k in range(1, TAPS):
                                    ins = dve.scalar_tensor_tensor(
                                        out=cv[:, t, :], in0=raw[:, t, 1 + k:1 + k + TW],
                                        scalar=gp[:, GP_W + 4 * t + k:GP_W + 4 * t + k + 1], in1=cv[:, t, :],
                                        op0=ALU.mult, op1=ALU.add)
                                    if k < TAPS - 1:
                                        link(dve, ins)
                                ins.then_inc(conv_s, 1)

                            def silu(t):
                                dve.wait_ge(th_s, t + 1)
                                src = cv[:, t, :] if t < 4 else raw[:, t, LEAD:]
                                dve.scalar_tensor_tensor(out=cv[:, t, :], in0=th[t % 2][:], scalar=1.0, in1=src,
                                                         op0=ALU.add, op1=ALU.mult).then_inc(silu_s, 1)

                            def weights(c):
                                c0, L = SCAN[c]
                                b = c % 2
                                if c >= 2:
                                    dve.wait_ge(ds_s, c - 1)
                                for r in range(HPG):
                                    ins = dve.tensor_scalar(dec[b][0:L, r, 0:L], acs_b[0:L, r, c0:c0 + L],
                                                            tok[0:L, c, 2, r:r + 1], 0.0, ALU.add, ALU.min)
                                ins.then_inc(dif_s, 1)
                                dve.wait_ge(cb_s, c + 1)
                                dve.tensor_tensor(xdt[b][0:L], psum[0:L, 4, 0:2 * P].rearrange("p (r d) -> p r d", r=HPG),
                                                  bcast_mid(tok[0:L, c, 0, :], HD), ALU.mult).then_inc(xd_s, 1)
                                dve.tensor_tensor(cbm[b][0:L, 0:L], psum[0:L, 4, 2 * P:2 * P + L], mask_u[0:L, 0:L],
                                                  ALU.mult).then_inc(cbe_s, 1)
                                dve.wait_ge(cbe_s, c + 1)
                                dve.wait_ge(dece_s, c + 1)
                                dve.tensor_tensor(dec[b][0:L, :, 0:L], dec[b][0:L, :, 0:L],
                                                  cbm[b][0:L, 0:L].unsqueeze(1).to_broadcast((L, HPG, L)), ALU.mult).then_inc(w_s, 1)

                            def outputs(c):
                                c0, L = SCAN[c]
                                dve.wait_ge(y_s, c + 1)
                                for t in range(2):
                                    ins = dve.scalar_tensor_tensor(out=y[:, t, c0:c0 + L], in0=cv[:, 2 + t, c0:c0 + L],
                                                             scalar=gp[:, GP_D + t:GP_D + t + 1],
                                                             in1=psum[:, 6, t * P:t * P + L], op0=ALU.mult, op1=ALU.add)
                                ins.then_inc(ye_s, 1)
                                dve.wait_ge(ds_s, c + 1)
                                d_s = psum[:, 7, 0:256].rearrange("p (r d) -> p r d", r=HPG)
                                if c == 0:
                                    dve.tensor_copy(h_p[:], d_s).then_inc(hst_s, 1)
                                    return
                                h_ = h_p if c < 4 else h_s0
                                link(dve, dve.tensor_tensor(h_[:], h_[:], e_b[:, :, c0 + L - 1:c0 + L].to_broadcast((P, HPG, HD)), ALU.mult))
                                dve.tensor_tensor(h_[:], h_[:], d_s, ALU.add).then_inc(hst_s, 1)

                            dve.wait_ge(par_s, 2)
                            dve.tensor_copy(raw[:, 0:4, LEAD + S0 - 3:LEAD + S0],
                                            gp[:, GP_CTX:GP_CTX + 12].rearrange("p (a b) -> p a b", a=4)).then_inc(ctx_s, 1)
                            dve.wait_ge(ctx_s, 1)
                            at.evac_scores(dve, 0)
                            at.evac_scores(dve, 1)
                            conv(0)
                            at.evac_scores(dve, 2)
                            at.evac_scores(dve, 3)
                            at.maxima(dve)
                            conv(1)
                            silu(0)
                            conv(2)
                            at.normalise(dve)
                            silu(1)
                            conv(3)
                            silu(2)
                            silu(3)
                            silu(4)
                            dve.wait_ge(eb_s, 1)
                            weights(0)
                            silu(5)
                            weights(1)
                            outputs(0)
                            dve.memset(y[:, :, T:S0], 0.0)
                            for c in range(1, NC5):
                                if c + 1 < NC5:
                                    weights(c + 1)
                                if c == 4:
                                    dve.wait_ge(h0_s, 16)
                                outputs(c)
                            dve.wait_ge(ye_s, NC5)
                            dve.wait_ge(silu_s, 6)
                            dve.scalar_tensor_tensor(out=y[:], in0=y[:], scalar=0.5, in1=cv[:, 4:6, :], op0=ALU.mult,
                                                     op1=ALU.mult).then_inc(yout_s, 1)

                        @block.tensor
                        def _(pe):
                            steps = iter(range(GT * KB))

                            def fill(n):
                                for _ in range(n):
                                    u = next(steps, None)
                                    if u is None:
                                        return
                                    t, k = divmod(u, KB)
                                    if k == 0 and t >= 2:
                                        pe.wait_ge(evac_s, t - 1)
                                    w.multiply(pe, slot(t % 2), hp_hi[:, k, :], hp_lo[:, k, :], k == 0, k == KB - 1)

                            def turn_scores(c):
                                c0, L = SCAN[c]
                                if c == 0:
                                    pe.wait_ge(silu_s, 4)
                                    pe.wait_ge(at.oc_s, 1)
                                else:
                                    pe.wait_ge(xd_s, c)
                                    pe.wait_ge(bt_s, c)
                                    pe.wait_ge(cbe_s, c)
                                for t in range(2):
                                    pe.transpose(psum[0:L, 4, t * P:t * P + P], cv[:, 2 + t, c0:c0 + L], ident[:])
                                pe.matmul(psum[0:L, 4, 2 * P:2 * P + L], cv[:, 0, c0:c0 + L], cv[:, 1, c0:c0 + L], start=True,
                                          stop=True).then_inc(cb_s, 1)
                                pe.transpose(psum[0:L, 5, 0:P], cv[:, 0, c0:c0 + L], ident[:]).then_inc(tr_s, 1)

                            def scan(c):
                                c0, L = SCAN[c]
                                b = c % 2
                                pe.wait_ge(w_s, c + 1)
                                if c >= 1:
                                    pe.wait_ge(ye_s, c)
                                    pe.wait_ge(hst_s, c)
                                if c == 4:
                                    pe.wait_ge(h0_s, 16)
                                pe.wait_ge(cdec_s, HPG)
                                h_ = h_p if c < 4 else h_s0
                                for r in range(HPG):
                                    half, t = r % 2, r // 2
                                    out = psum[64 * half:64 * half + 64, 6, t * P:t * P + L]
                                    mm = pe.matmul(out, xdt[b][0:L, r, :], dec[b][0:L, r, 0:L], start=True, stop=c == 0)
                                    if c > 0:
                                        mm = pe.matmul(out, h_[:, r, :], c_s_[:, r, c0:c0 + L], start=False, stop=True)
                                mm.then_inc(y_s, 1)
                                pe.wait_ge(bt_s, c + 1)
                                pe.wait_ge(xt_s, c + 1)
                                pe.matmul(psum[:, 7, 0:256], bt[b][0:L, :], xt[b][0:L].rearrange("p r d -> p (r d)"),
                                          start=True, stop=True).then_inc(ds_s, 1)

                            at.scores(pe, 0)
                            at.scores(pe, 1)
                            fill(3)
                            at.scores(pe, 2)
                            at.scores(pe, 3)
                            fill(14)
                            at.turn(pe, 0)
                            for kv in range(KV):
                                if kv + 1 < KV:
                                    at.turn(pe, kv + 1)
                                fill(1)
                                at.values(pe, kv)
                            fill(5)
                            turn_scores(0)
                            fill(2)
                            for c in range(NC5):
                                if c + 1 < NC5:
                                    turn_scores(c + 1)
                                fill(2)
                                scan(c)
                            fill(GT * KB)
                    nc.all_engine_barrier(sems_to_clear=sem_range)

                def raw_last(end):
                    return raw[:, 0:4, LEAD + end - 3:LEAD + end]

                nc.all_engine_barrier(sems_to_clear=range(first_sem, sem_range.stop))
                with nc.Block(no_gpsimd_drain=True) as block:
                    @block.vector
                    def _(dve):
                        dve.tensor_scalar(gp_all[:, :, 0:GP_CTX], gp_all[:, :, 0:GP_CTX], 0.5, None, ALU.mult).then_inc(dve_s, 1)
                        dve.wait_ge(dve_s, 1)
                nc.all_engine_barrier(sems_to_clear=sem_range)
                with nc.Fori(0, GROUPS) as g:
                    group(g)

            hq_st = ExitStack()
            hq_hi = sb(hq_st, "hq_hi", [P, KB, TW], F32R, side="right")
            hq_lo = sb(hq_st, "hq_lo", [P, KB, TW], F32R, side="right")
            with ExitStack() as st:
                AT_IN = 4
                al = [sb(st, f"al{n}", [P, TW]) for n in range(AT_IN)]
                gate_out, ahi_s, alo_s, row_done, row_s, turn_s, bias_s = sems(st, "p_gate_out p_ahi p_alo p_rowdone p_row p_turn p_bias")
                in_att = sems(st, " ".join(f"p_att{n}" for n in range(AT_IN)))
                with nc.Block(no_gpsimd_drain=True) as block:
                    @block.sync
                    def _(sp):
                        for t in range(KB):
                            if t >= AT_IN:
                                sp.wait_ge(alo_s, t - AT_IN + 1)
                            sp.dma_start(al[t % AT_IN][:], scratch["att"][:, t, :]).then_inc(in_att[t % AT_IN], 16)
                            if t == AT_IN - 1:
                                sp.dma_start(scratch["gate"], raw[:, :, LEAD:]).then_inc(gate_out, 16)
                        sp.wait_ge(gate_out, 16)

                    @block.scalar
                    def _(act):
                        for t in range(KB):
                            act.wait_ge(in_att[t % AT_IN], 16 * (t // AT_IN + 1))
                            act.activation(hq_hi[:, t, :], al[t % AT_IN][:], ACT.Copy).then_inc(ahi_s, 1)
                        for n in range(2):
                            act.wait_ge(row_done, n + 1)
                            act.activation(late_row[:, n, :], psum[0:2, n, :], ACT.Copy).then_inc(row_s, 1)

                    @block.vector
                    def _(dve):
                        for t in range(KB):
                            dve.wait_ge(ahi_s, t + 1)
                            dve.tensor_tensor(hq_lo[:, t, :], al[t % AT_IN][:], hq_hi[:, t, :].bitcast(F32), ALU.subtract).then_inc(alo_s, 1)
                        dve.wait_ge(turn_s, 1)
                        add_bias(dve, 2 * KB, 2 * KB, 2).then_inc(bias_s, 1)
                        dve.wait_ge(bias_s, 1)
                        dve.tensor_tensor(gate[:, 0], mod[:, 2 * KB:3 * KB, :], bcast_mid(vecs[:, 1, :], 2), ALU.mult).then_inc(bias_s, 1)

                    @block.tensor
                    def _(pe):
                        for n in range(2):
                            modulation(pe, psum[0:2, n, :], ada_g1[n]).then_inc(row_done, 1)
                        for n in (2, 3, 0, 1):
                            if n < 2:
                                pe.wait_ge(row_s, n + 1)
                            mm = turn_rows(pe, 2, 8 * n, late_row[:, n, :])
                        mm.then_inc(turn_s, 1)

        late_st.close()

        with ExitStack() as st:
            mrg = sb(st, "mrg", [P, KB, TW])
            tmp = [sb(st, f"tmp{n}", [P, TW]) for n in range(3)]
            th = sb(st, "th", [P, TW])

            def norm_terms(act, src, dst, sem, scale, bank_slot):
                act.activation(halves(dst[:]), slot(bank_slot), ACT.Sqrt, bias=eps_c, scale=scale).then_inc(sem, 1)

            with ExitStack() as ms:
                wide_hi = sb(ms, "y_hi", [P, 16, TW], F32R)
                wide_lo = sb(ms, "y_lo", [P, 16, TW], F32R)
                yl = [sb(ms, f"yl{n}", [P, 2, TW]) for n in range(2)]
                ys = sb(ms, "ys", [P, TW])
                rs = sb(ms, "rs", [P, TW])
                snorm = sb(ms, "snorm", [P, 16])
                first_att = [m + max(m - GT + 1, 0) for m in range(KB)]
                N1 = first_att[-1] + 1
                src = []
                for m in range(KB):
                    src += ([i["w_gate"][8 + m]] if m >= GT else []) + [i["w_att"][m]]
                for m in range(KB):
                    src += [i["w_gate"][m], i["w_ssm"][2 * m], i["w_ssm"][2 * m + 1]]
                w = Stream(ms, "m", src, NCH + GROUPS * GT, True, [i["w_out"][n] for n in range(RAW_SLOTS)])
                (in_y0, in_y1, in_c, sq_s, ss_s, root_s, rec_s, yn_s, yhi_s, ylo_s, th_s, m_s, dve_s,
                 in_g0, in_g1) = sems(
                    ms, "m_y0 m_y1 m_c m_sq m_ss m_root m_rec m_yn m_yhi m_ylo m_th m_m m_dve"
                        " m_g0 m_g1")
                in_g = [in_g0, in_g1]
                in_y = [in_y0, in_y1]
                gl = [tmp[1], tmp[2]]
                with nc.Block(no_gpsimd_drain=True) as block:
                    @block.sync
                    def _(sp):
                        for m in range(2):
                            sp.dma_start(gl[m][:], scratch["gate"][:, m, :]).then_inc(in_g[m], 16)
                        sp.dma_start(snorm[:], i["ssm_norm"]).then_inc(in_c, 16)
                        for n in range(RAW_SLOTS, RAW_SLOTS + HL_SLOTS):
                            w.load(sp, n)
                        for g in range(2):
                            sp.dma_start(yl[g][:].rearrange("p a b -> p (a b)"), scratch["y"][g * P:(g + 1) * P, :]).then_inc(in_y[g % 2], 16)
                        n = RAW_SLOTS + HL_SLOTS
                        for g in range(2, GROUPS):
                            while n <= first_att[g] + 1:
                                w.load(sp, n)
                                n += 1
                            if g < GT:
                                sp.wait_ge(th_s, g - 1)
                                sp.dma_start(gl[g % 2][:], scratch["gate"][:, g, :]).then_inc(in_g[g % 2], 16)
                            sp.wait_ge(ylo_s, 2 * (g - 1))
                            sp.dma_start(yl[g % 2][:].rearrange("p a b -> p (a b)"), scratch["y"][g * P:(g + 1) * P, :]).then_inc(in_y[g % 2], 16)
                        while n < w.own + RAW_SLOTS:
                            w.load(sp, n)
                            n += 1
                        w.all_landed(sp)

                    @block.gpsimd
                    def _(pool):
                        for n in range(w.own + HL_AHEAD):
                            w.split_lo(pool, n)
                        w.all_split(pool)

                    @block.scalar
                    def _(act):
                        def gate_tanh(n, k, src):
                            if n is None:
                                act.wait_ge(in_g[k % 2], 16 * (k // 2 + 1))
                            else:
                                act.wait_ge(w.used, n + 1)
                            if k >= 1:
                                act.wait_ge(m_s, k)
                            act.activation(halves(th[:]), src, ACT.Tanh, scale=0.5).then_inc(th_s, 1)

                        def y_norm(g):
                            act.wait_ge(in_y[g % 2], 16 * (g // 2 + 1))
                            for t in range(2):
                                if t == 1 or g > 0:
                                    act.wait_ge(ss_s, 2 * g + t)
                                act.activation(ys[:], yl[g % 2][:, t, :], ACT.Square).then_inc(sq_s, 1)
                            act.wait_ge(ss_s, 2 * g + 2)
                            if g >= 1:
                                act.wait_ge(yn_s, 2 * g)
                            norm_terms(act, None, rs, root_s, 1.0 / 256, 3)
                            for t in range(2):
                                act.wait_ge(yn_s, 2 * g + t + 1)
                                act.activation(wide_hi[:, 2 * g + t, :], yl[g % 2][:, t, :], ACT.Copy).then_inc(yhi_s, 1)

                        w.split_hi(act, 1)
                        for m in range(KB):
                            n = first_att[m]
                            if m >= GT:
                                w.split_hi(act, n + 1)
                                gate_tanh(n - 1, m, slot(0))
                            else:
                                gate_tanh(None, m, halves(gl[m % 2][:]))
                            w.split_hi(act, n + 2)
                            y_norm(m)
                        for n in range(24):
                            w.split_hi(act, N1 + n + 2)
                            if n % 3 == 0:
                                gate_tanh(N1 + n, 8 + n // 3, slot(2))

                    @block.vector
                    def _(dve):
                        link = chain(dve_s)
                        dve.wait_ge(in_c, 16)
                        for m in range(KB):
                            dve.wait_ge(th_s, m + 1)
                            dve.wait_ge(w.used, first_att[m] + 1)
                            dve.scalar_tensor_tensor(out=halves(mrg[:, m, :]), in0=halves(th[:]), scalar=1.0, in1=slot(1),
                                                     op0=ALU.add, op1=ALU.mult).then_inc(m_s, 1)
                            dve.wait_ge(root_s, m + 1)
                            link(dve, dve.reciprocal(rs[:], rs[:]))
                            for t in range(2):
                                dve.scalar_tensor_tensor(out=yl[m % 2][:, t, :], in0=yl[m % 2][:, t, :],
                                                         scalar=snorm[:, 2 * m + t:2 * m + t + 1], in1=rs[:], op0=ALU.mult,
                                                         op1=ALU.mult).then_inc(yn_s, 1)
                            for t in range(2):
                                dve.wait_ge(yhi_s, 2 * m + t + 1)
                                dve.tensor_tensor(wide_lo[:, 2 * m + t, :], yl[m % 2][:, t, :],
                                                  wide_hi[:, 2 * m + t, :].bitcast(F32), ALU.subtract).then_inc(ylo_s, 1)
                        for m in range(KB):
                            dve.wait_ge(th_s, 8 + m + 1)
                            dve.wait_ge(w.used, N1 + 3 * m + 3)
                            link(dve, dve.scalar_tensor_tensor(out=halves(tmp[0][:]), in0=halves(th[:]), scalar=1.0, in1=slot(m % 2),
                                                               op0=ALU.add, op1=ALU.mult))
                            dve.tensor_tensor(mrg[:, m, :], mrg[:, m, :], tmp[0][:], ALU.add).then_inc(m_s, 1)
                            dve.wait_ge(m_s, 8 + m + 1)

                    @block.tensor
                    def _(pe):
                        def tile(s, hi, lo, k0=0, nk=KB):
                            for k in range(k0, k0 + KB):
                                w.multiply(pe, slot(s), hi[:, k, :], lo[:, k, :], k == 0, k == nk - 1)

                        for m in range(KB):
                            if m >= GT:
                                pe.wait_ge(th_s, m)
                                tile(0, hp_hi, hp_lo)
                            if m >= 1:
                                pe.wait_ge(m_s, m)
                            tile(1, hq_hi, hq_lo)
                            for t in range(2):
                                if m >= 1 and t == 0:
                                    pe.wait_ge(root_s, m)
                                pe.wait_ge(sq_s, 2 * m + t + 1)
                                for hh in range(2):
                                    mm = pe.matmul(psum[:, 6 + hh, 0:HW], ones[:], ys[:, hh * HW:(hh + 1) * HW], start=t == 0, stop=t == 1)
                                mm.then_inc(ss_s, 1)
                        for m in range(KB):
                            if m >= 1:
                                pe.wait_ge(th_s, 8 + m)
                            tile(2, hp_hi, hp_lo)
                            if m == 0:
                                pe.wait_ge(ylo_s, 16)
                                pe.wait_ge(m_s, KB)
                            elif m >= 2:
                                pe.wait_ge(m_s, KB + m - 1)
                            tile(m % 2, wide_hi, wide_lo, 0, 16)
                            tile(m % 2, wide_hi, wide_lo, 8, 16)

            with ExitStack() as ms:
                ada = [sb(ms, f"ada_o{n}", [P, KB, ADA_W]) for n in range(4)]
                mod_row = sb(ms, "mod_row_o", [2, 2, ADA_W])
                sq = [sb(ms, f"osq{n}", [P, TW]) for n in range(2)]
                rs = [sb(ms, f"ors{n}", [P, TW]) for n in range(2)]
                xl = [*(sb(ms, f"xl{n}", [P, TW]) for n in range(2)), th]
                w = Stream(ms, "o", [i["w_out"][m] for m in range(KB)], w.base + w.own, True,
                           [i["w_ffn_in"][n] for n in range(RAW_SLOTS)])
                (hi_s, lo_s, ev_s, sq_s, ss_s, root_s, x_in0, x_in1, x_in2, x_s, h_s, hhi_s, dve_s, hlo_s) = sems(
                    ms, "o_hi_s o_lo_s o_ev o_sq o_ss o_root o_xin0 o_xin1 o_xin2 o_x o_h o_hhi o_dve o_hlo")
                x_in = [x_in0, x_in1, x_in2]
                in_ada = sems(ms, " ".join(f"o_ada{n}" for n in range(4)))
                row_done, row_s, turn_s = sems(ms, "o_rowdone o_row o_turn")
                with nc.Block(no_gpsimd_drain=True) as block:
                    @block.sync
                    def _(sp):
                        for n in range(RAW_SLOTS, RAW_SLOTS + HL_SLOTS):
                            w.load(sp, n)
                        for t in range(3):
                            sp.dma_start(xl[t][:], i["x"][:, t, :]).then_inc(x_in[t % 3], 16)
                        for n in range(RAW_SLOTS + HL_SLOTS, KB + RAW_SLOTS):
                            w.load(sp, n)
                            a = n - RAW_SLOTS - HL_SLOTS
                            if a < 4:
                                sp.dma_start(ada[a][:], i["w_ada"][SCALE2 + a]).then_inc(in_ada[a], 16)
                        for t in range(3, KB):
                            sp.wait_ge(x_s, t - 2)
                            sp.dma_start(xl[t % 3][:], i["x"][:, t, :]).then_inc(x_in[t % 3], 16)
                        w.all_landed(sp)

                    @block.gpsimd
                    def _(pool):
                        for n in range(KB + HL_AHEAD):
                            w.split_lo(pool, n)
                        for t in range(KB):
                            pool.wait_ge(hhi_s, t + 1)
                            pool.tensor_tensor(hq_lo[:, t, :], tmp[t % 3][:], hq_hi[:, t, :].bitcast(F32), ALU.subtract).then_inc(hlo_s, 1)
                        w.all_split(pool)
                        pool.wait_ge(hlo_s, KB)

                    @block.scalar
                    def _(act):
                        def square(t, count):
                            if count >= 2:
                                act.wait_ge(ss_s, count - 1)
                            act.activation(sq[count % 2][:], mrg[:, t, :], ACT.Square).then_inc(sq_s, 1)

                        w.split_hi(act, 1)
                        for t in range(KB):
                            act.activation(hp_hi[:, t, :], mrg[:, t, :], ACT.Copy, scale=0.5).then_inc(hi_s, 1)
                        for n in range(KB):
                            w.split_hi(act, n + 2)
                            act.wait_ge(w.used, n + 1)
                            act.activation(halves(mrg[:, n, :]), slot(n % 2), ACT.Copy).then_inc(ev_s, 1)
                            act.wait_ge(ev_s, n + 1)
                            square(n, n)
                        act.wait_ge(ss_s, KB)
                        norm_terms(act, None, rs[0], root_s, 1.0 / D, 3)
                        def row(a):
                            act.wait_ge(row_done, a + 1)
                            if a >= 2:
                                act.wait_ge(turn_s, 1)
                            act.activation(mod_row[:, a % 2, :], psum[0:2, a, :], ACT.Copy).then_inc(row_s, 1)

                        for t in range(KB):
                            act.wait_ge(x_s, t + 1)
                            square(t, KB + t)
                            if t == 1:
                                row(0)
                        row(1)
                        act.wait_ge(ss_s, 2 * KB)
                        norm_terms(act, None, rs[1], root_s, 1.0 / D, 2)
                        for t in range(KB):
                            act.wait_ge(h_s, t + 1)
                            act.activation(hq_hi[:, t, :], tmp[t % 3][:], ACT.Copy).then_inc(hhi_s, 1)
                        row(2)
                        row(3)

                    @block.vector
                    def _(dve):
                        link = chain(dve_s)
                        for t in range(KB):
                            dve.wait_ge(hi_s, t + 1)
                            dve.scalar_tensor_tensor(out=hp_lo[:, t, :], in0=mrg[:, t, :], scalar=0.5, in1=hp_hi[:, t, :].bitcast(F32),
                                                     op0=ALU.mult, op1=ALU.subtract).then_inc(lo_s, 1)
                        dve.wait_ge(root_s, 1)
                        link(dve, dve.reciprocal(rs[0][:], rs[0][:]))
                        for t in range(KB):
                            link(dve, dve.tensor_tensor(mrg[:, t, :], mrg[:, t, :], rs[0][:], ALU.mult))
                            dve.wait_ge(x_in[t % 3], 16 * (t // 3 + 1))
                            for c0, L, g in RANGES:
                                ins = dve.scalar_tensor_tensor(out=mrg[:, t, c0:c0 + L], in0=mrg[:, t, c0:c0 + L],
                                                               scalar=gate[:, 0, t, g:g + 1], in1=xl[t % 3][:, c0:c0 + L],
                                                               op0=ALU.mult, op1=ALU.add)
                            ins.then_inc(x_s, 1)
                        dve.wait_ge(root_s, 2)
                        link(dve, dve.reciprocal(rs[1][:], rs[1][:]))
                        dve.wait_ge(turn_s, 1)
                        link(dve, add_bias(dve, 4 * KB, KB, 6))
                        link(dve, dve.scalar_tensor_tensor(out=gain[:, 1], in0=mod[:, 4 * KB:5 * KB, :], scalar=1.0,
                                                           in1=bcast_mid(vecs[:, 2, :], 2), op0=ALU.add, op1=ALU.mult))
                        for t in range(KB):
                            if t >= 3:
                                dve.wait_ge(hlo_s, t - 2)
                            link(dve, dve.tensor_tensor(tmp[t % 3][:], mrg[:, t, :], rs[1][:], ALU.mult))
                            for c0, L, g in RANGES:
                                ins = dve.tensor_scalar(tmp[t % 3][:, c0:c0 + L], tmp[t % 3][:, c0:c0 + L], gain[:, 1, t, g:g + 1],
                                                        mod[:, 24 + t, g:g + 1], ALU.mult, ALU.add)
                            ins.then_inc(h_s, 1)
                        dve.wait_ge(turn_s, 2)
                        link(dve, add_bias(dve, 5 * KB, KB, 7))
                        link(dve, dve.tensor_tensor(gate[:, 1], mod[:, 5 * KB:6 * KB, :], bcast_mid(vecs[:, 3, :], 2), ALU.mult))

                    @block.tensor
                    def _(pe):
                        def squares(t, count, s):
                            pe.wait_ge(sq_s, count + 1)
                            for hh in range(2):
                                mm = pe.matmul(psum[:, 2 * s + hh, 0:HW], ones[:], sq[count % 2][:, hh * HW:(hh + 1) * HW],
                                               start=t == 0, stop=t == KB - 1)
                            mm.then_inc(ss_s, 1)

                        for m in range(KB):
                            if m == 0:
                                pe.wait_ge(lo_s, KB)
                            if m >= 2:
                                pe.wait_ge(ev_s, m - 1)
                            for k in range(KB):
                                w.multiply(pe, slot(m % 2), hp_hi[:, k, :], hp_lo[:, k, :], k == 0, k == KB - 1)
                            if m >= 1:
                                squares(m - 1, m - 1, 3)
                        squares(KB - 1, KB - 1, 3)

                        def block_step(a, k):
                            if k == 0:
                                pe.wait_ge(in_ada[a], 16)
                            mm = pe.matmul(psum[0:2, a, :], c_silu[:, k, :], ada[a][:, k, :], start=k == 0, stop=k == KB - 1)
                            if k == KB - 1:
                                mm.then_inc(row_done, 1)

                        def turn(vector, bank):
                            for a in (2 * vector, 2 * vector + 1):
                                pe.wait_ge(row_s, a + 1)
                                mm = turn_rows(pe, bank, 8 * (a % 2), mod_row[:, a % 2, :])
                            mm.then_inc(turn_s, 1)

                        pe.wait_ge(ev_s, KB)
                        for k in range(KB):
                            block_step(0, k)
                        for t in range(KB):
                            block_step(1, t)
                            squares(t, KB + t, 2)
                        pe.wait_ge(root_s, 1)
                        turn(0, 6)
                        for a in (2, 3):
                            for k in range(KB):
                                block_step(a, k)
                        turn(1, 7)

            wide_hi = sb(st, "wide_hi", [P, FT - KB, TW], F32R)
            wide_lo = sb(st, "wide_lo", [P, FT - KB, TW], F32R)
            with ExitStack() as ms:
                fpar = sb(ms, "fpar", [P, FT, 6])
                fr = [sb(ms, f"fr{n}", [P, LEAD + TW]) for n in range(2)]
                fst = sb(ms, "fst", [P, FT, 4])
                cvf = [tmp[1], tmp[2]]
                w = Stream(ms, "f", [i["w_ffn_in"][n] for n in range(2 * FT)], w.base + w.own, True,
                           [i["w_ffn_out"][n] for n in range(RAW_SLOTS)])
                (in_s, par_s, fe_s, ctx_s, fcv_s, fth_s, fsl_s, ff_s, fhi_s, flo_s, fst_s, dve_s, z_s, o_s) = sems(
                    ms, "f_in f_par f_e f_ctx f_cv f_th f_sl f_f f_fhi f_flo f_st f_dve f_z f_o")
                sl = [sb(ms, f"fs{n}", [P, TW]) for n in range(2)]

                def wide(f, part):
                    return ((hp_hi, hp_lo)[part][:, f, :] if f < KB else (wide_hi, wide_lo)[part][:, f - KB, :])

                with nc.Block(no_gpsimd_drain=True) as block:
                    @block.sync
                    def _(sp):
                        sp.dma_start(fpar[:], i["fpar"]).then_inc(in_s, 16)
                        for n in range(2 * FT + RAW_SLOTS):
                            w.load(sp, n)
                        w.all_landed(sp)
                        sp.wait_ge(fst_s, 2 * FT)
                        sp.dma_start(o["ffn"], fst[:]).then_inc(o_s, 16)
                        sp.wait_ge(o_s, 16)

                    @block.gpsimd
                    def _(pool):
                        for n in range(2):
                            pool.memset(fr[n][:, 0:LEAD], 0.0).then_inc(z_s, 1)
                        for n in range(2 * FT + 2 * HL_AHEAD):
                            w.split_lo(pool, n)
                            f, up = divmod(n, 2)
                            if up and f < FT:
                                pool.wait_ge(fe_s, f + 1)
                                pool.tensor_copy(fst[:, f, 0:2], fr[f % 2][:, LEAD + T - 2:LEAD + T]).then_inc(fst_s, 1)
                                pool.tensor_copy(fst[:, f, 2:4], fr[f % 2][:, LEAD + TW - 2:LEAD + TW]).then_inc(fst_s, 1)
                        w.all_split(pool)

                    @block.scalar
                    def _(act):
                        w.split_hi(act, 1)
                        act.wait_ge(z_s, 2)

                        def round_hi(f):
                            act.wait_ge(ff_s, f + 1)
                            act.activation(wide(f, 0), sl[f % 2][:], ACT.Copy).then_inc(fhi_s, 1)

                        for n in range(2 * FT):
                            w.split_hi(act, n + 2)
                            f, up = divmod(n, 2)
                            if not up:
                                act.wait_ge(w.used, n + 1)
                                if f >= 2:
                                    act.wait_ge(fcv_s, f - 1)
                                    act.wait_ge(fst_s, 2 * (f - 1))
                                act.activation(halves(fr[f % 2][:, LEAD:]), slot(f % 2), ACT.Copy).then_inc(fe_s, 1)
                                if f >= 1:
                                    round_hi(f - 1)
                            else:
                                act.wait_ge(fcv_s, f + 1)
                                if f >= 1:
                                    act.wait_ge(fsl_s, f)
                                act.activation(th[:], cvf[f % 2][:], ACT.Tanh).then_inc(fth_s, 1)
                        round_hi(FT - 1)

                    @block.vector
                    def _(dve):
                        link = chain(dve_s)
                        dve.wait_ge(in_s, 16)
                        link(dve, dve.tensor_scalar(fpar[:, :, 0:4], fpar[:, :, 0:4], 0.5, None, ALU.mult))

                        def round_lo(f):
                            dve.wait_ge(fhi_s, f + 1)
                            dve.tensor_tensor(wide(f, 1), sl[f % 2][:], wide(f, 0).bitcast(F32), ALU.subtract).then_inc(flo_s, 1)

                        for f in range(FT):
                            dve.wait_ge(fe_s, f + 1)
                            r, c = fr[f % 2], cvf[f % 2]
                            link(dve, dve.tensor_copy(r[:, LEAD + S0 - 2:LEAD + S0], fpar[:, f, 4:6]))
                            link(dve, dve.tensor_scalar(c[:], r[:, 2:2 + TW], fpar[:, f, 0:1], fpar[:, f, 3:4], ALU.mult, ALU.add))
                            link(dve, dve.scalar_tensor_tensor(out=c[:], in0=r[:, 3:3 + TW], scalar=fpar[:, f, 1:2], in1=c[:],
                                                               op0=ALU.mult, op1=ALU.add))
                            dve.scalar_tensor_tensor(out=c[:], in0=r[:, 4:4 + TW], scalar=fpar[:, f, 2:3], in1=c[:],
                                                     op0=ALU.mult, op1=ALU.add).then_inc(fcv_s, 1)
                            if f >= 1:
                                round_lo(f - 1)
                            dve.wait_ge(fth_s, f + 1)
                            if f >= 2:
                                dve.wait_ge(flo_s, f - 1)
                            dve.scalar_tensor_tensor(out=sl[f % 2][:], in0=th[:], scalar=1.0, in1=c[:], op0=ALU.add,
                                                     op1=ALU.mult).then_inc(fsl_s, 1)
                            dve.wait_ge(fsl_s, f + 1)
                            dve.wait_ge(w.used, 2 * f + 2)
                            dve.tensor_tensor(halves(sl[f % 2][:]), halves(sl[f % 2][:]), slot(2 + f % 2), ALU.mult).then_inc(ff_s, 1)
                        round_lo(FT - 1)

                    @block.tensor
                    def _(pe):
                        for n in range(2 * FT):
                            f, up = divmod(n, 2)
                            if f >= 2:
                                if up:
                                    pe.wait_ge(ff_s, f - 1)
                                else:
                                    pe.wait_ge(fe_s, f - 1)
                            for k in range(KB):
                                w.multiply(pe, slot(2 * up + f % 2), hq_hi[:, k, :], hq_lo[:, k, :], k == 0, k == KB - 1)

            hq_st.close()
            with ExitStack() as ms:
                sq = [sb(ms, f"zsq{n}", [P, TW]) for n in range(2)]
                rs0 = sb(ms, "zrs", [P, TW])
                w = Stream(ms, "z", [i["w_ffn_out"][n] for n in range(FT)], w.base + w.own, True, [])
                ev_s, tile_s, sq_s, ss_s, root_s, y_s, dve_s, o_s = sems(ms, "z_ev z_tile z_sq z_ss z_root z_y z_dve z_o")
                fo = sb(ms, "fo", [P, KB, TW])
                with nc.Block(no_gpsimd_drain=True) as block:
                    @block.sync
                    def _(sp):
                        for n in range(FT):
                            w.load(sp, n)
                        for t in range(KB):
                            sp.wait_ge(y_s, t + 1)
                            sp.dma_start(o["y"][:, t, :], mrg[:, t, :]).then_inc(o_s, 16)
                        sp.wait_ge(o_s, 16 * KB)

                    @block.gpsimd
                    def _(pool):
                        for n in range(FT):
                            w.split_lo(pool, n)

                    @block.scalar
                    def _(act):
                        w.split_hi(act, 1)
                        n = 2
                        for m in range(KB):
                            while n < FT and (n - 2 + 1) * KB <= (m + 1) * FT:
                                w.split_hi(act, n)
                                n += 1
                            if (m + 1) * FT % KB == 0:
                                act.wait_ge(w.used, (m + 1) * FT // KB)
                            else:
                                act.wait_ge(tile_s, sum((j + 1) * FT % KB != 0 for j in range(m + 1)))
                            act.activation(halves(fo[:, m, :]), slot(m % 2), ACT.Copy).then_inc(ev_s, 1)
                            act.wait_ge(ev_s, m + 1)
                            if m >= 2:
                                act.wait_ge(ss_s, m - 1)
                            act.activation(sq[m % 2][:], fo[:, m, :], ACT.Square).then_inc(sq_s, 1)
                        act.wait_ge(ss_s, KB)
                        norm_terms(act, None, rs0, root_s, 1.0 / D, 3)

                    @block.vector
                    def _(dve):
                        link = chain(dve_s)
                        dve.wait_ge(root_s, 1)
                        link(dve, dve.reciprocal(rs0[:], rs0[:]))
                        for t in range(KB):
                            link(dve, dve.tensor_tensor(tmp[t % 2][:], fo[:, t, :], rs0[:], ALU.mult))
                            for c0, L, g in RANGES:
                                ins = dve.scalar_tensor_tensor(out=mrg[:, t, c0:c0 + L], in0=tmp[t % 2][:, c0:c0 + L],
                                                               scalar=gate[:, 1, t, g:g + 1], in1=mrg[:, t, c0:c0 + L],
                                                               op0=ALU.mult, op1=ALU.add)
                            ins.then_inc(y_s, 1)

                    @block.tensor
                    def _(pe):
                        def squares(t):
                            pe.wait_ge(sq_s, t + 1)
                            for hh in range(2):
                                mm = pe.matmul(psum[:, 6 + hh, 0:HW], ones[:], sq[t % 2][:, hh * HW:(hh + 1) * HW],
                                               start=t == 0, stop=t == KB - 1)
                            mm.then_inc(ss_s, 1)

                        for m in range(KB):
                            if m >= 2:
                                pe.wait_ge(ev_s, m - 1)
                            for k in range(FT):
                                w.multiply(pe, slot(m % 2), wide(k, 0), wide(k, 1), k == 0, k == FT - 1,
                                           tile_s if k == FT - 1 else None)
                            if m >= 1:
                                squares(m - 1)
                        squares(KB - 1)


def columns(v):
    v = np.asarray(v)
    v = v.reshape(v.shape[:-1] + (-1, P))
    return np.ascontiguousarray(np.moveaxis(v, -1, 0))


def chunks(m):
    k, n = m.shape[0] // D, m.shape[1] // P
    return np.ascontiguousarray(m.reshape(k, KB, P, n, P).transpose(3, 0, 2, 1, 4).reshape(n * k, P, D))


def kernel(**inputs):
    import concourse.bacc as bacc
    from concourse.bass_utils import run_bass_kernel_spmd

    a = {n: np.asarray(v) for n, v in inputs.items()}
    f32 = np.float32
    x = np.zeros((P, KB, TW), a["x_prompt"].dtype)
    x[:, :, 0:T] = a["x_prompt"][0].T.reshape(KB, P, T).transpose(1, 0, 2)
    x[:, :, S0:] = a["x_sample"][0].T.reshape(KB, P, S).transpose(1, 0, 2)
    c = np.stack([a["c_prompt"][0], a["c_sample"][0]], -1).reshape(KB, P, 2).transpose(1, 0, 2)

    w_in = a["w_in"][0]
    inner, conv_dim, n_heads = 2048, 4096, 32
    at = np.cumsum([0, inner, conv_dim, n_heads, 1024, 256, 256, 2048])
    w_z, w_xbc, w_dt, w_q, w_k, w_v, w_g = (w_in[:, at[j]:at[j + 1]] for j in range(7))
    w_dt = np.concatenate([w_dt, np.zeros((D, P - n_heads), w_dt.dtype)], 1)
    zc, xc = chunks(w_z), chunks(w_xbc)
    w_grp = np.concatenate([np.stack([xc[16 + g], xc[24 + g], xc[2 * g], xc[2 * g + 1], zc[2 * g], zc[2 * g + 1]])
                            for g in range(GROUPS)])
    gc = chunks(w_g)
    w_att = chunks(a["w_att_out"][0])
    w_grp = np.concatenate([w_grp, gc[8:8 + GT], w_att[0:RAW_SLOTS]]).reshape(-1, D)
    fi = chunks(a["w_ffn_in"][0])
    w_ffn_in = np.stack([fi[f + FT * u] for f in range(FT) for u in range(2)])
    fo = a["w_ffn_out"][0].reshape(FT, P, KB, P).transpose(2, 0, 1, 3).reshape(FT, KB, P, P)
    w_ffn_out = np.ascontiguousarray(fo.transpose(0, 2, 1, 3)).reshape(FT, P, D)
    ada = a["w_ada"][0].reshape(KB, P, 6 * D // ADA_W, ADA_W).transpose(2, 1, 0, 3)

    cw, cb, ctx = columns(a["ssm_conv_w"][0]), columns(a["ssm_conv_b"][0]), columns(a["state_conv"][0, 0])
    heads = a["ssm_d"][0].reshape(GROUPS, 2, 2)
    gp = np.zeros((P, GROUPS, GP_N), cw.dtype)
    for g in range(GROUPS):
        for j, t in enumerate((16 + g, 24 + g, 2 * g, 2 * g + 1)):
            gp[:, g, GP_W + TAPS * j:GP_W + TAPS * (j + 1)] = cw[:, :, t]
            gp[:, g, GP_B + j] = cb[:, t]
            gp[:, g, GP_CTX + 3 * j:GP_CTX + 3 * j + 3] = ctx[:, :, t]
        gp[:, g, GP_D:GP_D + 2] = np.repeat(heads[g], HD, axis=1).T
    fw, fb, fctx = columns(a["ffn_conv_w"][0]), columns(a["ffn_conv_b"][0]), columns(a["state_ffn_conv"][0, 0])
    fpar = np.concatenate([fw.transpose(0, 2, 1), fb[:, :, None], fctx.transpose(0, 2, 1)], 2)

    half, theta = 8, 500000.0
    pos = np.zeros(TW, f32)
    pos[0:T] = np.arange(T)
    pos[S0:] = 256 + np.arange(S)
    inv = (f32(theta) ** (-np.arange(half, dtype=f32) / f32(half))).astype(f32)
    ang = (pos[None, :] * inv[:, None]).astype(f32)
    cos, sin, rot = np.ones((P, TW), f32), np.zeros((P, TW), f32), np.zeros((P, P), f32)
    for b in (0, 64):
        for j in range(half):
            cos[b + j] = cos[b + half + j] = np.cos(ang[j])
            sin[b + j], sin[b + half + j] = -np.sin(ang[j]), np.sin(ang[j])
            rot[b + half + j, b + j] = rot[b + j, b + half + j] = 1.0

    mask_k = np.zeros((1, WIN + T + CH), f32)
    mask_k[0, 0:WIN] = np.finfo(f32).min
    sk = a["attn_sinks"][0].reshape(KV, 2, 2)
    sinks = np.repeat(sk.transpose(1, 0, 2).reshape(2, 2 * KV), CH, axis=0)
    sinks_s = np.concatenate([np.repeat(sk.transpose(1, 0, 2).reshape(2, 2 * KV), S, axis=0)] * 2, axis=0)
    state = a["state_ssm"][0, 0].reshape(GROUPS, HPG * HD, NS).transpose(0, 2, 1).reshape(GROUPS * P, HPG * HD)
    consts = np.zeros((P, 2), f32)
    consts[:, 0], consts[:, 1] = EPS, 1.0

    ins = dict(
        x=x, c=c, ident=np.eye(P, dtype=f32), consts=consts, mask_u=np.triu(np.ones((P, P), f32)),
        vecs=np.stack([columns(a[n][0]) for n in ("norm_mix_pre", "norm_mix_post", "norm_ffn_pre", "norm_ffn_post")], 1),
        b_ada=columns(a["b_ada"][0]), w_ada=ada, w_qkv=np.concatenate([chunks(w_k), chunks(w_q), chunks(w_dt), chunks(w_v)]),
        w_grp=w_grp, w_gate=gc, w_att=w_att, w_ssm=chunks(a["w_ssm_out"][0]), w_out=chunks(a["w_out"][0]),
        w_ffn_in=w_ffn_in, w_ffn_out=w_ffn_out, gp=gp, fpar=fpar, cos=cos, sin=sin, rot=rot,
        dt_par=np.stack([a["ssm_dt_bias"][0], a["ssm_a_log"][0]], 1), mask_k=mask_k, sinks=sinks, sinks_s=sinks_s, state=state,
        ssm_norm=columns(a["ssm_norm"][0]),
        cache_k=a["cache_k"][0, 0].transpose(2, 1, 0), cache_v=a["cache_v"][0, 0].reshape(WIN, 256),
    )
    outs = dict(y=(P, KB, TW), ssm_p=(GROUPS * P, 256), ssm_s=(GROUPS * P, 256), conv_p=(GROUPS * P, 4, 3), conv_s=(GROUPS * P, 4, 3),
                k_p=(256, WIN), k_s=(256, WIN), v_p=(WIN, 256), v_s=(WIN, 256), ffn=(P, FT, 4))
    inner_dram = dict(q=(ATT_CHUNKS + 1, P, KB, CH), qs=(P, KB, S), k=(64, KV, WIN + T + CH), ks=(64, KV, WIN + S), v=(WIN + T + CH, 256),
                      vs=(WIN + S, 256), acs=(32, TW), att=(P, KB, TW), gate=(P, GT, TW), y=(GROUPS * P, 2 * TW))

    nc = bacc.Bacc("TRN2", target_bir_lowering=False, num_devices=1)
    arrays = {f"in_{n}": np.ascontiguousarray(v) for n, v in ins.items()}
    i = {n: nc.dram_tensor(f"in_{n}", v.shape, F32, kind="ExternalInput").ap() for n, v in ins.items()}
    o = {n: nc.dram_tensor(f"out_{n}", s, F32, kind="ExternalOutput").ap() for n, s in outs.items()}
    scratch = {n: nc.dram_tensor(f"mem_{n}", s, F32, kind="Internal").ap() for n, s in inner_dram.items()}
    build_layer(nc, i, o, scratch)
    r = run_bass_kernel_spmd(nc, [arrays], core_ids=[0]).results[0]
    got = {n: np.asarray(r[f"out_{n}"]) for n in outs}

    def rows(cols):
        return got["y"][:, :, cols].transpose(2, 1, 0).reshape(1, -1, D)

    def state_out(s):
        return s.reshape(GROUPS, NS, HPG, HD).transpose(0, 2, 3, 1).reshape(1, 1, 32, HD, NS)

    def conv_out(s):
        s = s.reshape(GROUPS, P, 4, 3)
        parts = [s[:, :, 2:4].transpose(3, 0, 2, 1).reshape(3, inner), s[:, :, 0].transpose(2, 0, 1).reshape(3, 1024),
                 s[:, :, 1].transpose(2, 0, 1).reshape(3, 1024)]
        return np.concatenate(parts, 1).reshape(1, 1, 3, conv_dim)

    def kv_out(s):
        return s.reshape(1, 1, WIN, KV, HD)

    def ffn_out(s):
        return s.transpose(2, 1, 0).reshape(1, 1, 2, FT * P)

    return (rows(slice(0, T)), rows(slice(S0, TW)), state_out(got["ssm_p"]), conv_out(got["conv_p"]), kv_out(got["k_p"].T),
            kv_out(got["v_p"]), ffn_out(got["ffn"][:, :, 0:2]), state_out(got["ssm_s"]), conv_out(got["conv_s"]),
            kv_out(got["k_s"].T), kv_out(got["v_s"]), ffn_out(got["ffn"][:, :, 2:4]))
```

```python
from contextlib import ExitStack

import concourse.bass as bass
import numpy as np
from concourse import mybir

F32 = mybir.dt.float32
F32R = mybir.dt.float32r
ALU = mybir.AluOpType
ACT = mybir.ActivationFunctionType
AX = mybir.AxisListType

P = 128
D = 1024
KB = D // P
T, S = 512, 32
GAP = 4
S0 = T + GAP
TW = S0 + S
HW = TW // 2
LEAD = 4
GROUPS, HPG, HD, NS = 8, 4, 64, 128
GT = 6
KV, CH, WIN = 4, 64, 128
KEYS = WIN + CH
FT = 22
ATT_CHUNKS = T // CH
EPS = 1e-6
TAPS, FTAPS = 4, 3
GP_W, GP_B, GP_CTX, GP_D, GP_N = 0, 16, 20, 32, 34
SCAN = [(128 * c, 128) for c in range(T // 128)] + [(S0, S)]
RAW_SLOTS, HL_SLOTS = 3, 2
HL_AHEAD = 1
ADA_W = 512
(SHIFT1, SCALE1, GATE1, SHIFT2, SCALE2, GATE2) = range(0, 6 * D // ADA_W, D // ADA_W)
RANGES = [(0, T, 0), (S0, S, 1)]


def halves(ap):
    return ap.rearrange("p (a b) -> p a b", a=2)


def flat(t):
    return t[:].rearrange("p a b -> p (a b)")


def bcast_mid(ap, n):
    return ap.unsqueeze(2).to_broadcast((ap.shape[0], ap.shape[1], n))


def build_layer(nc, i, o, scratch):
    top = ExitStack()

    def sb(stack, name, shape, dt=F32, side=None):
        return stack.enter_context(nc.sbuf_tensor(name, shape, dt, side=side))

    def sems(stack, names):
        return [stack.enter_context(nc.semaphore(n)) for n in names.split()]

    with top:
        psum = top.enter_context(nc.psum_tensor("psum", [P, 8, 512], F32))
        ident = sb(top, "ident", [P, P])
        ones = sb(top, "ones", [P, P])
        consts = sb(top, "consts", [P, 2])
        eps_c, one_c = consts[:, 0:1], consts[:, 1:2]
        vecs = sb(top, "vecs", [P, 4, KB])
        mod = sb(top, "mod", [P, 48, 2])
        gain = sb(top, "gain", [P, 2, KB, 2])
        gate = sb(top, "gate", [P, 2, KB, 2])
        c_silu = sb(top, "c_silu", [P, KB, 2])
        b_ada = sb(top, "b_ada", [P, 48])
        raw_w = [sb(top, f"raw_w{n}", [P, D]) for n in range(RAW_SLOTS)]
        w_hi = [sb(top, f"w_hi{n}", [P, KB, P], F32R) for n in range(HL_SLOTS)]
        w_lo = [sb(top, f"w_lo{n}", [P, KB, P], F32R) for n in range(HL_SLOTS)]
        hp_hi = sb(top, "hp_hi", [P, KB, TW], F32R)
        hp_lo = sb(top, "hp_lo", [P, KB, TW], F32R)

        def slot(s):
            return psum[:, 2 * s:2 * s + 2, 0:HW]

        class Stream:

            def __init__(self, stack, tag, sources, base, ready, following):
                self.own, self.src, self.base = len(sources), sources + following, base
                self.raw_ready, self.hl_ready = (RAW_SLOTS, HL_AHEAD) if ready else (0, 0)
                self.landed = sems(stack, " ".join(f"{tag}_landed{n}" for n in range(RAW_SLOTS)))
                self.hi_done, self.lo_done, self.used = sems(stack, f"{tag}_hi {tag}_lo {tag}_used")
                self.all = [*self.landed, self.hi_done, self.lo_done, self.used]
                self.block = 0

            def raw_slot(self, n):
                return (self.base + n) % RAW_SLOTS

            def hl_slot(self, n):
                return (self.base + n) % HL_SLOTS

            def landings(self, n):
                return (n - self.raw_ready) // RAW_SLOTS + 1

            def load(self, sp, n):
                if not self.raw_ready <= n < len(self.src):
                    return
                if n - RAW_SLOTS >= self.hl_ready:
                    sp.wait_ge(self.lo_done, n - RAW_SLOTS - self.hl_ready + 1)
                sp.dma_start(raw_w[self.raw_slot(n)][:], self.src[n]).then_inc(self.landed[self.raw_slot(n)], 16)

            def all_landed(self, sp):
                for n in range(max(len(self.src) - RAW_SLOTS, self.raw_ready), len(self.src)):
                    sp.wait_ge(self.landed[self.raw_slot(n)], 16 * self.landings(n))

            def splits(self, n):
                return self.hl_ready <= n < min(self.own + HL_AHEAD, len(self.src))

            def split_hi(self, act, n):
                if not self.splits(n):
                    return
                if n >= self.raw_ready:
                    act.wait_ge(self.landed[self.raw_slot(n)], 16 * self.landings(n))
                if n >= HL_SLOTS:
                    act.wait_ge(self.used, n - HL_SLOTS + 1)
                act.activation(flat(w_hi[self.hl_slot(n)]), raw_w[self.raw_slot(n)][:], ACT.Copy).then_inc(self.hi_done, 1)

            def split_lo(self, eng, n):
                if not self.splits(n):
                    return
                eng.wait_ge(self.hi_done, n - self.hl_ready + 1)
                eng.tensor_tensor(flat(w_lo[self.hl_slot(n)]), raw_w[self.raw_slot(n)][:],
                                  flat(w_hi[self.hl_slot(n)]).bitcast(F32), ALU.subtract).then_inc(self.lo_done, 1)

            def all_split(self, eng):
                eng.wait_ge(self.lo_done, min(self.own + HL_AHEAD, len(self.src)) - self.hl_ready)

            def wait_split(self, pe, n):
                if n >= self.hl_ready:
                    pe.wait_ge(self.lo_done, n - self.hl_ready + 1)

            def multiply(self, pe, out, hi, lo, first, last, done=None):
                n, k = divmod(self.block, KB)
                self.block += 1
                if k == 0:
                    self.wait_split(pe, n)
                wh, wl = w_hi[self.hl_slot(n)][:, k, :], w_lo[self.hl_slot(n)][:, k, :]
                for h in range(2):
                    cols = slice(h * HW, (h + 1) * HW)
                    for j, (w, x) in enumerate(((wh, hi), (wh, lo), (wl, hi))):
                        mm = pe.matmul(out[:, h, :], w, x[:, cols], start=first and j == 0, stop=last and j == 2)
                if k == KB - 1:
                    mm.then_inc(self.used, 1)
                elif done is not None:
                    mm.then_inc(done, 1)

        def chain(sem):
            count = [0]

            def link(eng, ins):
                count[0] += 1
                ins.then_inc(sem, 1)
                eng.wait_ge(sem, count[0])
            return link

        def modulation(pe, out, block):
            for k in range(KB):
                mm = pe.matmul(out, c_silu[:, k, :], block[:, k, :], start=k == 0, stop=k == KB - 1)
            return mm

        def turn_rows(pe, bank, col, row):
            for b in range(ADA_W // P):
                mm = pe.transpose(psum[:, bank, col + 2 * b:col + 2 * b + 2], row[:, b * P:(b + 1) * P], ident[0:2, 0:2])
            return mm

        def add_bias(dve, first, count, bank):
            return dve.tensor_tensor(mod[:, first:first + count, :], psum[:, bank, 0:2 * count].rearrange("p (a b) -> p a b", b=2),
                                     bcast_mid(b_ada[:, first:first + count], 2), ALU.add)

        def load_y(sp, dst, g, sem):
            sp.dma_start(flat(dst), scratch["y"][g * P:(g + 1) * P, :]).then_inc(sem, 16)

        late_st = ExitStack()
        late_row = sb(late_st, "late_row", [2, 4, ADA_W])

        def group_chunk(n):
            return i["w_grp"][bass.ds(n * P, P), :]

        NK, NQ = 2, 8
        QK = NK + NQ
        DT, V0, G0 = QK, QK + 1, QK + 3
        NCH = G0 + GT
        w = Stream(top, "b", [i["w_qkv"][n] for n in range(G0)] + [group_chunk(n) for n in range(GT)],
                   0, False, [group_chunk(GT + n) for n in range(RAW_SLOTS)])

        with ExitStack() as st:
            UP = [SHIFT1, SHIFT1 + 1, SCALE1, SCALE1 + 1]
            BLOCKS = UP + [SHIFT2, SHIFT2 + 1]
            ADA_SLOTS = 5
            ada = [sb(st, f"ada{n}", [P, KB, ADA_W]) for n in range(ADA_SLOTS)]
            mod_row = sb(st, "mod_row", [2, len(UP), ADA_W])
            x = sb(st, "x", [P, KB, TW])
            c_in = sb(st, "c_in", [P, KB, 2])
            c_th = sb(st, "c_th", [P, KB, 2])
            sq = [sb(st, f"sq{n}", [P, TW]) for n in range(2)]
            rstd = sb(st, "rstd", [P, TW])
            h = [sb(st, f"h{n}", [P, TW]) for n in range(2)]
            xr = [sb(st, f"xr{n}", [P, TW]) for n in range(2)]
            (in_x, in_c, c_s, ada_done, row_s, turn_s, sq_s, root_s, dve_s, h_s, hi_s, sq_used, const_s,
             lo_s, add_s) = sems(
                st, "a_x a_c a_silu a_ada_done a_row a_turn a_sq a_root a_dve a_h a_hi a_squsd a_const a_lo a_add")
            in_ada = sems(st, " ".join(f"a_ada{n}" for n in range(2 * len(BLOCKS))))
            first_sem = in_x.num
            with nc.Block(no_gpsimd_drain=True) as block:
                @block.sync
                def _(sp):
                    sp.dma_start(c_in[:], i["c"]).then_inc(in_c, 16)
                    sp.dma_start(ident[:], i["ident"]).then_inc(in_c, 16)
                    sp.dma_start(consts[:], i["consts"]).then_inc(in_c, 16)
                    sp.dma_start(vecs[:], i["vecs"]).then_inc(in_c, 16)
                    sp.dma_start(b_ada[:], i["b_ada"]).then_inc(in_c, 16)
                    for n in range(2 * len(BLOCKS)):
                        if n == 4:
                            sp.dma_start(x[:], i["x"]).then_inc(in_x, 16)
                        a, ks = n // 2, slice(KB // 2 * (n % 2), KB // 2 * (n % 2 + 1))
                        if a >= ADA_SLOTS:
                            sp.wait_ge(ada_done, a - ADA_SLOTS + 1)
                        sp.dma_start(ada[a % ADA_SLOTS][:, ks, :], i["w_ada"][BLOCKS[a], :, ks, :]).then_inc(in_ada[n], 16)
                    for n in range(RAW_SLOTS):
                        w.load(sp, n)

                @block.gpsimd
                def _(pool):
                    pool.memset(ones[:], 1.0).then_inc(const_s, 1)
                    pool.memset(h[0][:, T:S0], 0.0).then_inc(const_s, 1)
                    pool.memset(h[1][:, T:S0], 0.0).then_inc(const_s, 1)
                    for n in range(HL_SLOTS):
                        w.split_lo(pool, n)
                    for t in range(KB):
                        pool.wait_ge(hi_s, t + 1)
                        pool.tensor_tensor(hp_lo[:, t, :], h[t % 2][:], hp_hi[:, t, :].bitcast(F32),
                                           ALU.subtract).then_inc(lo_s, 1)
                    pool.wait_ge(lo_s, KB)

                @block.scalar
                def _(act):
                    act.wait_ge(in_c, 80)
                    act.activation(c_th[:], c_in[:], ACT.Tanh, scale=0.5).then_inc(c_s, 1)
                    act.wait_ge(in_x, 16)
                    for t in range(KB):
                        if t >= 2:
                            act.wait_ge(add_s, max(t - 2, 1))
                        act.activation(sq[t % 2][:], x[:, t, :], ACT.Square).then_inc(sq_s, 1)
                    for a in range(len(UP)):
                        act.wait_ge(ada_done, a + 1)
                        act.activation(mod_row[:, a, :], psum[0:2, 2 + a, :], ACT.Copy).then_inc(row_s, 1)
                    act.wait_ge(sq_used, 1)
                    act.activation(halves(rstd[:]), slot(0), ACT.Sqrt, bias=eps_c, scale=1.0 / D).then_inc(root_s, 1)
                    for n in range(HL_SLOTS):
                        w.split_hi(act, n)
                    for t in range(KB):
                        act.wait_ge(h_s, t + 1)
                        act.activation(hp_hi[:, t, :], h[t % 2][:], ACT.Copy).then_inc(hi_s, 1)
                    for a in range(len(UP), len(BLOCKS)):
                        act.wait_ge(ada_done, a + 1)
                        act.activation(late_row[:, a - 2, :], psum[0:2, 2 + a % 4, :], ACT.Copy).then_inc(row_s, 1)

                @block.vector
                def _(dve):
                    link = chain(dve_s)
                    dve.wait_ge(c_s, 1)
                    link(dve, dve.scalar_tensor_tensor(out=c_silu[:], in0=c_th[:], scalar=1.0, in1=c_in[:],
                                                       op0=ALU.add, op1=ALU.mult))
                    dve.tensor_scalar(c_silu[:], c_silu[:], 0.5, None, ALU.mult).then_inc(c_s, 1)
                    for t in range(1, KB):
                        dve.wait_ge(sq_s, t + 1)
                        dve.tensor_tensor(rstd[:], sq[0][:] if t == 1 else rstd[:], sq[t % 2][:], ALU.add).then_inc(add_s, 1)
                        dve.wait_ge(add_s, t)
                    dve.wait_ge(turn_s, 1)
                    link(dve, add_bias(dve, 0, 2 * KB, 6))
                    link(dve, dve.scalar_tensor_tensor(out=gain[:, 0], in0=mod[:, KB:2 * KB, :], scalar=1.0,
                                                       in1=bcast_mid(vecs[:, 0, :], 2), op0=ALU.add, op1=ALU.mult))
                    dve.wait_ge(root_s, 1)
                    link(dve, dve.reciprocal(rstd[:], rstd[:]))
                    dve.wait_ge(const_s, 3)
                    for t in range(KB):
                        link(dve, dve.tensor_tensor(xr[t % 2][:], x[:, t, :], rstd[:], ALU.mult))
                        if t >= 2:
                            dve.wait_ge(lo_s, t - 1)
                        dve.tensor_scalar(h[t % 2][:, 0:T], xr[t % 2][:, 0:T], gain[:, 0, t, 0:1],
                                          mod[:, t, 0:1], ALU.mult, ALU.add)
                        dve.tensor_scalar(h[t % 2][:, S0:TW], xr[t % 2][:, S0:TW], gain[:, 0, t, 1:2],
                                          mod[:, t, 1:2], ALU.mult, ALU.add).then_inc(h_s, 1)

                @block.tensor
                def _(pe):
                    pe.wait_ge(c_s, 2)
                    def block_product(a):
                        out = psum[0:2, 2 + a % 4, :]
                        for k in range(KB):
                            if k % (KB // 2) == 0:
                                pe.wait_ge(in_ada[2 * a + k // (KB // 2)], 16)
                            mm = pe.matmul(out, c_silu[:, k, :], ada[a % ADA_SLOTS][:, k, :], start=k == 0, stop=k == KB - 1)
                        mm.then_inc(ada_done, 1)

                    for a in range(len(UP)):
                        block_product(a)
                    pe.wait_ge(const_s, 1)
                    pe.wait_ge(add_s, KB - 1)
                    for hh in range(2):
                        mm = pe.matmul(psum[:, hh, 0:HW], ones[:], rstd[:, hh * HW:(hh + 1) * HW], start=True, stop=True)
                    mm.then_inc(sq_used, 1)
                    pe.wait_ge(in_c, 80)
                    for a in range(len(UP)):
                        pe.wait_ge(row_s, a + 1)
                        mm = turn_rows(pe, 6, 8 * a, mod_row[:, a, :])
                    mm.then_inc(turn_s, 1)
                    for a in range(len(UP), len(BLOCKS)):
                        block_product(a)
                    for k in range(KB):
                        pe.wait_ge(lo_s, k + 1)
                        w.multiply(pe, slot(0), hp_hi[:, k, :], hp_lo[:, k, :], k == 0, k == KB - 1)

        with ExitStack() as loop_st:
            raw = sb(loop_st, "raw", [P, GT, LEAD + TW])
            gp_all = sb(loop_st, "gp_all", [P, GROUPS, GP_N])
            tok_all = sb(loop_st, "tok_all", [P, GROUPS, 5, 3, HPG])
            mask_u = sb(loop_st, "mask_u", [P, P])
            ada_g1 = [sb(loop_st, f"ada_g{n}", [P, KB, ADA_W]) for n in range(2)]

            att = ExitStack()
            loop_st.enter_context(att)
            kw = sb(att, "kw", [P, KV, KEYS])
            vw0 = sb(att, "vw0", [P, 256])
            vw1 = sb(att, "vw1", [CH, 256])
            mask_k = sb(att, "mask_k", [P, KEYS])
            sink = sb(att, "sink", [P, 2 * KV])
            sc = sb(att, "sc", [P, 2 * KV, KEYS])
            mx = sb(att, "mx", [P, 2 * KV])
            nmx = sb(att, "nmx", [P, 2 * KV])
            sm = sb(att, "sm", [P, 2 * KV])
            es = sb(att, "es", [P, 2 * KV])
            rden = sb(att, "rden", [P, 2 * KV])
            pt0 = [sb(att, f"pt0{n}", [P, 2, P]) for n in range(2)]
            pt1 = [sb(att, f"pt1{n}", [CH, 2, P]) for n in range(2)]
            oc = sb(att, "oc", [P, KB, CH])

            q_loop = sb(att, "q_loop", [P, KB, CH])

            def load_attention(sp, sem, n, q_buf, q, k, v0, v1, mask):
                for dst, src in ((q_buf[:], q), (kw[0:64, :, 0:WIN + n], k), (kw[64:128, :, 0:WIN + n], k), (vw0[:], v0),
                                 (vw1[0:n, :], v1), (mask_k[:], mask), (sink[:], i["sinks"] if n == CH else i["sinks_s"])):
                    sp.dma_start(dst, src).then_inc(sem, 16)

            ATT_IN = 7 * 16

            def load_chunk(sp, sem, g):
                load_attention(sp, sem, CH, q_loop, scratch["q"][bass.ds(g, 1)].rearrange("c p t k -> p (c t) k"),
                               scratch["k"][:, :, bass.ds(g * CH, KEYS)], scratch["v"][bass.ds(g * CH, WIN), :],
                               scratch["v"][bass.ds(g * CH + WIN, CH), :],
                               i["mask_k"][:, bass.ds(g * CH, KEYS)].to_broadcast((P, KEYS)))

            class Attention:

                def __init__(self, stack, tag, rows, masked, q, ahead):
                    self.n, self.masked, self.q, self.ahead = rows, masked, q, ahead
                    self.all = sems(stack, " ".join(f"{tag}_{x}" for x in (
                        "keys_in scores scores_read maxima exps normed turned turned_read values out_read stored order").split()))
                    (self.in_s, self.s_s, self.se_s, self.nm_s, self.ex_s, self.pn_s, self.pt_s, self.pe_s, self.pv_s,
                     self.oc_s, self.out_s, self.dv_s) = self.all

                def scores(self, pe, kv):
                    n, m = self.n, 2 * self.n
                    if kv == 0 and not self.ahead:
                        pe.wait_ge(self.in_s, ATT_IN)
                    if kv >= 2:
                        pe.wait_ge(self.se_s, kv - 1)
                    for par in range(2):
                        rows = slice(64 * par, 64 * par + 64)
                        mm = pe.matmul(psum[0:m, 4 + 2 * (kv % 2) + par, 0:WIN + n], self.q[rows, 2 * kv:2 * kv + 2, :].rearrange("p a b -> p (a b)"),
                                       kw[rows, kv, 0:WIN + n], start=True, stop=True)
                    mm.then_inc(self.s_s, 1)

                def evac_scores(self, dve, kv):
                    n, m = self.n, 2 * self.n
                    dve.wait_ge(self.s_s, kv + 1)
                    dst = sc[0:m, 2 * kv:2 * kv + 2, 0:WIN + n]
                    src = psum[0:m, 4 + 2 * (kv % 2):6 + 2 * (kv % 2), 0:WIN + n]
                    if self.masked:
                        dve.scalar_tensor_tensor(out=dst, in0=src, scalar=HD ** -0.5,
                                                 in1=mask_k[0:m, 0:WIN + n].unsqueeze(1).to_broadcast((m, 2, WIN + n)),
                                                 op0=ALU.mult, op1=ALU.add).then_inc(self.se_s, 1)
                    else:
                        dve.tensor_scalar(dst, src, HD ** -0.5, None, ALU.mult).then_inc(self.se_s, 1)

                def maxima(self, dve):
                    m, w_ = 2 * self.n, WIN + self.n
                    dve.wait_ge(self.se_s, KV)
                    dve.tensor_reduce(mx[0:m], sc[0:m, :, 0:w_], AX.X, ALU.max).then_inc(self.dv_s, 1)
                    dve.wait_ge(self.dv_s, 1)
                    dve.tensor_tensor(mx[0:m], mx[0:m], sink[0:m], ALU.max).then_inc(self.dv_s, 1)
                    dve.wait_ge(self.dv_s, 2)
                    dve.tensor_scalar(nmx[0:m], mx[0:m], -1.0, None, ALU.mult).then_inc(self.nm_s, 1)
                    dve.tensor_tensor(es[0:m], sink[0:m], mx[0:m], ALU.subtract).then_inc(self.nm_s, 1)

                def exps(self, act):
                    m, w_ = 2 * self.n, WIN + self.n
                    act.wait_ge(self.nm_s, 2)
                    for u in range(2 * KV):
                        act.activation(sc[0:m, u, 0:w_], sc[0:m, u, 0:w_], ACT.Exp, bias=nmx[0:m, u:u + 1],
                                       accum_out=sm[0:m, u:u + 1])
                    act.activation(es[0:m], es[0:m], ACT.Exp).then_inc(self.ex_s, 1)

                def normalise(self, dve):
                    m, w_ = 2 * self.n, WIN + self.n
                    dve.wait_ge(self.ex_s, 1)
                    dve.tensor_tensor(sm[0:m], sm[0:m], es[0:m], ALU.add).then_inc(self.dv_s, 1)
                    dve.wait_ge(self.dv_s, 3)
                    dve.reciprocal(rden[0:m], sm[0:m]).then_inc(self.dv_s, 1)
                    dve.wait_ge(self.dv_s, 4)
                    for u in range(2 * KV):
                        dve.tensor_scalar(sc[0:m, u, 0:w_], sc[0:m, u, 0:w_], rden[0:m, u:u + 1], None,
                                          ALU.mult).then_inc(self.pn_s, 1)

                def turn(self, pe, kv):
                    n, m, bank = self.n, 2 * self.n, 4 + kv % 2
                    pe.wait_ge(self.pn_s, 2 * kv + 2)
                    if kv >= 2:
                        pe.wait_ge(self.pe_s, kv - 1)
                    for par in range(2):
                        pe.transpose(psum[:, bank, par * P:par * P + m], sc[0:m, 2 * kv + par, 0:WIN], ident[0:m, 0:m])
                        mm = pe.transpose(psum[0:n, bank, 256 + par * P:256 + par * P + m], sc[0:m, 2 * kv + par, WIN:WIN + n],
                                          ident[0:m, 0:m])
                    mm.then_inc(self.pt_s, 1)

                def evac_turned(self, act, kv):
                    n, m, bank = self.n, 2 * self.n, 4 + kv % 2
                    act.wait_ge(self.pt_s, kv + 1)
                    if kv >= 2:
                        act.wait_ge(self.pv_s, kv - 1)
                    act.activation(pt0[kv % 2][:, :, 0:m], psum[:, bank, 0:256].rearrange("p (a b) -> p a b", a=2)[:, :, 0:m], ACT.Copy)
                    act.activation(pt1[kv % 2][0:n, :, 0:m], psum[0:n, bank, 256:512].rearrange("p (a b) -> p a b", a=2)[:, :, 0:m],
                                   ACT.Copy).then_inc(self.pe_s, 1)

                def values(self, pe, kv):
                    n, m = self.n, 2 * self.n
                    pe.wait_ge(self.pe_s, kv + 1)
                    for par in range(2):
                        out = psum[64 * par:64 * par + 64, 7, kv * m:kv * m + m]
                        pe.matmul(out, vw0[:, 64 * kv:64 * kv + 64], pt0[kv % 2][:, par, 0:m], start=True, stop=False)
                        mm = pe.matmul(out, vw1[0:n, 64 * kv:64 * kv + 64], pt1[kv % 2][0:n, par, 0:m], start=False, stop=True)
                    mm.then_inc(self.pv_s, 1)

                def evac_out(self, act):
                    n = self.n
                    act.wait_ge(self.pv_s, KV)
                    act.activation(oc[:, :, 0:n], psum[:, 7, 0:8 * n].rearrange("p (a b) -> p a b", a=8), ACT.Copy).then_inc(self.oc_s, 1)

                def store(self, sp, dst):
                    sp.wait_ge(self.oc_s, 1)
                    sp.dma_start(dst, oc[:, :, 0:self.n]).then_inc(self.out_s, 16)

            with ExitStack() as st:
                cos = sb(st, "cos", [P, TW])
                sin = sb(st, "sin", [P, TW])
                rot = sb(st, "rot", [P, P])
                zeros = sb(st, "zeros", [P, 256])
                qk = [sb(st, f"qk{n}", [P, TW]) for n in range(2)]
                t_cos = [sb(st, f"t_cos{n}", [P, TW]) for n in range(2)]
                qk_rot = [sb(st, f"qk_rot{n}", [P, TW]) for n in range(2)]
                v_sb = sb(st, "v_sb", [P, 5, 256])
                dt_v = sb(st, "dt_v", [32, TW])
                dt_n = sb(st, "dt_n", [32, TW])
                dt_e = sb(st, "dt_e", [32, TW])
                dt_l = sb(st, "dt_l", [32, TW])
                dt = sb(st, "dt", [32, TW])
                da = sb(st, "da", [32, TW])
                acs = sb(st, "acs", [32, TW])
                edt = sb(st, "edt", [32, TW])
                nacs = sb(st, "nacs", [32, TW])
                dt_par = sb(st, "dt_par", [32, 2])
                a_exp = sb(st, "a_exp", [32, 1])
                AT = G0 + 2
                (in_s, init_s, evac_s, rot_s, rope_s, out_s0, out_s1, copy_s, acs_s, tr_s, dtp_s, sc_s,
                 dve_s, e_s) = sems(
                    st, "b_in b_init b_evac b_rot b_rope b_out0 b_out1 b_copy b_acs b_tr b_dtp b_sc b_dve b_e")
                ada_in, acs_out, tok_s = sems(st, "b_ada_in b_acs_out b_tok")
                at = Attention(st, "s", S, False, sb(st, "q_sample", [P, KB, S]), False)
                next_in, vt_s, v_s = sems(st, "b_next_in b_vt b_v")
                out_s = [out_s0, out_s1]

                def q_dst(t):
                    return scratch["q"][0:ATT_CHUNKS, :, t, :].rearrange("c p k -> p c k")

                with nc.Block(no_gpsimd_drain=True) as block:
                    @block.sync
                    def _(sp):
                        for n in range(RAW_SLOTS, RAW_SLOTS + HL_SLOTS):
                            w.load(sp, n)
                        for dst, name in ((cos, "cos"), (sin, "sin"), (rot, "rot"), (dt_par, "dt_par"),
                                          (gp_all, "gp"), (mask_u, "mask_u")):
                            sp.dma_start(dst[:], i[name]).then_inc(in_s, 16)
                        sp.wait_ge(init_s, 1)
                        sp.dma_start(scratch["k"][:, 0:2, 0:WIN], zeros[0:64, :].rearrange("p (a b) -> p a b", a=2)).then_inc(copy_s, 16)
                        sp.dma_start(scratch["k"][:, 2:4, 0:WIN], zeros[0:64, :].rearrange("p (a b) -> p a b", a=2)).then_inc(copy_s, 16)
                        sp.dma_start(scratch["v"][0:WIN, :], zeros[:]).then_inc(copy_s, 16)
                        sp.dma_start(scratch["k"][:, :, WIN + T:], zeros[0:64, 0:KV * CH].rearrange("p (a b) -> p a b", a=KV)).then_inc(copy_s, 16)
                        sp.dma_start(scratch["v"][WIN + T:, :], zeros[0:CH, :]).then_inc(copy_s, 16)
                        for t in range(0, KB, 4):
                            sp.dma_start(scratch["q"][ATT_CHUNKS, :, t:t + 4, :], zeros[:].rearrange("p (a b) -> p a b", a=4)).then_inc(copy_s, 16)
                        sp.dma_start(scratch["att"][:, :, T:S0], zeros[:, 0:KB * GAP].rearrange("p (a b) -> p a b", a=KB)).then_inc(copy_s, 16)
                        sp.dma_start(scratch["ks"][:, :, 0:WIN], i["cache_k"]).then_inc(copy_s, 16)
                        sp.dma_start(scratch["vs"][0:WIN, :], i["cache_v"]).then_inc(copy_s, 16)
                        for j in range(NK):
                            for a in range(2):
                                kv = 2 * j + a
                                sp.dma_start(o["k_s"][64 * kv:64 * kv + 64, 0:WIN - S], i["cache_k"][:, kv, S:WIN]).then_inc(copy_s, 16)
                        sp.dma_start(o["v_s"][0:WIN - S, :], i["cache_v"][S:WIN, :]).then_inc(copy_s, 16)
                        n_copy = 15
                        for n in range(2):
                            sp.dma_start(ada_g1[n][:], i["w_ada"][GATE1 + n]).then_inc(ada_in, 16)
                        for n in range(RAW_SLOTS + HL_SLOTS, NCH):
                            w.load(sp, n)
                            j = n - RAW_SLOTS - HL_SLOTS
                            if j < QK:
                                sp.wait_ge(rope_s, j + 1)
                                r = qk_rot[j % 2]
                                if j < NK:
                                    for a in range(2):
                                        rows, kv = slice(64 * a, 64 * a + 64), 2 * j + a
                                        sp.dma_start(scratch["k"][:, kv, WIN:WIN + T], r[rows, 0:T]).then_inc(out_s[j % 2], 16)
                                        sp.dma_start(scratch["ks"][:, kv, WIN:WIN + S], r[rows, S0:TW]).then_inc(out_s[j % 2], 16)
                                    sp.dma_start(o["k_p"][P * j:P * j + P, :], r[:, T - WIN:T]).then_inc(out_s[j % 2], 16)
                                    sp.dma_start(o["k_s"][P * j:P * j + P, WIN - S:WIN], r[:, S0:TW]).then_inc(out_s[j % 2], 16)
                                else:
                                    t = j - NK
                                    sp.dma_start(q_dst(t), r[:, 0:T].rearrange("p (c k) -> p c k", k=CH)).then_inc(out_s[j % 2], 16)
                                    sp.dma_start(scratch["qs"][:, t, :], r[:, S0:TW]).then_inc(out_s[j % 2], 16)
                        sp.wait_ge(v_s, 2)
                        sp.dma_start(scratch["v"][WIN:WIN + T, :].rearrange("(a p) d -> p a d", p=P), v_sb[:, 0:4, :]).then_inc(copy_s, 16)
                        sp.dma_start(scratch["vs"][WIN:WIN + S, :], v_sb[0:S, 4, :]).then_inc(copy_s, 16)
                        sp.dma_start(o["v_p"], v_sb[:, 3, :]).then_inc(copy_s, 16)
                        sp.dma_start(o["v_s"][WIN - S:WIN, :], v_sb[0:S, 4, :]).then_inc(copy_s, 16)
                        sp.wait_ge(acs_s, 1)
                        sp.dma_start(scratch["acs"], acs[:]).then_inc(acs_out, 16)
                        for s in out_s:
                            sp.wait_ge(s, 96 + 32 * (NQ // 2))
                        sp.wait_ge(copy_s, 16 * (n_copy + 4))
                        load_attention(sp, at.in_s, S, at.q, scratch["qs"], scratch["ks"], scratch["vs"][0:WIN, :], scratch["vs"][WIN:WIN + S, :],
                                i["mask_k"][:, 0:KEYS].to_broadcast((P, KEYS)))
                        for n in range(NCH, NCH + RAW_SLOTS):
                            w.load(sp, n)
                        w.all_landed(sp)
                        sp.wait_ge(ada_in, 32)
                        sp.wait_ge(acs_out, 16)
                        at.store(sp, scratch["att"][:, :, S0:TW])
                        load_chunk(sp, next_in, 0)
                        sp.wait_ge(next_in, ATT_IN)
                        sp.wait_ge(at.out_s, 16)

                    @block.gpsimd
                    def _(pool):
                        pool.memset(zeros[:], 0.0).then_inc(init_s, 1)
                        pool.memset(raw[:, :, 0:LEAD], 0.0).then_inc(init_s, 1)
                        pool.memset(acs[:], 0.0).then_inc(init_s, 1)
                        pool.memset(edt[:], 0.0).then_inc(init_s, 1)
                        pool.memset(tok_all[:], 0.0).then_inc(init_s, 1)
                        for n in range(HL_SLOTS, NCH + HL_AHEAD):
                            w.split_lo(pool, n)
                        w.all_split(pool)

                    @block.scalar
                    def _(act):
                        for n in range(NCH):
                            w.split_hi(act, n + 2)
                            act.wait_ge(w.used, n + 1)
                            if n < QK:
                                if n >= 2:
                                    act.wait_ge(rope_s, n - 1)
                                act.activation(halves(qk[n % 2][:]), slot(n % 2), ACT.Copy).then_inc(evac_s, 1)
                            elif n == DT:
                                act.wait_ge(in_s, 96)
                                act.activation(halves(dt_v[:]), psum[0:32, 2 * (n % 2):2 * (n % 2) + 2, 0:HW], ACT.Identity,
                                               bias=dt_par[:, 0:1]).then_inc(evac_s, 1)
                                act.activation(a_exp[:], dt_par[:, 1:2], ACT.Exp).then_inc(e_s, 1)
                                act.wait_ge(dtp_s, 1)
                                act.activation(dt_e[:], dt_n[:], ACT.Exp).then_inc(e_s, 1)
                                act.wait_ge(e_s, 2)
                                act.activation(dt_l[:], dt_e[:], ACT.Ln, bias=one_c[0:32]).then_inc(e_s, 1)
                            elif n < G0:
                                if n == V0:
                                    act.wait_ge(rope_s, QK)
                                act.activation(halves(qk[n % 2][:]), slot(n % 2), ACT.Copy).then_inc(evac_s, 1)
                            else:
                                if n == G0:
                                    act.wait_ge(acs_s, 1)
                                    for ci, (c0, L) in enumerate(SCAN):
                                        act.activation(edt[:, c0:c0 + L], acs[:, c0:c0 + L], ACT.Exp, scale=-1.0,
                                                       bias=acs[:, c0 + L - 1:c0 + L]).then_inc(sc_s, 1)
                                    act.wait_ge(init_s, 5)
                                act.activation(halves(raw[:, n - G0, LEAD:]), slot(n % 2), ACT.Copy).then_inc(evac_s, 1)
                                if n == AT + 1:
                                    at.exps(act)
                                    at.evac_turned(act, 0)
                                    at.evac_turned(act, 1)
                                if n == AT + 2:
                                    at.evac_turned(act, 2)
                                    at.evac_turned(act, 3)
                                    at.evac_out(act)

                    @block.vector
                    def _(dve):
                        link = chain(dve_s)
                        dve.wait_ge(in_s, 96)
                        link(dve, dve.tensor_scalar(gp_all[:, :, 0:GP_CTX], gp_all[:, :, 0:GP_CTX], 0.5, None, ALU.mult))
                        for n in range(QK):
                            dve.wait_ge(evac_s, n + 1)
                            if n >= 2:
                                dve.wait_ge(out_s[n % 2], 96 + 32 * ((n - 2) // 2))
                            link(dve, dve.tensor_tensor(t_cos[n % 2][:], qk[n % 2][:], cos[:], ALU.mult))
                            dve.wait_ge(rot_s, n + 1)
                            link(dve, dve.tensor_tensor(halves(qk_rot[n % 2][:]), slot(2 + n % 2), halves(sin[:]), ALU.mult))
                            dve.tensor_tensor(qk_rot[n % 2][:], qk_rot[n % 2][:], t_cos[n % 2][:], ALU.add).then_inc(rope_s, 1)
                        dve.wait_ge(evac_s, DT + 1)
                        dve.scalar_tensor_tensor(out=dt_n[:], in0=dt_v[:], scalar=-1.0, in1=dt_v[:], op0=ALU.mult,
                                                 op1=ALU.min).then_inc(dtp_s, 1)
                        dve.wait_ge(e_s, 3)
                        dve.wait_ge(init_s, 5)
                        link(dve, dve.scalar_tensor_tensor(out=dt[:], in0=dt_v[:], scalar=0.0, in1=dt_l[:], op0=ALU.max, op1=ALU.add))
                        link(dve, dve.tensor_scalar(da[:], dt[:], a_exp[:], -1.0, ALU.mult, ALU.mult))
                        for c0, L in SCAN:
                            ins = dve.tensor_tensor_scan(acs[:, c0:c0 + L], ones[0:32, 0:L], da[:, c0:c0 + L], 0.0,
                                                         ALU.mult, ALU.add)
                        ins.then_inc(acs_s, 1)
                        for j in range(2):
                            dve.wait_ge(vt_s, j + 1)
                            dve.tensor_copy(v_sb[:, 0:4, j * P:(j + 1) * P], psum[:, 4 + j, :].rearrange("p (a c) -> p a c", a=4))
                            dve.tensor_copy(v_sb[0:S, 4, j * P:(j + 1) * P], psum[0:S, 6 + j, 0:P]).then_inc(v_s, 1)
                        dve.wait_ge(sc_s, 5)
                        dve.tensor_scalar(nacs[:], acs[:], -1.0, None, ALU.mult).then_inc(sc_s, 1)
                        dve.wait_ge(tr_s, 1)
                        for ci, (c0, L) in enumerate(SCAN):
                            ins = dve.tensor_copy(tok_all[0:L, :, ci, :, :],
                                            psum[0:L, 7, 96 * ci:96 * ci + 96].rearrange("p (a g r) -> p g a r", a=3, g=GROUPS))
                        ins.then_inc(tok_s, 1)
                        for kv in range(KV):
                            at.evac_scores(dve, kv)
                        at.maxima(dve)
                        at.normalise(dve)

                    @block.tensor
                    def _(pe):
                        for n in range(NCH):
                            if n >= 2:
                                pe.wait_ge(evac_s, n - 1)
                            for k in range(KB):
                                if n > 0:
                                    w.multiply(pe, slot(n % 2), hp_hi[:, k, :], hp_lo[:, k, :], k == 0, k == KB - 1)
                                if V0 < n <= G0 and k == 3:
                                    j = n - 1 - V0
                                    pe.wait_ge(evac_s, n)
                                    pe.wait_ge(rope_s, QK)
                                    for a, (c0, L) in enumerate(SCAN):
                                        out = psum[0:L, 4 + j, a * P:a * P + P] if a < 4 else psum[0:L, 6 + j, 0:P]
                                        mm = pe.transpose(out, qk[(n - 1) % 2][:, c0:c0 + L], ident[:])
                                    mm.then_inc(vt_s, 1)
                                if n == AT + 1 and k == 1:
                                    pe.wait_ge(tok_s, 1)
                                if n == AT + 1 and k in (1, 3):
                                    for kv in (k - 1, k):
                                        at.scores(pe, kv)
                                u = (n - AT - 2) * KB + k - 3
                                if 0 <= u < 8:
                                    step, kv = ((at.turn, 0), (at.turn, 1), (at.values, 0), (at.turn, 2), (at.values, 1),
                                                (at.turn, 3), (at.values, 2), (at.values, 3))[u]
                                    step(pe, kv)
                            if 1 <= n <= QK:
                                j = n - 1
                                if j == 0:
                                    pe.wait_ge(in_s, 96)
                                pe.wait_ge(evac_s, j + 1)
                                if j >= 2:
                                    pe.wait_ge(rope_s, j - 1)
                                for hh in range(2):
                                    mm = pe.matmul(psum[:, 4 + 2 * (j % 2) + hh, 0:HW], rot[:], qk[j % 2][:, hh * HW:(hh + 1) * HW],
                                                   start=True, stop=True)
                                mm.then_inc(rot_s, 1)
                            if n == AT:
                                pe.wait_ge(sc_s, 6)
                                pe.wait_ge(rope_s, QK)
                                for ci, (c0, L) in enumerate(SCAN):
                                    for a, src in enumerate((dt, edt, nacs)):
                                        mm = pe.transpose(psum[0:L, 7, 96 * ci + 32 * a:96 * ci + 32 * a + 32],
                                                          src[:, c0:c0 + L], ident[0:32, 0:32])
                                mm.then_inc(tr_s, 1)

            with ExitStack() as st:
                gp = sb(st, "gp", [P, GP_N])
                tok = sb(st, "tok", [P, 5, 3, HPG])
                cv = sb(st, "cv", [P, GT, TW])
                th = [sb(st, f"th{n}", [P, TW]) for n in range(2)]
                acs_b = sb(st, "acs_b", [P, HPG, TW])
                e_b = sb(st, "e_b", [P, HPG, TW])
                c_s_ = sb(st, "c_dec", [P, HPG, TW])
                xdt = [sb(st, f"xdt{n}", [P, HPG, HD]) for n in range(2)]
                xt = [sb(st, f"xt{n}", [P, HPG, HD]) for n in range(2)]
                bt = [sb(st, f"bt{n}", [P, NS]) for n in range(2)]
                cbm = [sb(st, f"cbm{n}", [P, P]) for n in range(2)]
                dec = [sb(st, f"dec{n}", [P, HPG, P]) for n in range(2)]
                y = sb(st, "y", [P, 2, TW])
                h_p = sb(st, "h_p", [P, HPG, HD])
                h_s0 = sb(st, "h_s0", [P, HPG, HD])
                names = ("g_par g_conv g_th g_silu g_eb g_cdec g_tr g_cb g_xd g_bt g_w g_xt g_dif g_dece g_y g_ds g_ye g_h"
                         " g_evac g_yout g_out g_acs g_dve g_h0 g_cbe g_conv_out g_ctx")
                handles = sems(st, names)
                (par_s, conv_s, th_s, silu_s, eb_s, cdec_s, tr_s, cb_s, xd_s, bt_s, w_s, xt_s, dif_s, dece_s, y_s, ds_s,
                 ye_s, hst_s, evac_s, yout_s, gout_s, acsb_s, dve_s, h0_s, cbe_s, cout_s, ctx_s) = handles
                w = Stream(st, "g", [None] * GT, NCH, True, [None] * RAW_SLOTS)
                assert GT % RAW_SLOTS == 0 and GT % HL_SLOTS == 0
                at = Attention(st, "g", CH, True, q_loop, True)
                nums = sorted(s.num for s in handles + w.all + at.all)
                assert nums == list(range(nums[0], nums[-1] + 1))
                sem_range = range(nums[0], nums[-1] + 1)
                NC5 = len(SCAN)

                def group(g):
                    w.src = [group_chunk(GT + n + g * GT) for n in range(GT + RAW_SLOTS)]
                    w.block = 0
                    with nc.Block(no_gpsimd_drain=True) as block:
                        @block.sync
                        def _(sp):
                            for n in range(RAW_SLOTS, RAW_SLOTS + HL_SLOTS):
                                w.load(sp, n)
                            sp.wait_ge(ctx_s, 1)
                            sp.dma_start(acs_b[:], scratch["acs"][bass.ds(g * HPG, HPG), :].unsqueeze(0)
                                         .to_broadcast((P, HPG, TW))).then_inc(acsb_s, 16)
                            sp.dma_start(h_s0[:].rearrange("p a b -> p (a b)"), i["state"][bass.ds(g * P, P), :]).then_inc(h0_s, 16)
                            sp.dma_start(o["conv_p"][bass.ds(g * P, P), :], raw_last(T)).then_inc(cout_s, 16)
                            sp.dma_start(o["conv_s"][bass.ds(g * P, P), :], raw_last(TW)).then_inc(cout_s, 16)
                            w.load(sp, RAW_SLOTS + HL_SLOTS)
                            at.store(sp, scratch["att"][:, :, bass.ds(g * CH, CH)])
                            load_chunk(sp, at.in_s, g + 1)
                            for n in range(GT, GT + RAW_SLOTS):
                                w.load(sp, n)
                            sp.wait_ge(hst_s, 4)
                            sp.dma_start(o["ssm_p"][bass.ds(g * P, P), :], h_p[:].rearrange("p a b -> p (a b)")).then_inc(gout_s, 16)
                            sp.wait_ge(hst_s, 5)
                            sp.dma_start(o["ssm_s"][bass.ds(g * P, P), :], h_s0[:].rearrange("p a b -> p (a b)")).then_inc(gout_s, 16)
                            sp.wait_ge(yout_s, 1)
                            sp.dma_start(scratch["y"][bass.ds(g * P, P), :], y[:].rearrange("p a b -> p (a b)")).then_inc(gout_s, 16)
                            w.all_landed(sp)
                            sp.wait_ge(at.in_s, ATT_IN)
                            sp.wait_ge(gout_s, 48)
                            sp.wait_ge(cout_s, 32)
                            sp.wait_ge(at.out_s, 16)

                        @block.gpsimd
                        def _(pool):
                            pool.tensor_copy(gp[:], gp_all[:, bass.ds(g, 1), :].rearrange("p a b -> p (a b)")).then_inc(par_s, 1)
                            pool.tensor_copy(tok[:].rearrange("p a b c -> p (a b c)"),
                                             tok_all[:, bass.ds(g, 1)].rearrange("p g a b c -> p (g a b c)")).then_inc(par_s, 1)
                            w.split_lo(pool, 1)
                            w.split_lo(pool, 2)
                            pool.wait_ge(eb_s, 1)
                            pool.wait_ge(silu_s, 2)
                            for r in range(HPG):
                                pool.tensor_tensor(c_s_[:, r, :], e_b[:, r, :], cv[:, 1, :], ALU.mult).then_inc(cdec_s, 1)

                            def end_weighted(c):
                                L, b = SCAN[c][1], c % 2
                                pool.wait_ge(xd_s, c + 1)
                                if c >= 2:
                                    pool.wait_ge(ds_s, c - 1)
                                pool.tensor_tensor(xt[b][0:L], xdt[b][0:L], bcast_mid(tok[0:L, c, 1, :], HD),
                                                   ALU.mult).then_inc(xt_s, 1)

                            w.split_lo(pool, 3)
                            w.split_lo(pool, 4)
                            end_weighted(0)
                            end_weighted(1)
                            w.split_lo(pool, 5)
                            end_weighted(2)
                            end_weighted(3)
                            end_weighted(4)
                            for n in range(GT, GT + HL_AHEAD):
                                w.split_lo(pool, n)
                            w.all_split(pool)

                        @block.scalar
                        def _(act):
                            def tanh(t):
                                act.wait_ge(conv_s, min(t, 3) + 1)
                                if t >= 2:
                                    act.wait_ge(silu_s, t - 1)
                                if t < 4:
                                    act.activation(th[t % 2][:], cv[:, t, :], ACT.Tanh).then_inc(th_s, 1)
                                else:
                                    act.activation(th[t % 2][:], raw[:, t, LEAD:], ACT.Tanh, scale=0.5).then_inc(th_s, 1)

                            def evac(t):
                                act.wait_ge(w.used, t + 1)
                                if t < 4:
                                    act.wait_ge(conv_s, t + 1)
                                    act.wait_ge(cout_s, 32)
                                else:
                                    act.wait_ge(silu_s, t + 1)
                                act.activation(halves(raw[:, t, LEAD:]), slot(t % 2), ACT.Copy).then_inc(evac_s, 1)

                            def scan_exp(c):
                                L = SCAN[c][1]
                                b = c % 2
                                act.wait_ge(dif_s, c + 1)
                                act.activation(dec[b][0:L, :, 0:L], dec[b][0:L, :, 0:L], ACT.Exp).then_inc(dece_s, 1)
                                act.wait_ge(tr_s, c + 1)
                                act.activation(bt[b][0:L, :], psum[0:L, 5, 0:P], ACT.Copy).then_inc(bt_s, 1)

                            w.split_hi(act, 1)
                            tanh(0)
                            w.split_hi(act, 2)
                            at.exps(act)
                            evac(0)
                            tanh(1)
                            act.wait_ge(acsb_s, 16)
                            act.activation(e_b[:], acs_b[:], ACT.Exp).then_inc(eb_s, 1)
                            tanh(2)
                            w.split_hi(act, 3)
                            evac(1)
                            for kv in range(KV):
                                at.evac_turned(act, kv)
                            at.evac_out(act)
                            tanh(3)
                            tanh(4)
                            tanh(5)
                            w.split_hi(act, 4)
                            evac(2)
                            scan_exp(0)
                            scan_exp(1)
                            scan_exp(2)
                            w.split_hi(act, 5)
                            evac(3)
                            scan_exp(3)
                            scan_exp(4)
                            w.split_hi(act, GT)
                            evac(4)
                            evac(5)

                        @block.vector
                        def _(dve):
                            link = chain(dve_s)

                            def conv(t):
                                link(dve, dve.tensor_scalar(cv[:, t, :], raw[:, t, 1:1 + TW], gp[:, GP_W + 4 * t:GP_W + 4 * t + 1],
                                                            gp[:, GP_B + t:GP_B + t + 1], ALU.mult, ALU.add))
                                for k in range(1, TAPS):
                                    ins = dve.scalar_tensor_tensor(
                                        out=cv[:, t, :], in0=raw[:, t, 1 + k:1 + k + TW],
                                        scalar=gp[:, GP_W + 4 * t + k:GP_W + 4 * t + k + 1], in1=cv[:, t, :],
                                        op0=ALU.mult, op1=ALU.add)
                                    if k < TAPS - 1:
                                        link(dve, ins)
                                ins.then_inc(conv_s, 1)

                            def silu(t):
                                dve.wait_ge(th_s, t + 1)
                                src = cv[:, t, :] if t < 4 else raw[:, t, LEAD:]
                                dve.scalar_tensor_tensor(out=cv[:, t, :], in0=th[t % 2][:], scalar=1.0, in1=src,
                                                         op0=ALU.add, op1=ALU.mult).then_inc(silu_s, 1)

                            def weights(c):
                                c0, L = SCAN[c]
                                b = c % 2
                                if c >= 2:
                                    dve.wait_ge(ds_s, c - 1)
                                for r in range(HPG):
                                    ins = dve.tensor_scalar(dec[b][0:L, r, 0:L], acs_b[0:L, r, c0:c0 + L],
                                                            tok[0:L, c, 2, r:r + 1], 0.0, ALU.add, ALU.min)
                                ins.then_inc(dif_s, 1)
                                dve.wait_ge(cb_s, c + 1)
                                dve.tensor_tensor(xdt[b][0:L], psum[0:L, 4, 0:2 * P].rearrange("p (r d) -> p r d", r=HPG),
                                                  bcast_mid(tok[0:L, c, 0, :], HD), ALU.mult).then_inc(xd_s, 1)
                                dve.tensor_tensor(cbm[b][0:L, 0:L], psum[0:L, 4, 2 * P:2 * P + L], mask_u[0:L, 0:L],
                                                  ALU.mult).then_inc(cbe_s, 1)
                                dve.wait_ge(cbe_s, c + 1)
                                dve.wait_ge(dece_s, c + 1)
                                dve.tensor_tensor(dec[b][0:L, :, 0:L], dec[b][0:L, :, 0:L],
                                                  cbm[b][0:L, 0:L].unsqueeze(1).to_broadcast((L, HPG, L)), ALU.mult).then_inc(w_s, 1)

                            def outputs(c):
                                c0, L = SCAN[c]
                                dve.wait_ge(y_s, c + 1)
                                for t in range(2):
                                    ins = dve.scalar_tensor_tensor(out=y[:, t, c0:c0 + L], in0=cv[:, 2 + t, c0:c0 + L],
                                                             scalar=gp[:, GP_D + t:GP_D + t + 1],
                                                             in1=psum[:, 6, t * P:t * P + L], op0=ALU.mult, op1=ALU.add)
                                ins.then_inc(ye_s, 1)
                                dve.wait_ge(ds_s, c + 1)
                                d_s = psum[:, 7, 0:256].rearrange("p (r d) -> p r d", r=HPG)
                                if c == 0:
                                    dve.tensor_copy(h_p[:], d_s).then_inc(hst_s, 1)
                                    return
                                h_ = h_p if c < 4 else h_s0
                                link(dve, dve.tensor_tensor(h_[:], h_[:], e_b[:, :, c0 + L - 1:c0 + L].to_broadcast((P, HPG, HD)), ALU.mult))
                                dve.tensor_tensor(h_[:], h_[:], d_s, ALU.add).then_inc(hst_s, 1)

                            dve.wait_ge(par_s, 2)
                            dve.tensor_copy(raw[:, 0:4, LEAD + S0 - 3:LEAD + S0],
                                            gp[:, GP_CTX:GP_CTX + 12].rearrange("p (a b) -> p a b", a=4)).then_inc(ctx_s, 1)
                            dve.wait_ge(ctx_s, 1)
                            at.evac_scores(dve, 0)
                            at.evac_scores(dve, 1)
                            conv(0)
                            at.evac_scores(dve, 2)
                            at.evac_scores(dve, 3)
                            at.maxima(dve)
                            conv(1)
                            silu(0)
                            conv(2)
                            at.normalise(dve)
                            silu(1)
                            conv(3)
                            silu(2)
                            silu(3)
                            silu(4)
                            dve.wait_ge(eb_s, 1)
                            weights(0)
                            silu(5)
                            weights(1)
                            outputs(0)
                            dve.memset(y[:, :, T:S0], 0.0)
                            for c in range(1, NC5):
                                if c + 1 < NC5:
                                    weights(c + 1)
                                if c == 4:
                                    dve.wait_ge(h0_s, 16)
                                outputs(c)
                            dve.wait_ge(ye_s, NC5)
                            dve.wait_ge(silu_s, 6)
                            dve.scalar_tensor_tensor(out=y[:], in0=y[:], scalar=0.5, in1=cv[:, 4:6, :], op0=ALU.mult,
                                                     op1=ALU.mult).then_inc(yout_s, 1)

                        @block.tensor
                        def _(pe):
                            steps = iter(range(GT * KB))

                            def fill(n):
                                for _ in range(n):
                                    u = next(steps, None)
                                    if u is None:
                                        return
                                    t, k = divmod(u, KB)
                                    if k == 0 and t >= 2:
                                        pe.wait_ge(evac_s, t - 1)
                                    w.multiply(pe, slot(t % 2), hp_hi[:, k, :], hp_lo[:, k, :], k == 0, k == KB - 1)

                            def turn_scores(c):
                                c0, L = SCAN[c]
                                if c == 0:
                                    pe.wait_ge(silu_s, 4)
                                    pe.wait_ge(at.oc_s, 1)
                                else:
                                    pe.wait_ge(xd_s, c)
                                    pe.wait_ge(bt_s, c)
                                    pe.wait_ge(cbe_s, c)
                                for t in range(2):
                                    pe.transpose(psum[0:L, 4, t * P:t * P + P], cv[:, 2 + t, c0:c0 + L], ident[:])
                                pe.matmul(psum[0:L, 4, 2 * P:2 * P + L], cv[:, 0, c0:c0 + L], cv[:, 1, c0:c0 + L], start=True,
                                          stop=True).then_inc(cb_s, 1)
                                pe.transpose(psum[0:L, 5, 0:P], cv[:, 0, c0:c0 + L], ident[:]).then_inc(tr_s, 1)

                            def scan(c):
                                c0, L = SCAN[c]
                                b = c % 2
                                pe.wait_ge(w_s, c + 1)
                                if c >= 1:
                                    pe.wait_ge(ye_s, c)
                                    pe.wait_ge(hst_s, c)
                                if c == 4:
                                    pe.wait_ge(h0_s, 16)
                                pe.wait_ge(cdec_s, HPG)
                                h_ = h_p if c < 4 else h_s0
                                for r in range(HPG):
                                    half, t = r % 2, r // 2
                                    out = psum[64 * half:64 * half + 64, 6, t * P:t * P + L]
                                    mm = pe.matmul(out, xdt[b][0:L, r, :], dec[b][0:L, r, 0:L], start=True, stop=c == 0)
                                    if c > 0:
                                        mm = pe.matmul(out, h_[:, r, :], c_s_[:, r, c0:c0 + L], start=False, stop=True)
                                mm.then_inc(y_s, 1)
                                pe.wait_ge(bt_s, c + 1)
                                pe.wait_ge(xt_s, c + 1)
                                pe.matmul(psum[:, 7, 0:256], bt[b][0:L, :], xt[b][0:L].rearrange("p r d -> p (r d)"),
                                          start=True, stop=True).then_inc(ds_s, 1)

                            at.scores(pe, 0)
                            at.scores(pe, 1)
                            fill(3)
                            at.scores(pe, 2)
                            at.scores(pe, 3)
                            fill(14)
                            at.turn(pe, 0)
                            for kv in range(KV):
                                if kv + 1 < KV:
                                    at.turn(pe, kv + 1)
                                fill(1)
                                at.values(pe, kv)
                            fill(5)
                            turn_scores(0)
                            fill(2)
                            for c in range(NC5):
                                if c + 1 < NC5:
                                    turn_scores(c + 1)
                                fill(2)
                                scan(c)
                            fill(GT * KB)
                    nc.all_engine_barrier(sems_to_clear=sem_range)

                def raw_last(end):
                    return raw[:, 0:4, LEAD + end - 3:LEAD + end]

                nc.all_engine_barrier(sems_to_clear=range(first_sem, sem_range.stop))
                with nc.Fori(0, GROUPS) as g:
                    group(g)

            att.close()
            hq_st = ExitStack()
            hq_hi = sb(hq_st, "hq_hi", [P, KB, TW], F32R, side="right")
            hq_lo = sb(hq_st, "hq_lo", [P, KB, TW], F32R, side="right")
            rr_st = ExitStack()
            y_rstd = sb(rr_st, "y_rstd", [GROUPS, TW], side="right")
            with ExitStack() as st:
                AT_IN, Y_IN = 4, 3
                pick = sb(st, "pick", [P, GROUPS, GROUPS])
                yl = [sb(st, f"yp{n}", [P, 2, TW]) for n in range(Y_IN)]
                sq = [sb(st, f"ysq{n}", [P, 2, TW]) for n in range(2)]
                sq_sum = [sb(st, f"ysum{n}", [P, TW]) for n in range(2)]
                in_y = sems(st, " ".join(f"p_y{n}" for n in range(Y_IN)))
                pick_in, sq_s, add_s, ss_s, root_s = sems(st, "p_pick p_sq p_add p_ss p_root")
                al = [sb(st, f"al{n}", [P, TW]) for n in range(AT_IN)]
                gate_out, ahi_s, alo_s, row_done, row_s, turn_s, bias_s = sems(st, "p_gate_out p_ahi p_alo p_rowdone p_row p_turn p_bias")
                in_att = sems(st, " ".join(f"p_att{n}" for n in range(AT_IN)))
                with nc.Block(no_gpsimd_drain=True) as block:
                    @block.sync
                    def _(sp):
                        sp.dma_start(pick[:], i["pick"]).then_inc(pick_in, 16)
                        for t in range(KB):
                            if t >= AT_IN:
                                sp.wait_ge(alo_s, t - AT_IN + 1)
                            sp.dma_start(al[t % AT_IN][:], scratch["att"][:, t, :]).then_inc(in_att[t % AT_IN], 16)
                            if t == AT_IN - 1:
                                for g in range(Y_IN):
                                    load_y(sp, yl[g], g, in_y[g])
                        for g in range(Y_IN, GROUPS):
                            sp.wait_ge(sq_s, g - Y_IN + 1)
                            load_y(sp, yl[g % Y_IN], g, in_y[g % Y_IN])
                        sp.dma_start(scratch["gate"], raw[:, :, LEAD:]).then_inc(gate_out, 16)
                        sp.wait_ge(gate_out, 16)

                    @block.scalar
                    def _(act):
                        for t in range(KB):
                            act.wait_ge(in_att[t % AT_IN], 16 * (t // AT_IN + 1))
                            act.activation(hq_hi[:, t, :], al[t % AT_IN][:], ACT.Copy).then_inc(ahi_s, 1)
                        for g in range(GROUPS):
                            act.wait_ge(in_y[g % Y_IN], 16 * (g // Y_IN + 1))
                            if g >= 2:
                                act.wait_ge(add_s, g - 1)
                            act.activation(sq[g % 2][:], yl[g % Y_IN][:], ACT.Square).then_inc(sq_s, 1)
                        act.wait_ge(ss_s, GROUPS)
                        act.activation(halves(y_rstd[:]), psum[0:GROUPS, 6:8, 0:HW], ACT.Sqrt, bias=eps_c[0:GROUPS],
                                       scale=1.0 / (2 * P)).then_inc(root_s, 1)
                        for n in range(2):
                            act.wait_ge(row_done, n + 1)
                            act.activation(late_row[:, n, :], psum[0:2, n, :], ACT.Copy).then_inc(row_s, 1)

                    @block.vector
                    def _(dve):
                        for t in range(KB):
                            dve.wait_ge(ahi_s, t + 1)
                            dve.tensor_tensor(hq_lo[:, t, :], al[t % AT_IN][:], hq_hi[:, t, :].bitcast(F32), ALU.subtract).then_inc(alo_s, 1)
                        for g in range(GROUPS):
                            dve.wait_ge(sq_s, g + 1)
                            if g >= 2:
                                dve.wait_ge(ss_s, g - 1)
                            dve.tensor_tensor(sq_sum[g % 2][:], sq[g % 2][:, 0, :], sq[g % 2][:, 1, :], ALU.add).then_inc(add_s, 1)
                        dve.wait_ge(root_s, 1)
                        dve.reciprocal(y_rstd[:], y_rstd[:]).then_inc(root_s, 1)
                        dve.wait_ge(turn_s, 1)
                        add_bias(dve, 2 * KB, 2 * KB, 2).then_inc(bias_s, 1)
                        dve.wait_ge(bias_s, 1)
                        dve.tensor_tensor(gate[:, 0], mod[:, 2 * KB:3 * KB, :], bcast_mid(vecs[:, 1, :], 2), ALU.mult).then_inc(bias_s, 1)

                    @block.tensor
                    def _(pe):
                        for n in range(2):
                            modulation(pe, psum[0:2, n, :], ada_g1[n]).then_inc(row_done, 1)
                        pe.wait_ge(pick_in, 16)
                        for g in range(GROUPS):
                            pe.wait_ge(add_s, g + 1)
                            for hh in range(2):
                                mm = pe.matmul(psum[0:GROUPS, 6 + hh, 0:HW], pick[:, g, :], sq_sum[g % 2][:, hh * HW:(hh + 1) * HW],
                                               start=g == 0, stop=g == GROUPS - 1)
                            mm.then_inc(ss_s, 1)
                        for n in (2, 3, 0, 1):
                            if n < 2:
                                pe.wait_ge(row_s, n + 1)
                            mm = turn_rows(pe, 2, 8 * n, late_row[:, n, :])
                        mm.then_inc(turn_s, 1)

        late_st.close()

        with ExitStack() as st:
            first_att = [m + max(m - GT + 1, 0) for m in range(KB)]
            N1 = first_att[-1] + 1
            src = []
            for m in range(KB):
                src += ([i["w_gate"][8 + m]] if m >= GT else []) + [i["w_att"][m]]
            for m in range(KB):
                src += [i["w_gate"][m], i["w_ssm"][2 * m], i["w_ssm"][2 * m + 1]]
            O0 = len(src)
            F0, Z0, END = O0 + KB, O0 + KB + 2 * FT, O0 + KB + 3 * FT
            src += ([i["w_out"][n] for n in range(KB)] + [i["w_ffn_in"][n] for n in range(2 * FT)] +
                    [i["w_ffn_out"][n] for n in range(FT)])
            w = Stream(st, "m", src, NCH + GROUPS * GT, True, [])
            mrg = sb(st, "mrg", [P, KB, TW])
            tmp = [sb(st, f"tmp{n}", [P, TW]) for n in range(3)]
            th = sb(st, "th", [P, TW])

            def root(act, dst, sem, scale, bank_slot):
                act.activation(halves(dst[:]), slot(bank_slot), ACT.Sqrt, bias=eps_c, scale=scale).then_inc(sem, 1)

            with ExitStack() as ms:
                wide_hi = sb(ms, "y_hi", [P, 16, TW], F32R)
                wide_lo = sb(ms, "y_lo", [P, 16, TW], F32R)
                yl = [sb(ms, f"yl{n}", [P, 2, TW]) for n in range(2)]
                spread = sb(ms, "spread", [GROUPS, GROUPS, P])
                snorm = sb(ms, "snorm", [P, 16])
                mhi_s, mlo_s = sems(ms, "m_mhi m_mlo")
                (in_y0, in_y1, in_c, pick_s, yn_s, yhi_s, ylo_s, th_s, m_s, dve_s,
                 in_g0, in_g1) = sems(
                    ms, "m_y0 m_y1 m_c m_pick m_yn m_yhi m_ylo m_th m_m m_dve"
                        " m_g0 m_g1")
                in_g = [in_g0, in_g1]
                in_y = [in_y0, in_y1]
                gl = [tmp[1], tmp[2]]
                with nc.Block(no_gpsimd_drain=True) as block:
                    @block.sync
                    def _(sp):
                        sp.dma_start(snorm[:], i["ssm_norm"]).then_inc(in_c, 16)
                        sp.dma_start(spread[:], i["spread"]).then_inc(in_c, 16)
                        for m in range(2):
                            sp.dma_start(gl[m][:], scratch["gate"][:, m, :]).then_inc(in_g[m], 16)
                        for g in range(2):
                            load_y(sp, yl[g], g, in_y[g])
                        for n in range(RAW_SLOTS, RAW_SLOTS + HL_SLOTS):
                            w.load(sp, n)
                        n = RAW_SLOTS + HL_SLOTS
                        for g in range(2, GROUPS):
                            while n <= first_att[g] + 1:
                                w.load(sp, n)
                                n += 1
                            if g < GT:
                                sp.wait_ge(th_s, g - 1)
                                sp.dma_start(gl[g % 2][:], scratch["gate"][:, g, :]).then_inc(in_g[g % 2], 16)
                            sp.wait_ge(ylo_s, 2 * (g - 1))
                            load_y(sp, yl[g % 2], g, in_y[g % 2])
                        while n < O0 + RAW_SLOTS:
                            w.load(sp, n)
                            n += 1

                    @block.gpsimd
                    def _(pool):
                        for n in range(O0 + HL_SLOTS):
                            w.split_lo(pool, n)

                    @block.scalar
                    def _(act):
                        def gate_tanh(n, k, src):
                            if n is None:
                                act.wait_ge(in_g[k % 2], 16 * (k // 2 + 1))
                            else:
                                act.wait_ge(w.used, n + 1)
                            if k >= 1:
                                act.wait_ge(m_s, k)
                            act.activation(halves(th[:]), src, ACT.Tanh, scale=0.5).then_inc(th_s, 1)

                        def y_hi(g):
                            for t in range(2):
                                act.wait_ge(yn_s, 2 * g + t + 1)
                                act.activation(wide_hi[:, 2 * g + t, :], yl[g % 2][:, t, :], ACT.Copy).then_inc(yhi_s, 1)

                        w.split_hi(act, 1)
                        for m in range(KB):
                            n = first_att[m]
                            if m >= GT:
                                w.split_hi(act, n + 1)
                                gate_tanh(n - 1, m, slot(2))
                            else:
                                gate_tanh(None, m, halves(gl[m % 2][:]))
                            w.split_hi(act, n + 2)
                            y_hi(m)
                        for n in range(23):
                            w.split_hi(act, N1 + n + 2)
                            if n % 3 == 0:
                                gate_tanh(N1 + n, 8 + n // 3, slot(2))
                        for t in range(KB):
                            if t == KB - 1:
                                w.split_hi(act, O0 + 1)
                            act.wait_ge(m_s, KB + t + 1)
                            act.activation(hp_hi[:, t, :], mrg[:, t, :], ACT.Copy, scale=0.5).then_inc(mhi_s, 1)

                    @block.vector
                    def _(dve):
                        link = chain(dve_s)
                        dve.wait_ge(in_c, 32)
                        for m in range(KB):
                            dve.wait_ge(in_y[m % 2], 16 * (m // 2 + 1))
                            dve.wait_ge(pick_s, m + 1)
                            for t in range(2):
                                dve.scalar_tensor_tensor(out=halves(yl[m % 2][:, t, :]), in0=halves(yl[m % 2][:, t, :]),
                                                         scalar=snorm[:, 2 * m + t:2 * m + t + 1], in1=slot(3), op0=ALU.mult,
                                                         op1=ALU.mult).then_inc(yn_s, 1)
                            for t in range(2):
                                dve.wait_ge(yhi_s, 2 * m + t + 1)
                                dve.tensor_tensor(wide_lo[:, 2 * m + t, :], yl[m % 2][:, t, :],
                                                  wide_hi[:, 2 * m + t, :].bitcast(F32), ALU.subtract).then_inc(ylo_s, 1)
                            dve.wait_ge(th_s, m + 1)
                            dve.wait_ge(w.used, first_att[m] + 1)
                            dve.scalar_tensor_tensor(out=halves(mrg[:, m, :]), in0=halves(th[:]), scalar=1.0, in1=slot(m % 2),
                                                     op0=ALU.add, op1=ALU.mult).then_inc(m_s, 1)

                        def merged_lo(t):
                            dve.wait_ge(mhi_s, t + 1)
                            dve.scalar_tensor_tensor(out=hp_lo[:, t, :], in0=mrg[:, t, :], scalar=0.5, in1=hp_hi[:, t, :].bitcast(F32),
                                                     op0=ALU.mult, op1=ALU.subtract).then_inc(mlo_s, 1)

                        for m in range(KB):
                            if m == KB - 1:
                                for t in range(KB - 1):
                                    merged_lo(t)
                            dve.wait_ge(th_s, 8 + m + 1)
                            dve.wait_ge(w.used, N1 + 3 * m + 3)
                            link(dve, dve.scalar_tensor_tensor(out=halves(tmp[0][:]), in0=halves(th[:]), scalar=1.0, in1=slot(m % 2),
                                                               op0=ALU.add, op1=ALU.mult))
                            dve.tensor_tensor(mrg[:, m, :], mrg[:, m, :], tmp[0][:], ALU.add).then_inc(m_s, 1)
                            dve.wait_ge(m_s, 8 + m + 1)
                        merged_lo(KB - 1)
                        dve.wait_ge(mlo_s, KB)

                    @block.tensor
                    def _(pe):
                        def tile(s, hi, lo, k0=0, nk=KB):
                            for k in range(k0, k0 + KB):
                                w.multiply(pe, slot(s), hi[:, k, :], lo[:, k, :], k == 0, k == nk - 1)

                        for m in range(KB):
                            if m >= GT:
                                pe.wait_ge(th_s, m)
                                tile(2, hp_hi, hp_lo)
                            if m >= 2:
                                pe.wait_ge(m_s, m - 1)
                            tile(m % 2, hq_hi, hq_lo)
                            if m == 0:
                                pe.wait_ge(in_c, 32)
                            if m >= 1:
                                pe.wait_ge(yn_s, 2 * m)
                            for hh in range(2):
                                mm = pe.matmul(psum[:, 6 + hh, 0:HW], spread[:, m, :], y_rstd[:, hh * HW:(hh + 1) * HW], start=True,
                                               stop=True)
                            mm.then_inc(pick_s, 1)
                        for m in range(KB):
                            pe.wait_ge(th_s, 8 + m)
                            tile(2, hp_hi, hp_lo)
                            if m == 0:
                                pe.wait_ge(ylo_s, 16)
                                pe.wait_ge(m_s, KB)
                            elif m >= 2:
                                pe.wait_ge(m_s, KB + m - 1)
                            tile(m % 2, wide_hi, wide_lo, 0, 16)
                            tile(m % 2, wide_hi, wide_lo, 8, 16)
                        for k in range(KB):
                            pe.wait_ge(mlo_s, k + 1)
                            w.multiply(pe, slot(0), hp_hi[:, k, :], hp_lo[:, k, :], k == 0, k == KB - 1)

            rr_st.close()

            with ExitStack() as ms:
                ada = [sb(ms, f"ada_o{n}", [P, KB, ADA_W]) for n in range(4)]
                mod_row = sb(ms, "mod_row_o", [2, 2, ADA_W])
                sq = [sb(ms, f"osq{n}", [P, TW]) for n in range(2)]
                rs = [sb(ms, f"ors{n}", [P, TW]) for n in range(2)]
                xl = [*(sb(ms, f"xl{n}", [P, TW]) for n in range(2)), th]
                (add_s, ev_s, sq_s, ss_s, root_s, x_in0, x_in1, x_in2, x_s, h_s, hhi_s, dve_s, hlo_s) = sems(
                    ms, "o_add o_ev o_sq o_ss o_root o_xin0 o_xin1 o_xin2 o_x o_h o_hhi o_dve o_hlo")
                x_in = [x_in0, x_in1, x_in2]
                in_ada = sems(ms, " ".join(f"o_ada{n}" for n in range(4)))
                row_done, row_s, turn_s = sems(ms, "o_rowdone o_row o_turn")
                with nc.Block(no_gpsimd_drain=True) as block:
                    @block.sync
                    def _(sp):
                        for n in range(RAW_SLOTS, RAW_SLOTS + HL_SLOTS):
                            w.load(sp, O0 + n)
                        for t in range(3):
                            sp.dma_start(xl[t][:], i["x"][:, t, :]).then_inc(x_in[t % 3], 16)
                        for n in range(RAW_SLOTS + HL_SLOTS, KB + RAW_SLOTS):
                            w.load(sp, O0 + n)
                            a = n - RAW_SLOTS - HL_SLOTS
                            if a < 4:
                                sp.dma_start(ada[a][:], i["w_ada"][SCALE2 + a]).then_inc(in_ada[a], 16)
                        for t in range(3, KB):
                            sp.wait_ge(x_s, t - 2)
                            sp.dma_start(xl[t % 3][:], i["x"][:, t, :]).then_inc(x_in[t % 3], 16)

                    @block.gpsimd
                    def _(pool):
                        for n in range(HL_SLOTS, KB + HL_SLOTS):
                            w.split_lo(pool, O0 + n)
                        for t in range(KB):
                            pool.wait_ge(hhi_s, t + 1)
                            pool.tensor_tensor(hq_lo[:, t, :], tmp[t % 3][:], hq_hi[:, t, :].bitcast(F32), ALU.subtract).then_inc(hlo_s, 1)
                        pool.wait_ge(hlo_s, KB)

                    @block.scalar
                    def _(act):
                        def square(t, count):
                            if 2 <= count < KB:
                                act.wait_ge(add_s, max(count - 2, 1))
                            elif count == KB:
                                act.wait_ge(add_s, KB - 1)
                            elif count >= KB + 2:
                                act.wait_ge(ss_s, count - KB)
                            act.activation(sq[count % 2][:], mrg[:, t, :], ACT.Square).then_inc(sq_s, 1)

                        for n in range(KB):
                            if n < KB - 1:
                                w.split_hi(act, O0 + n + 2)
                            act.wait_ge(w.used, O0 + n + 1)
                            act.activation(halves(mrg[:, n, :]), slot(n % 2), ACT.Copy).then_inc(ev_s, 1)
                            act.wait_ge(ev_s, n + 1)
                            square(n, n)
                        w.split_hi(act, F0 + 1)
                        act.wait_ge(ss_s, 1)
                        root(act, rs[0], root_s, 1.0 / D, 3)
                        def row(a):
                            act.wait_ge(row_done, a + 1)
                            if a >= 2:
                                act.wait_ge(turn_s, 1)
                            act.activation(mod_row[:, a % 2, :], psum[0:2, a, :], ACT.Copy).then_inc(row_s, 1)

                        for t in range(KB):
                            act.wait_ge(x_s, t + 1)
                            square(t, KB + t)
                            if t == 1:
                                row(0)
                        row(1)
                        act.wait_ge(ss_s, KB + 1)
                        root(act, rs[1], root_s, 1.0 / D, 2)
                        for t in range(KB):
                            act.wait_ge(h_s, t + 1)
                            act.activation(hq_hi[:, t, :], tmp[t % 3][:], ACT.Copy).then_inc(hhi_s, 1)
                        row(2)
                        row(3)

                    @block.vector
                    def _(dve):
                        link = chain(dve_s)
                        for t in range(1, KB):
                            dve.wait_ge(sq_s, t + 1)
                            ins = dve.tensor_tensor(rs[1][:], sq[0][:] if t == 1 else rs[1][:], sq[t % 2][:], ALU.add)
                            ins.then_inc(add_s, 1)
                            dve.wait_ge(add_s, t)
                        dve.wait_ge(root_s, 1)
                        link(dve, dve.reciprocal(rs[0][:], rs[0][:]))
                        for t in range(KB):
                            link(dve, dve.tensor_tensor(mrg[:, t, :], mrg[:, t, :], rs[0][:], ALU.mult))
                            dve.wait_ge(x_in[t % 3], 16 * (t // 3 + 1))
                            for c0, L, g in RANGES:
                                ins = dve.scalar_tensor_tensor(out=mrg[:, t, c0:c0 + L], in0=mrg[:, t, c0:c0 + L],
                                                               scalar=gate[:, 0, t, g:g + 1], in1=xl[t % 3][:, c0:c0 + L],
                                                               op0=ALU.mult, op1=ALU.add)
                            ins.then_inc(x_s, 1)
                        dve.wait_ge(root_s, 2)
                        link(dve, dve.reciprocal(rs[1][:], rs[1][:]))
                        dve.wait_ge(turn_s, 1)
                        link(dve, add_bias(dve, 4 * KB, KB, 6))
                        link(dve, dve.scalar_tensor_tensor(out=gain[:, 1], in0=mod[:, 4 * KB:5 * KB, :], scalar=1.0,
                                                           in1=bcast_mid(vecs[:, 2, :], 2), op0=ALU.add, op1=ALU.mult))
                        for t in range(KB):
                            if t >= 3:
                                dve.wait_ge(hlo_s, t - 2)
                            link(dve, dve.tensor_tensor(tmp[t % 3][:], mrg[:, t, :], rs[1][:], ALU.mult))
                            for c0, L, g in RANGES:
                                ins = dve.tensor_scalar(tmp[t % 3][:, c0:c0 + L], tmp[t % 3][:, c0:c0 + L], gain[:, 1, t, g:g + 1],
                                                        mod[:, 24 + t, g:g + 1], ALU.mult, ALU.add)
                            ins.then_inc(h_s, 1)
                        dve.wait_ge(turn_s, 2)
                        link(dve, add_bias(dve, 5 * KB, KB, 7))
                        link(dve, dve.tensor_tensor(gate[:, 1], mod[:, 5 * KB:6 * KB, :], bcast_mid(vecs[:, 3, :], 2), ALU.mult))

                    @block.tensor
                    def _(pe):
                        def squares(src, s, first, last):
                            for hh in range(2):
                                mm = pe.matmul(psum[:, 2 * s + hh, 0:HW], ones[:], src[:, hh * HW:(hh + 1) * HW],
                                               start=first, stop=last)
                            mm.then_inc(ss_s, 1)

                        for m in range(1, KB):
                            if m >= 2:
                                pe.wait_ge(ev_s, m - 1)
                            for k in range(KB):
                                w.multiply(pe, slot(m % 2), hp_hi[:, k, :], hp_lo[:, k, :], k == 0, k == KB - 1)
                        pe.wait_ge(add_s, KB - 1)
                        squares(rs[1], 3, True, True)

                        def block_step(a, k):
                            if k == 0:
                                pe.wait_ge(in_ada[a], 16)
                            mm = pe.matmul(psum[0:2, a, :], c_silu[:, k, :], ada[a][:, k, :], start=k == 0, stop=k == KB - 1)
                            if k == KB - 1:
                                mm.then_inc(row_done, 1)

                        def turn(vector, bank):
                            for a in (2 * vector, 2 * vector + 1):
                                pe.wait_ge(row_s, a + 1)
                                mm = turn_rows(pe, bank, 8 * (a % 2), mod_row[:, a % 2, :])
                            mm.then_inc(turn_s, 1)

                        pe.wait_ge(ev_s, KB)
                        for k in range(KB):
                            block_step(0, k)
                        for t in range(KB):
                            block_step(1, t)
                            pe.wait_ge(sq_s, KB + t + 1)
                            squares(sq[t % 2], 2, t == 0, t == KB - 1)
                        pe.wait_ge(root_s, 1)
                        turn(0, 6)
                        for a in (2, 3):
                            for k in range(KB):
                                block_step(a, k)
                        for k in range(KB):
                            pe.wait_ge(hlo_s, k + 1)
                            w.multiply(pe, slot(0), hq_hi[:, k, :], hq_lo[:, k, :], k == 0, k == KB - 1)
                        turn(1, 7)

            tile_s, = sems(st, "z_tile")
            wide_hi = sb(st, "wide_hi", [P, FT - KB, TW], F32R)
            wide_lo = sb(st, "wide_lo", [P, FT - KB, TW], F32R)
            with ExitStack() as ms:
                fpar = sb(ms, "fpar", [P, FT, 6])
                fr = [sb(ms, f"fr{n}", [P, LEAD + TW]) for n in range(2)]
                fst = sb(ms, "fst", [P, FT, 4])
                cvf = [tmp[1], tmp[2]]
                (in_s, fe_s, fcv_s, fth_s, fsl_s, ff_s, fhi_s, flo_s, fst_s, dve_s, z_s, o_s) = sems(
                    ms, "f_in f_e f_cv f_th f_sl f_f f_fhi f_flo f_st f_dve f_z f_o")
                sl = [sb(ms, f"fs{n}", [P, TW]) for n in range(2)]

                def wide(f, part):
                    return ((hp_hi, hp_lo)[part][:, f, :] if f < KB else (wide_hi, wide_lo)[part][:, f - KB, :])

                with nc.Block(no_gpsimd_drain=True) as block:
                    @block.sync
                    def _(sp):
                        sp.dma_start(fpar[:], i["fpar"]).then_inc(in_s, 16)
                        for n in range(F0 + RAW_SLOTS, Z0 + RAW_SLOTS + 2):
                            w.load(sp, n)
                        sp.wait_ge(fst_s, 2 * FT)
                        sp.dma_start(o["ffn"], fst[:]).then_inc(o_s, 16)
                        sp.wait_ge(o_s, 16)

                    @block.gpsimd
                    def _(pool):
                        for n in range(2):
                            pool.memset(fr[n][:, 0:LEAD], 0.0).then_inc(z_s, 1)
                        for n in range(2 * FT):
                            w.split_lo(pool, F0 + n + HL_SLOTS)
                            f, up = divmod(n, 2)
                            if up:
                                pool.wait_ge(fe_s, f + 1)
                                pool.tensor_copy(fst[:, f, 0:2], fr[f % 2][:, LEAD + T - 2:LEAD + T]).then_inc(fst_s, 1)
                                pool.tensor_copy(fst[:, f, 2:4], fr[f % 2][:, LEAD + TW - 2:LEAD + TW]).then_inc(fst_s, 1)
                        w.split_lo(pool, Z0 + 2)

                    @block.scalar
                    def _(act):
                        act.wait_ge(z_s, 2)

                        def round_hi(f):
                            act.wait_ge(ff_s, f + 1)
                            act.activation(wide(f, 0), sl[f % 2][:], ACT.Copy).then_inc(fhi_s, 1)

                        for n in range(2 * FT):
                            w.split_hi(act, F0 + n + 2)
                            f, up = divmod(n, 2)
                            if not up:
                                act.wait_ge(w.used, F0 + n + 1)
                                if f >= 2:
                                    act.wait_ge(fcv_s, f - 1)
                                    act.wait_ge(fst_s, 2 * (f - 1))
                                act.activation(halves(fr[f % 2][:, LEAD:]), slot(f % 2), ACT.Copy).then_inc(fe_s, 1)
                                if f >= 1:
                                    round_hi(f - 1)
                            else:
                                act.wait_ge(fcv_s, f + 1)
                                if f >= 1:
                                    act.wait_ge(fsl_s, f)
                                act.activation(th[:], cvf[f % 2][:], ACT.Tanh).then_inc(fth_s, 1)
                        round_hi(FT - 1)
                        w.split_hi(act, Z0 + 2)

                    @block.vector
                    def _(dve):
                        link = chain(dve_s)
                        dve.wait_ge(in_s, 16)
                        link(dve, dve.tensor_scalar(fpar[:, :, 0:4], fpar[:, :, 0:4], 0.5, None, ALU.mult))

                        def round_lo(f):
                            dve.wait_ge(fhi_s, f + 1)
                            dve.tensor_tensor(wide(f, 1), sl[f % 2][:], wide(f, 0).bitcast(F32), ALU.subtract).then_inc(flo_s, 1)

                        for f in range(FT):
                            dve.wait_ge(fe_s, f + 1)
                            r, c = fr[f % 2], cvf[f % 2]
                            link(dve, dve.tensor_copy(r[:, LEAD + S0 - 2:LEAD + S0], fpar[:, f, 4:6]))
                            link(dve, dve.tensor_scalar(c[:], r[:, 2:2 + TW], fpar[:, f, 0:1], fpar[:, f, 3:4], ALU.mult, ALU.add))
                            link(dve, dve.scalar_tensor_tensor(out=c[:], in0=r[:, 3:3 + TW], scalar=fpar[:, f, 1:2], in1=c[:],
                                                               op0=ALU.mult, op1=ALU.add))
                            dve.scalar_tensor_tensor(out=c[:], in0=r[:, 4:4 + TW], scalar=fpar[:, f, 2:3], in1=c[:],
                                                     op0=ALU.mult, op1=ALU.add).then_inc(fcv_s, 1)
                            if f >= 1:
                                round_lo(f - 1)
                            dve.wait_ge(fth_s, f + 1)
                            if f >= 2:
                                dve.wait_ge(flo_s, f - 1)
                            dve.scalar_tensor_tensor(out=sl[f % 2][:], in0=th[:], scalar=1.0, in1=c[:], op0=ALU.add,
                                                     op1=ALU.mult).then_inc(fsl_s, 1)
                            dve.wait_ge(fsl_s, f + 1)
                            dve.wait_ge(w.used, F0 + 2 * f + 2)
                            dve.tensor_tensor(halves(sl[f % 2][:]), halves(sl[f % 2][:]), slot(2 + f % 2), ALU.mult).then_inc(ff_s, 1)
                        round_lo(FT - 1)

                    @block.tensor
                    def _(pe):
                        for n in range(1, 2 * FT):
                            f, up = divmod(n, 2)
                            if f >= 2:
                                if up:
                                    pe.wait_ge(ff_s, f - 1)
                                else:
                                    pe.wait_ge(fe_s, f - 1)
                            for k in range(KB):
                                w.multiply(pe, slot(2 * up + f % 2), hq_hi[:, k, :], hq_lo[:, k, :], k == 0, k == KB - 1)
                        pe.wait_ge(fe_s, FT - 1)
                        for k in range(FT):
                            if k >= FT - 3:
                                pe.wait_ge(flo_s, k + 1)
                            w.multiply(pe, slot(0), wide(k, 0), wide(k, 1), k == 0, k == FT - 1, tile_s if k == FT - 1 else None)

            hq_st.close()
            with ExitStack() as ms:
                sq = [sb(ms, f"zsq{n}", [P, TW]) for n in range(2)]
                rs0 = sb(ms, "zrs", [P, TW])
                ev_s, sq_s, ss_s, root_s, y_s, dve_s, o_s = sems(ms, "z_ev z_sq z_ss z_root z_y z_dve z_o")
                fo = sb(ms, "fo", [P, KB, TW])
                sq_sum = sb(ms, "zsum", [P, TW])
                add_s, gated_s, rec_s, py_s, y_pool = sems(ms, "z_add z_gated z_rec z_py z_ypool")
                ON_POOL = (2, 5)
                with nc.Block(no_gpsimd_drain=True) as block:
                    @block.sync
                    def _(sp):
                        for n in range(Z0 + RAW_SLOTS + 2, END):
                            w.load(sp, n)
                        for t in range(KB):
                            if t in ON_POOL:
                                sp.wait_ge(y_pool, ON_POOL.index(t) + 1)
                            else:
                                sp.wait_ge(y_s, t + 1 - sum(p < t for p in ON_POOL))
                            sp.dma_start(o["y"][:, t, :], mrg[:, t, :]).then_inc(o_s, 16)
                        sp.wait_ge(o_s, 16 * KB)

                    @block.gpsimd
                    def _(pool):
                        for n in range(Z0 + 3, END):
                            w.split_lo(pool, n)
                        pool.wait_ge(rec_s, 1)
                        pool.wait_ge(gated_s, KB)
                        for j, t in enumerate(ON_POOL):
                            pool.tensor_tensor(fo[:, t, :], fo[:, t, :], rs0[:], ALU.mult).then_inc(py_s, 1)
                            pool.wait_ge(py_s, j + 1)
                            pool.tensor_tensor(mrg[:, t, :], mrg[:, t, :], fo[:, t, :], ALU.add).then_inc(y_pool, 1)

                    @block.scalar
                    def _(act):
                        n = 3
                        for m in range(KB):
                            while n < FT and (n - 2 + 1) * KB <= (m + 1) * FT:
                                w.split_hi(act, Z0 + n)
                                n += 1
                            if (m + 1) * FT % KB == 0:
                                act.wait_ge(w.used, Z0 + (m + 1) * FT // KB)
                            else:
                                act.wait_ge(tile_s, sum((j + 1) * FT % KB != 0 for j in range(m + 1)))
                            act.activation(halves(fo[:, m, :]), slot(m % 2), ACT.Copy).then_inc(ev_s, 1)
                            act.wait_ge(ev_s, m + 1)
                            if m >= 2:
                                act.wait_ge(add_s, max(m - 2, 1))
                            act.activation(sq[m % 2][:], fo[:, m, :], ACT.Square).then_inc(sq_s, 1)
                        act.wait_ge(ss_s, 1)
                        root(act, rs0, root_s, 1.0 / D, 3)

                    @block.vector
                    def _(dve):
                        link = chain(dve_s)

                        def gated(t):
                            for c0, L, g in RANGES:
                                ins = dve.tensor_scalar(fo[:, t, c0:c0 + L], fo[:, t, c0:c0 + L], gate[:, 1, t, g:g + 1], None, ALU.mult)
                            ins.then_inc(gated_s, 1)

                        for t in range(1, KB):
                            dve.wait_ge(sq_s, t + 1)
                            dve.tensor_tensor(sq_sum[:], sq[0][:] if t == 1 else sq_sum[:], sq[t % 2][:], ALU.add).then_inc(add_s, 1)
                            dve.wait_ge(add_s, t)
                            gated(t - 1)
                        gated(KB - 1)
                        dve.wait_ge(root_s, 1)
                        dve.reciprocal(rs0[:], rs0[:]).then_inc(rec_s, 1)
                        dve.wait_ge(rec_s, 1)
                        dve.wait_ge(gated_s, KB)
                        for t in range(KB):
                            if t not in ON_POOL:
                                link(dve, dve.tensor_tensor(fo[:, t, :], fo[:, t, :], rs0[:], ALU.mult))
                                dve.tensor_tensor(mrg[:, t, :], mrg[:, t, :], fo[:, t, :], ALU.add).then_inc(y_s, 1)

                    @block.tensor
                    def _(pe):
                        for m in range(1, KB):
                            if m >= 2:
                                pe.wait_ge(ev_s, m - 1)
                            for k in range(FT):
                                w.multiply(pe, slot(m % 2), wide(k, 0), wide(k, 1), k == 0, k == FT - 1,
                                           tile_s if k == FT - 1 else None)
                        pe.wait_ge(add_s, KB - 1)
                        for hh in range(2):
                            mm = pe.matmul(psum[:, 6 + hh, 0:HW], ones[:], sq_sum[:, hh * HW:(hh + 1) * HW], start=True, stop=True)
                        mm.then_inc(ss_s, 1)


def columns(v):
    v = np.asarray(v)
    v = v.reshape(v.shape[:-1] + (-1, P))
    return np.ascontiguousarray(np.moveaxis(v, -1, 0))


def chunks(m):
    k, n = m.shape[0] // D, m.shape[1] // P
    return np.ascontiguousarray(m.reshape(k, KB, P, n, P).transpose(3, 0, 2, 1, 4).reshape(n * k, P, D))


def kernel(**inputs):
    import concourse.bacc as bacc
    from concourse.bass_utils import run_bass_kernel_spmd

    a = {n: np.asarray(v) for n, v in inputs.items()}
    f32 = np.float32
    x = np.zeros((P, KB, TW), a["x_prompt"].dtype)
    x[:, :, 0:T] = a["x_prompt"][0].T.reshape(KB, P, T).transpose(1, 0, 2)
    x[:, :, S0:] = a["x_sample"][0].T.reshape(KB, P, S).transpose(1, 0, 2)
    c = np.stack([a["c_prompt"][0], a["c_sample"][0]], -1).reshape(KB, P, 2).transpose(1, 0, 2)

    w_in = a["w_in"][0]
    inner, conv_dim, n_heads = 2048, 4096, 32
    at = np.cumsum([0, inner, conv_dim, n_heads, 1024, 256, 256, 2048])
    w_z, w_xbc, w_dt, w_q, w_k, w_v, w_g = (w_in[:, at[j]:at[j + 1]] for j in range(7))
    w_dt = np.concatenate([w_dt, np.zeros((D, P - n_heads), w_dt.dtype)], 1)
    zc, xc = chunks(w_z), chunks(w_xbc)
    w_grp = np.concatenate([np.stack([xc[16 + g], xc[24 + g], xc[2 * g], xc[2 * g + 1], zc[2 * g], zc[2 * g + 1]])
                            for g in range(GROUPS)])
    gc = chunks(w_g)
    w_att = chunks(a["w_att_out"][0])
    w_grp = np.concatenate([w_grp, gc[8:8 + GT], w_att[0:RAW_SLOTS]]).reshape(-1, D)
    fi = chunks(a["w_ffn_in"][0])
    w_ffn_in = np.stack([fi[f + FT * u] for f in range(FT) for u in range(2)])
    fo = a["w_ffn_out"][0].reshape(FT, P, KB, P).transpose(2, 0, 1, 3).reshape(FT, KB, P, P)
    w_ffn_out = np.ascontiguousarray(fo.transpose(0, 2, 1, 3)).reshape(FT, P, D)
    ada = a["w_ada"][0].reshape(KB, P, 6 * D // ADA_W, ADA_W).transpose(2, 1, 0, 3)

    cw, cb, ctx = columns(a["ssm_conv_w"][0]), columns(a["ssm_conv_b"][0]), columns(a["state_conv"][0, 0])
    heads = a["ssm_d"][0].reshape(GROUPS, 2, 2)
    gp = np.zeros((P, GROUPS, GP_N), cw.dtype)
    for g in range(GROUPS):
        for j, t in enumerate((16 + g, 24 + g, 2 * g, 2 * g + 1)):
            gp[:, g, GP_W + TAPS * j:GP_W + TAPS * (j + 1)] = cw[:, :, t]
            gp[:, g, GP_B + j] = cb[:, t]
            gp[:, g, GP_CTX + 3 * j:GP_CTX + 3 * j + 3] = ctx[:, :, t]
        gp[:, g, GP_D:GP_D + 2] = np.repeat(heads[g], HD, axis=1).T
    fw, fb, fctx = columns(a["ffn_conv_w"][0]), columns(a["ffn_conv_b"][0]), columns(a["state_ffn_conv"][0, 0])
    fpar = np.concatenate([fw.transpose(0, 2, 1), fb[:, :, None], fctx.transpose(0, 2, 1)], 2)

    half, theta = 8, 500000.0
    pos = np.zeros(TW, f32)
    pos[0:T] = np.arange(T)
    pos[S0:] = 256 + np.arange(S)
    inv = (f32(theta) ** (-np.arange(half, dtype=f32) / f32(half))).astype(f32)
    ang = (pos[None, :] * inv[:, None]).astype(f32)
    cos, sin, rot = np.ones((P, TW), f32), np.zeros((P, TW), f32), np.zeros((P, P), f32)
    for b in (0, 64):
        for j in range(half):
            cos[b + j] = cos[b + half + j] = np.cos(ang[j])
            sin[b + j], sin[b + half + j] = -np.sin(ang[j]), np.sin(ang[j])
            rot[b + half + j, b + j] = rot[b + j, b + half + j] = 1.0

    mask_k = np.zeros((1, WIN + T + CH), f32)
    mask_k[0, 0:WIN] = np.finfo(f32).min
    sk = a["attn_sinks"][0].reshape(KV, 2, 2)
    sinks = np.repeat(sk.transpose(1, 0, 2).reshape(2, 2 * KV), CH, axis=0)
    sinks_s = np.concatenate([np.repeat(sk.transpose(1, 0, 2).reshape(2, 2 * KV), S, axis=0)] * 2, axis=0)
    state = a["state_ssm"][0, 0].reshape(GROUPS, HPG * HD, NS).transpose(0, 2, 1).reshape(GROUPS * P, HPG * HD)
    consts = np.zeros((P, 2), f32)
    consts[:, 0], consts[:, 1] = EPS, 1.0

    ins = dict(
        x=x, c=c, ident=np.eye(P, dtype=f32), consts=consts, mask_u=np.triu(np.ones((P, P), f32)),
        vecs=np.stack([columns(a[n][0]) for n in ("norm_mix_pre", "norm_mix_post", "norm_ffn_pre", "norm_ffn_post")], 1),
        b_ada=columns(a["b_ada"][0]), w_ada=ada, w_qkv=np.concatenate([chunks(w_k), chunks(w_q), chunks(w_dt), chunks(w_v)]),
        w_grp=w_grp, w_gate=gc, w_att=w_att, w_ssm=chunks(a["w_ssm_out"][0]), w_out=chunks(a["w_out"][0]),
        w_ffn_in=w_ffn_in, w_ffn_out=w_ffn_out, gp=gp, fpar=fpar, cos=cos, sin=sin, rot=rot,
        dt_par=np.stack([a["ssm_dt_bias"][0], a["ssm_a_log"][0]], 1), mask_k=mask_k, sinks=sinks, sinks_s=sinks_s, state=state,
        ssm_norm=columns(a["ssm_norm"][0]), pick=np.tile(np.eye(GROUPS, dtype=f32), (P, 1, 1)),
        spread=np.repeat(np.eye(GROUPS, dtype=f32)[:, :, None], P, axis=2),
        cache_k=a["cache_k"][0, 0].transpose(2, 1, 0), cache_v=a["cache_v"][0, 0].reshape(WIN, 256),
    )
    outs = dict(y=(P, KB, TW), ssm_p=(GROUPS * P, 256), ssm_s=(GROUPS * P, 256), conv_p=(GROUPS * P, 4, 3), conv_s=(GROUPS * P, 4, 3),
                k_p=(256, WIN), k_s=(256, WIN), v_p=(WIN, 256), v_s=(WIN, 256), ffn=(P, FT, 4))
    inner_dram = dict(q=(ATT_CHUNKS + 1, P, KB, CH), qs=(P, KB, S), k=(64, KV, WIN + T + CH), ks=(64, KV, WIN + S), v=(WIN + T + CH, 256),
                      vs=(WIN + S, 256), acs=(32, TW), att=(P, KB, TW), gate=(P, GT, TW), y=(GROUPS * P, 2 * TW))

    nc = bacc.Bacc("TRN2", target_bir_lowering=False, num_devices=1)
    arrays = {f"in_{n}": np.ascontiguousarray(v) for n, v in ins.items()}
    i = {n: nc.dram_tensor(f"in_{n}", v.shape, F32, kind="ExternalInput").ap() for n, v in ins.items()}
    o = {n: nc.dram_tensor(f"out_{n}", s, F32, kind="ExternalOutput").ap() for n, s in outs.items()}
    scratch = {n: nc.dram_tensor(f"mem_{n}", s, F32, kind="Internal").ap() for n, s in inner_dram.items()}
    build_layer(nc, i, o, scratch)
    r = run_bass_kernel_spmd(nc, [arrays], core_ids=[0]).results[0]
    got = {n: np.asarray(r[f"out_{n}"]) for n in outs}

    def rows(cols):
        return got["y"][:, :, cols].transpose(2, 1, 0).reshape(1, -1, D)

    def state_out(s):
        return s.reshape(GROUPS, NS, HPG, HD).transpose(0, 2, 3, 1).reshape(1, 1, 32, HD, NS)

    def conv_out(s):
        s = s.reshape(GROUPS, P, 4, 3)
        parts = [s[:, :, 2:4].transpose(3, 0, 2, 1).reshape(3, inner), s[:, :, 0].transpose(2, 0, 1).reshape(3, 1024),
                 s[:, :, 1].transpose(2, 0, 1).reshape(3, 1024)]
        return np.concatenate(parts, 1).reshape(1, 1, 3, conv_dim)

    def kv_out(s):
        return s.reshape(1, 1, WIN, KV, HD)

    def ffn_out(s):
        return s.transpose(2, 1, 0).reshape(1, 1, 2, FT * P)

    return (rows(slice(0, T)), rows(slice(S0, TW)), state_out(got["ssm_p"]), conv_out(got["conv_p"]), kv_out(got["k_p"].T),
            kv_out(got["v_p"]), ffn_out(got["ffn"][:, :, 0:2]), state_out(got["ssm_s"]), conv_out(got["conv_s"]),
            kv_out(got["k_s"].T), kv_out(got["v_s"]), ffn_out(got["ffn"][:, :, 2:4]))
```
